# Optimizing a Trainium2 kernel written in Bass

```python
import math
import jax
import jax.numpy as jnp
from jax import lax
import numpy as np

D_MODEL = 1024
BATCH = 1
SEQ = 128
DEPTH = 1
DEC_BATCH = 1
DEC_SEQ = 512
PAST_LEN = 128

GRID_W = 64
POS_BASE = 10000.0
CONV_K = 5
GDN_HEADS = 8
GDN_DK = 128
GDN_DV = 128
GDN_CHUNK = 64
SSD_HEADS = 32
SSD_P = 64
SSD_INNER = SSD_HEADS * SSD_P
SSD_GROUPS = 4
SSD_N = 128
SSD_CHUNK = 128
N_GROUPS = 4
EXPERTS_PER_GROUP = 8
N_EXPERTS = N_GROUPS * EXPERTS_PER_GROUP
TOP_K_IN_GROUP = 2
D_EXPERT = 256
DT_MIN = 0.001
DT_MAX = 0.1
EPS = 1e-6
ALPHA = (2.0 * DEPTH) ** 0.25
IN_SPLITS = (2 * GDN_HEADS * GDN_DK + GDN_HEADS * GDN_DV, GDN_HEADS * GDN_DV, 2 * GDN_HEADS, 2 * GDN_HEADS,
             SSD_INNER + 2 * SSD_GROUPS * SSD_N, SSD_INNER, 2 * SSD_HEADS, 2 * D_MODEL)
IN_COLS = sum(IN_SPLITS)

kernel_name = "bidir_gdn_ssd_hiermoe_prefix_dit"

def _split_cols(t, sizes):
    return jnp.split(t, np.cumsum(sizes)[:-1].tolist(), axis=-1)

def _layernorm(x, g=None, b=None):
    xf = x.astype(jnp.float32)
    mu = jnp.mean(xf, axis=-1, keepdims=True)
    var = jnp.mean(jnp.square(xf - mu), axis=-1, keepdims=True)
    y = (xf - mu) * lax.rsqrt(var + EPS)
    if g is not None:
        y = y * g.astype(jnp.float32) + b.astype(jnp.float32)
    return y.astype(x.dtype)

def _rms(x):
    return x * lax.rsqrt(jnp.mean(jnp.square(x), axis=-1, keepdims=True) + EPS)

def _l2norm(x):
    return x * lax.rsqrt(jnp.sum(jnp.square(x), axis=-1, keepdims=True) + EPS)

def _flip(t):
    return jnp.flip(t, axis=1)

def _grid_pos_embed(n_tokens, d):
    rows = n_tokens // GRID_W
    rr, cc = jnp.meshgrid(jnp.arange(rows, dtype=jnp.float32), jnp.arange(GRID_W, dtype=jnp.float32), indexing="ij")
    quarter = d // 4
    freqs = jnp.exp(-math.log(POS_BASE) * jnp.arange(quarter, dtype=jnp.float32) / quarter)
    ang_r = rr.reshape(-1, 1) * freqs
    ang_c = cc.reshape(-1, 1) * freqs
    return jnp.concatenate([jnp.sin(ang_r), jnp.cos(ang_r), jnp.sin(ang_c), jnp.cos(ang_c)], axis=-1)

def _dwconv_centred(u, w, bias):
    k, ch = w.shape
    pad = k // 2
    out = lax.conv_general_dilated(u, w[:, None, :].astype(u.dtype), window_strides=(1,), padding=((pad, pad),),
                                   dimension_numbers=("NWC", "WIO", "NWC"), feature_group_count=ch)
    return out + bias.astype(u.dtype)

def _to_chunks(t, size):
    b, l, h = t.shape[:3]
    t = t.reshape(b, l // size, size, h, *t.shape[3:])
    return jnp.moveaxis(t, 3, 1)

def _gdn_chunked(q, k, v, beta, g, s0):
    b, l, h, _ = q.shape
    q, k, v, beta, g = (_to_chunks(t, GDN_CHUNK) for t in (q, k, v, beta, g))
    gc = jnp.cumsum(g, axis=-1)
    incl = jnp.tril(jnp.ones((GDN_CHUNK, GDN_CHUNK), dtype=bool))
    strict = jnp.tril(jnp.ones((GDN_CHUNK, GDN_CHUNK), dtype=bool), k=-1)
    decay = jnp.exp(jnp.where(incl, gc[..., :, None] - gc[..., None, :], -jnp.inf))
    kb = k * beta[..., None]
    lmat = jnp.where(strict, jnp.einsum("bhnik,bhnjk->bhnij", kb, k) * decay, 0.0)
    eye = jnp.eye(GDN_CHUNK, dtype=q.dtype)
    tinv = lax.linalg.triangular_solve(eye + lmat, jnp.broadcast_to(eye, lmat.shape), left_side=True,
                                       lower=True, unit_diagonal=True)
    u = tinv @ (v * beta[..., None])
    w = tinv @ (kb * jnp.exp(gc)[..., None])
    attn = jnp.einsum("bhnik,bhnjk->bhnij", q, k) * decay
    qg = q * jnp.exp(gc)[..., None]
    kdec = k * jnp.exp(gc[..., -1:] - gc)[..., None]
    glast = jnp.exp(gc[..., -1])

    def step(S, xs):
        qg_c, kdec_c, u_c, w_c, attn_c, glast_c = xs
        v_new = u_c - jnp.einsum("bhck,bhkv->bhcv", w_c, S)
        o = jnp.einsum("bhck,bhkv->bhcv", qg_c, S) + jnp.einsum("bhij,bhjv->bhiv", attn_c, v_new)
        S = S * glast_c[..., None, None] + jnp.einsum("bhck,bhcv->bhkv", kdec_c, v_new)
        return S, o

    xs = tuple(jnp.moveaxis(t, 2, 0) for t in (qg, kdec, u, w, attn, glast))
    s_fin, o = lax.scan(step, s0, xs)
    o = jnp.moveaxis(o, 0, 2).reshape(b, h, l, -1)
    return jnp.swapaxes(o, 1, 2), s_fin

def _ssd_chunked(x, dt, a_neg, bm, cm, s0):
    b, l, h, p = x.shape
    g, s = bm.shape[2], bm.shape[3]
    r = h // g
    n = l // SSD_CHUNK
    c = SSD_CHUNK
    xr = x.reshape(b, n, c, g, r, p)
    dtr = dt.reshape(b, n, c, g, r)
    acum = jnp.cumsum((dt * a_neg).reshape(b, n, c, g, r), axis=2)
    bmr = bm.reshape(b, n, c, g, s)
    cmr = cm.reshape(b, n, c, g, s)
    incl = jnp.tril(jnp.ones((c, c), dtype=bool))
    seg = acum[:, :, :, None] - acum[:, :, None, :]
    decay = jnp.exp(jnp.where(incl[:, :, None, None], seg, -jnp.inf))
    cb = jnp.einsum("bnigs,bnjgs->bnijg", cmr, bmr)
    y_diag = jnp.einsum("bnijg,bnijgr,bnjgrp->bnigrp", cb, decay, dtr[..., None] * xr)
    x_end = xr * (dtr * jnp.exp(acum[:, :, -1:] - acum))[..., None]
    states = jnp.einsum("bncgs,bncgrp->bngrps", bmr, x_end)
    chunk_decay = jnp.exp(acum[:, :, -1])

    def step(hst, xs):
        st, cd = xs
        return hst * cd[..., None, None] + st, hst

    h_fin, h_prev = lax.scan(step, s0.reshape(b, g, r, p, s),
                             (jnp.moveaxis(states, 1, 0), jnp.moveaxis(chunk_decay, 1, 0)))
    h_prev = jnp.moveaxis(h_prev, 0, 1)
    y_off = jnp.einsum("bncgs,bngrps->bncgrp", cmr, h_prev) * jnp.exp(acum)[..., None]
    y = (y_diag + y_off).reshape(b, l, h, p)
    return y, h_fin.reshape(b, h, p, s)

def _token_mixer(h, s_gdn0, s_ssd0, lp):
    f32 = jnp.float32
    b, l, _ = h.shape
    proj = h @ lp["w_in"]
    qkv, z_g, beta_raw, a_raw, xbc, z_s, dt_raw, gate_raw = _split_cols(proj, IN_SPLITS)
    qkv = jax.nn.silu(_dwconv_centred(qkv, lp["gdn_conv_w"], lp["gdn_conv_b"])).astype(f32)
    q, k, v = _split_cols(qkv, (GDN_HEADS * GDN_DK, GDN_HEADS * GDN_DK, GDN_HEADS * GDN_DV))
    q = _l2norm(q.reshape(b, l, GDN_HEADS, GDN_DK)) * (GDN_DK ** -0.5)
    k = _l2norm(k.reshape(b, l, GDN_HEADS, GDN_DK))
    v = v.reshape(b, l, GDN_HEADS, GDN_DV)
    beta = jax.nn.sigmoid(beta_raw.astype(f32)).reshape(b, l, 2, GDN_HEADS)
    gdec = -jnp.exp(lp["gdn_a_log"].astype(f32)) * jax.nn.softplus(
        a_raw.astype(f32).reshape(b, l, 2, GDN_HEADS) + lp["gdn_dt_bias"].astype(f32))
    s0g = s_gdn0.astype(f32)
    o_f, sg_f = _gdn_chunked(q, k, v, beta[:, :, 0], gdec[:, :, 0], s0g[:, 0])
    o_b, sg_b = _gdn_chunked(_flip(q), _flip(k), _flip(v), _flip(beta[:, :, 1]), _flip(gdec[:, :, 1]), s0g[:, 1])
    o = _rms(o_f + _flip(o_b)) * lp["gdn_norm_w"].astype(f32) * jax.nn.silu(
        z_g.astype(f32).reshape(b, l, GDN_HEADS, GDN_DV))
    u_g = o.reshape(b, l, GDN_HEADS * GDN_DV).astype(h.dtype) @ lp["w_gdn_out"]
    xbc = jax.nn.silu(_dwconv_centred(xbc, lp["ssd_conv_w"], lp["ssd_conv_b"])).astype(f32)
    xs, bm, cm = _split_cols(xbc, (SSD_INNER, SSD_GROUPS * SSD_N, SSD_GROUPS * SSD_N))
    xs = xs.reshape(b, l, SSD_HEADS, SSD_P)
    bm = bm.reshape(b, l, SSD_GROUPS, SSD_N)
    cm = cm.reshape(b, l, SSD_GROUPS, SSD_N)
    dt = jax.nn.softplus(dt_raw.astype(f32).reshape(b, l, 2, SSD_HEADS) + lp["ssd_dt_bias"].astype(f32))
    a_neg = -jnp.exp(lp["ssd_a_log"].astype(f32))
    s0s = s_ssd0.astype(f32)
    y_f, ss_f = _ssd_chunked(xs, dt[:, :, 0], a_neg[0], bm, cm, s0s[:, 0])
    y_b, ss_b = _ssd_chunked(_flip(xs), _flip(dt[:, :, 1]), a_neg[1], _flip(bm), _flip(cm), s0s[:, 1])
    y = y_f + _flip(y_b) + lp["ssd_d"].astype(f32)[:, None] * xs
    y = y.reshape(b, l, SSD_INNER) * jax.nn.silu(z_s.astype(f32))
    y = _rms(y.reshape(b, l, SSD_GROUPS, SSD_INNER // SSD_GROUPS)).reshape(b, l, SSD_INNER)
    y = y * lp["ssd_norm_w"].astype(f32)
    u_s = y.astype(h.dtype) @ lp["w_ssd_out"]
    gate_g, gate_s = jnp.split(gate_raw, 2, axis=-1)
    m = jax.nn.sigmoid(gate_g) * u_g + jax.nn.sigmoid(gate_s) * u_s
    out = m @ lp["w_o"]
    return out, jnp.stack([sg_f, sg_b], axis=1), jnp.stack([ss_f, ss_b], axis=1)

def _hier_moe(h, lp):
    f32 = jnp.float32
    hf = h.astype(f32)
    p_grp = jax.nn.softmax(hf @ lp["w_router_group"].astype(f32) + lp["b_router_group"].astype(f32), axis=-1)
    p_top, g_idx = lax.top_k(p_grp, 1)
    le = (hf @ lp["w_router_expert"].astype(f32) + lp["b_router_expert"].astype(f32)).reshape(
        *h.shape[:-1], N_GROUPS, EXPERTS_PER_GROUP)
    le_sel = jnp.einsum("blge,blg->ble", le, jax.nn.one_hot(g_idx[..., 0], N_GROUPS, dtype=f32))
    p_e = jax.nn.softmax(le_sel, axis=-1)
    w_top, e_idx = lax.top_k(p_e, TOP_K_IN_GROUP)
    w_top = w_top / jnp.sum(w_top, axis=-1, keepdims=True) * p_top
    expert_id = g_idx * EXPERTS_PER_GROUP + e_idx
    gates = jnp.sum(jax.nn.one_hot(expert_id, N_EXPERTS, dtype=f32) * w_top[..., None], axis=-2)
    hidden = jax.nn.silu(jnp.einsum("bld,edf->blef", h, lp["w_exp_gate"])) * jnp.einsum(
        "bld,edf->blef", h, lp["w_exp_up"])
    hidden = hidden * gates.astype(h.dtype)[..., None]
    return jnp.einsum("blef,efd->bld", hidden, lp["w_exp_down"])

def _adaln(cvec, w, b):
    return (jax.nn.silu(cvec.astype(jnp.float32)) @ w.astype(jnp.float32) + b.astype(jnp.float32))[:, None, :]

def _layer(x, ada, s_gdn0, s_ssd0, lp):
    shift1, scale1, gate1, shift2, scale2, gate2 = jnp.split(ada.astype(x.dtype), 6, axis=-1)
    h = _layernorm(x) * (1 + scale1) + shift1
    mix, s_gdn, s_ssd = _token_mixer(h, s_gdn0, s_ssd0, lp)
    x = _layernorm(ALPHA * x + gate1 * mix, lp["ln1_g"], lp["ln1_b"])
    h = _layernorm(x) * (1 + scale2) + shift2
    x = _layernorm(ALPHA * x + gate2 * _hier_moe(h, lp), lp["ln2_g"], lp["ln2_b"])
    return x, s_gdn, s_ssd

def setup_inputs(seed: int = 0) -> dict:
    key = jax.random.key(seed)
    ks = iter(jax.random.split(key, 48))
    f32 = jnp.float32
    beta_dn = (8.0 * DEPTH) ** -0.25

    def nrm(shape, scale):
        return jax.random.normal(next(ks), shape, f32) * scale

    def dt_bias(shape):
        u = jax.random.uniform(next(ks), shape, f32)
        dt = jnp.exp(u * (math.log(DT_MAX) - math.log(DT_MIN)) + math.log(DT_MIN))
        return dt + jnp.log(-jnp.expm1(-dt))

    def a_log(shape):
        return jnp.log(jax.random.uniform(next(ks), shape, f32, 1.0, 16.0))

    conv_ch_g = 2 * GDN_HEADS * GDN_DK + GDN_HEADS * GDN_DV
    conv_ch_s = SSD_INNER + 2 * SSD_GROUPS * SSD_N
    return {
        "x_prompt": nrm((BATCH, SEQ, D_MODEL), 1.0),
        "x_sample": nrm((DEC_BATCH, DEC_SEQ, D_MODEL), 1.0),
        "state_gdn": nrm((DEC_BATCH, DEPTH, 2, GDN_HEADS, GDN_DK, GDN_DV), 0.1),
        "state_ssd": nrm((DEC_BATCH, DEPTH, 2, SSD_HEADS, SSD_P, SSD_N), 0.1),
        "c": nrm((DEC_BATCH, D_MODEL), 1.0),
        "c_ctx": nrm((D_MODEL,), 1.0),
        "w_ada": nrm((DEPTH, D_MODEL, 6 * D_MODEL), 0.5 * D_MODEL ** -0.5),
        "b_ada": nrm((DEPTH, 6 * D_MODEL), 0.02),
        "w_in": nrm((DEPTH, D_MODEL, IN_COLS), D_MODEL ** -0.5),
        "gdn_conv_w": nrm((DEPTH, CONV_K, conv_ch_g), CONV_K ** -0.5),
        "gdn_conv_b": nrm((DEPTH, conv_ch_g), 0.02),
        "gdn_a_log": a_log((DEPTH, 2, GDN_HEADS)),
        "gdn_dt_bias": dt_bias((DEPTH, 2, GDN_HEADS)),
        "gdn_norm_w": 1.0 + nrm((DEPTH, GDN_DV), 0.02),
        "w_gdn_out": nrm((DEPTH, GDN_HEADS * GDN_DV, D_MODEL), beta_dn * (GDN_HEADS * GDN_DV) ** -0.5),
        "ssd_conv_w": nrm((DEPTH, CONV_K, conv_ch_s), CONV_K ** -0.5),
        "ssd_conv_b": nrm((DEPTH, conv_ch_s), 0.02),
        "ssd_a_log": a_log((DEPTH, 2, SSD_HEADS)),
        "ssd_dt_bias": dt_bias((DEPTH, 2, SSD_HEADS)),
        "ssd_d": 1.0 + nrm((DEPTH, SSD_HEADS), 0.02),
        "ssd_norm_w": 1.0 + nrm((DEPTH, SSD_INNER), 0.02),
        "w_ssd_out": nrm((DEPTH, SSD_INNER, D_MODEL), beta_dn * SSD_INNER ** -0.5),
        "w_o": nrm((DEPTH, D_MODEL, D_MODEL), beta_dn * D_MODEL ** -0.5),
        "ln1_g": 1.0 + nrm((DEPTH, D_MODEL), 0.02),
        "ln1_b": nrm((DEPTH, D_MODEL), 0.02),
        "w_router_group": nrm((DEPTH, D_MODEL, N_GROUPS), D_MODEL ** -0.5),
        "b_router_group": nrm((DEPTH, N_GROUPS), 0.01),
        "w_router_expert": nrm((DEPTH, D_MODEL, N_EXPERTS), D_MODEL ** -0.5),
        "b_router_expert": nrm((DEPTH, N_EXPERTS), 0.01),
        "w_exp_gate": nrm((DEPTH, N_EXPERTS, D_MODEL, D_EXPERT), D_MODEL ** -0.5),
        "w_exp_up": nrm((DEPTH, N_EXPERTS, D_MODEL, D_EXPERT), D_MODEL ** -0.5),
        "w_exp_down": nrm((DEPTH, N_EXPERTS, D_EXPERT, D_MODEL), beta_dn * D_EXPERT ** -0.5),
        "ln2_g": 1.0 + nrm((DEPTH, D_MODEL), 0.02),
        "ln2_b": nrm((DEPTH, D_MODEL), 0.02),
    }

def reference(x_prompt, x_sample, state_gdn, state_ssd, c, c_ctx, w_ada, b_ada, w_in, gdn_conv_w, gdn_conv_b,
              gdn_a_log, gdn_dt_bias, gdn_norm_w, w_gdn_out, ssd_conv_w, ssd_conv_b, ssd_a_log, ssd_dt_bias,
              ssd_d, ssd_norm_w, w_ssd_out, w_o, ln1_g, ln1_b, w_router_group, b_router_group,
              w_router_expert, b_router_expert, w_exp_gate, w_exp_up, w_exp_down, ln2_g, ln2_b):
    f32 = jnp.float32
    xc = x_prompt
    pos = _grid_pos_embed(x_sample.shape[1], D_MODEL)
    xl = x_sample + pos.astype(x_sample.dtype)[None]
    zeros_gdn = jnp.zeros((xc.shape[0], 2, GDN_HEADS, GDN_DK, GDN_DV), f32)
    zeros_ssd = jnp.zeros((xc.shape[0], 2, SSD_HEADS, SSD_P, SSD_N), f32)
    new_gdn, new_ssd = [], []
    for l in range(DEPTH):
        lp = {
            "w_in": w_in[l], "gdn_conv_w": gdn_conv_w[l], "gdn_conv_b": gdn_conv_b[l],
            "gdn_a_log": gdn_a_log[l], "gdn_dt_bias": gdn_dt_bias[l], "gdn_norm_w": gdn_norm_w[l],
            "w_gdn_out": w_gdn_out[l], "ssd_conv_w": ssd_conv_w[l], "ssd_conv_b": ssd_conv_b[l],
            "ssd_a_log": ssd_a_log[l], "ssd_dt_bias": ssd_dt_bias[l], "ssd_d": ssd_d[l],
            "ssd_norm_w": ssd_norm_w[l], "w_ssd_out": w_ssd_out[l], "w_o": w_o[l],
            "ln1_g": ln1_g[l], "ln1_b": ln1_b[l], "w_router_group": w_router_group[l],
            "b_router_group": b_router_group[l], "w_router_expert": w_router_expert[l],
            "b_router_expert": b_router_expert[l], "w_exp_gate": w_exp_gate[l], "w_exp_up": w_exp_up[l],
            "w_exp_down": w_exp_down[l], "ln2_g": ln2_g[l], "ln2_b": ln2_b[l],
        }
        ada_ctx = _adaln(c_ctx[None], w_ada[l], b_ada[l])
        ada_lat = _adaln(c, w_ada[l], b_ada[l])
        xc, s_g, s_s = _layer(xc, ada_ctx, zeros_gdn, zeros_ssd, lp)
        xl, _, _ = _layer(xl, ada_lat, state_gdn[:, l], state_ssd[:, l], lp)
        new_gdn.append(s_g)
        new_ssd.append(s_s)
    new_state_gdn = jnp.stack(new_gdn, axis=1).astype(x_prompt.dtype)
    new_state_ssd = jnp.stack(new_ssd, axis=1).astype(x_prompt.dtype)
    return (xc, xl, new_state_gdn, new_state_ssd)


_drawn_inputs = setup_inputs


def setup_inputs(seed=0):
    import zlib

    import numpy as np

    out = dict(_drawn_inputs(seed))
    spreads = {}
    factors = {'state_gdn': 8.0,
     'state_ssd': 8.0,
     'gdn_norm_w': 64.0,
     'ssd_d': 64.0,
     'ssd_norm_w': 62.345,
     'ln1_g': 8.103,
     'ln1_b': 7.952,
     'b_router_group': 64.0,
     'b_router_expert': 64.0,
     'ln2_g': 7.543,
     'ln2_b': 7.776,
     'w_router_group': 3.9,
     'w_router_expert': 3.897,
     'w_exp_gate': 3.683,
     'w_exp_up': 3.489,
     'w_exp_down': 3.484}
    for name, (base, spread) in spreads.items():
        noise = np.random.default_rng([zlib.crc32(name.encode()), seed]).standard_normal(out[name].shape)
        drawn = base * np.exp(spread * noise) if base else spread * noise
        out[name] = jnp.asarray(drawn.astype(out[name].dtype))
    for name, factor in factors.items():
        out[name] = (out[name] * factor).astype(out[name].dtype)
    return out
```

```python
from contextlib import ExitStack

import numpy as np

import concourse.bass as bass
from concourse import mybir

F32 = mybir.dt.float32
I32 = mybir.dt.int32
U32 = mybir.dt.uint32
ACT = mybir.ActivationFunctionType
ALU = mybir.AluOpType
AX = mybir.AxisListType

P = 128
SEQ, DEC = 128, 512
NT = (SEQ + DEC) // P
T = NT * P
D = 1024
KD = D // P
GH = 8
SH, SP_, SG, SN = 32, 64, 4, 128
HG = SH // SG
TAPS = 5
NST = 2 * GH + 2 * SH
O_QKV, O_ZG = 0, 3 * D
O_BETA = O_ZG + D
O_A = O_BETA + 2 * GH
O_XBC = O_A + 2 * GH
O_ZS = O_XBC + SH * SP_ + 2 * SG * SN
O_DT = O_ZS + SH * SP_
O_GATE = O_DT + 2 * SH
NX = 32
XG, XE = 4, 8
FX = 256
ALPHA = 2.0 ** 0.25
EPS = 1e-6
PADW = 2 + SEQ + 2 + 2 + DEC + 2
CW = PADW - 4
LAT = SEQ + 4

(C_ID, C_LE, C_GE, C_GT, C_LT, C_ONE, C_N1F, C_N1B) = range(8)
NC_ = 8
LEVELS = 6


def constants():
    k = np.arange(P)[:, None]
    i = np.arange(P)[None, :]

    def below(s):
        return ((k // s) == (i // s) + 1) & ((i // s) % 2 == 0)

    c = [k == i, k <= i, k >= i, k > i, k < i, np.ones((P, P), bool), below(1).T, below(1)]
    c = [m.astype(np.float32) for m in c]
    c[C_N1F] = -c[C_N1F]
    c[C_N1B] = -c[C_N1B]
    levels = []
    for n in range(LEVELS):
        m = below(2 << n).astype(np.float32)
        levels += [-m, -m.T]
    return np.stack(c, 1), np.stack(levels, 1)


NMORE = (2 * T) // (P + 1)
NPLACE = (NX + NMORE) * P
(S_E, S_LIST, S_GRP, S_TOK, S_MORE, S_FAR) = (0, NX, 2 * NX, 2 * NX + XG, 2 * NX + XG + NT, 2 * NX + XG + NT + NMORE)
NCOL = S_FAR + NX


def small_constants():
    row = np.concatenate([np.arange(NX), np.arange(NX) * P, XG - np.arange(XG)])
    end = np.concatenate([np.arange(NMORE), (NX - 1 - np.arange(NX)) * P])
    tok = np.arange(P)[:, None] + P * np.arange(NT)[None, :]
    return np.concatenate([np.broadcast_to(row, (P, row.size)), tok, np.broadcast_to(end, (P, end.size))], 1).astype(np.float32)


def positions():
    n, q = DEC, D // 4
    rr = (np.arange(n) // 64).astype(np.float32)[:, None]
    cc = (np.arange(n) % 64).astype(np.float32)[:, None]
    f = np.exp((-np.log(np.float32(10000.0)) * np.arange(q, dtype=np.float32) / q).astype(np.float32)).astype(np.float32)
    return np.concatenate([np.sin(rr * f), np.cos(rr * f), np.sin(cc * f), np.cos(cc * f)], -1).astype(np.float32)



class Steps:

    def __init__(self, eng, sem, base=0, held=False):
        self.eng, self.sem, self.base, self.n, self.held = eng, sem, base, 0, held

    def add(self, ins):
        ins.then_inc(self.sem, 1)
        self.n += 1

    def wait(self, back=0):
        if self.held:
            hold(self.eng, self.sem, self.base + (self.n - back))
        else:
            self.eng.wait_ge(self.sem, self.base + (self.n - back))

    def link(self, ins):
        self.add(ins)
        self.wait()


def hold(eng, sem, value):
    value = eng.to_reg(value)
    eng.wait_ge(sem, 1)
    eng.wait_ge(sem, value)


def build(nc, x_prompt, x_sample, state_gdn, state_ssd, c, c_ctx, w_ada, b_ada, w_in, gdn_conv_w, gdn_conv_b,
          gdn_a_log, gdn_dt_bias, gdn_norm_w, w_gdn_out, ssd_conv_w, ssd_conv_b, ssd_a_log, ssd_dt_bias,
          ssd_d, ssd_norm_w, w_ssd_out, w_o, ln1_g, ln1_b, w_router_group, b_router_group,
          w_router_expert, b_router_expert, w_exp_gate, w_exp_up, w_exp_down, ln2_g, ln2_b,
          const, small, levels, pos, y_prompt, y_sample, new_gdn, new_ssd):
    top = ExitStack()
    def sb(name, shape, dt=F32, where=None):
        return (where or top).enter_context(nc.sbuf_tensor(name, shape, dt))

    def stage(fn, *args):
        with ExitStack() as stack:
            taken = []

            def sem(name):
                taken.append(stack.enter_context(nc.semaphore(name)))
                return taken[-1]

            fn(nc, sb, sem, *args)
            with nc.Block() as block:
                @block.gpsimd
                def _(pool):
                    for one in taken:
                        pool.sem_clear(one)

    sem = lambda name: top.enter_context(nc.semaphore(name))

    with top:
        bank = [top.enter_context(nc.psum_tensor(f"bank{i}", [P, 512], F32)) for i in range(8)]
        cst = sb("cst", [P, NC_, P])
        cols = sb("cols", [P, NCOL])
        half = sb("half", [P, 16])
        C = lambda n: cst[:, n, :]
        ada = nc.dram_tensor("ada", [2, 6 * D], F32, kind="Internal").ap()
        h2d = nc.dram_tensor("h2d", [T, D], F32, kind="Internal").ap()
        lists = nc.dram_tensor("lists", [NPLACE, 1], F32, kind="Internal").ap()
        yd = nc.dram_tensor("yd", [NPLACE, D], F32, kind="Internal").ap()
        mix_stack = ExitStack()
        with mix_stack:
            shared = sb("shared", [P, 6 * KD * P], F32, mix_stack)
            mT = shared[:, 0:KD * T].rearrange("p (k t) -> p k t", k=KD)
            bulk = ExitStack()
            with bulk:
                hT = sb("hT", [P, KD, T], F32, bulk)
                modT = sb("modT", [P, 2, KD, 2], F32, bulk)
                cwT = sb("cwT", [P, 2, TAPS, 24], F32, bulk)
                vecT = sb("vecT", [P, 2 * 24 + 1 + 16], F32, bulk)
                ST = sb("ST", [P, 5, NT, NST], F32, bulk)
                stage(condition, bank, cst, C, cols, hT, ada, modT, cwT, vecT, half, x_prompt, x_sample, c, c_ctx, w_ada,
                          b_ada, gdn_conv_w, gdn_conv_b, gdn_norm_w, ssd_conv_w, ssd_conv_b, ssd_norm_w, const, small, pos)
                stage(statistics, bank, cst, C, hT, ST, w_in, gdn_a_log, gdn_dt_bias, ssd_a_log, ssd_dt_bias)
                yT = sb("yT", [P, SH * SP_ // P, T], F32, bulk)
                stage(ssd, bank, cst, C, hT, ST, cwT, vecT, half, shared, yT, w_in, ssd_d, state_ssd, new_ssd)
                oT = sb("oT", [P, KD, T], F32, bulk)
                stage(deltanet, bank, cst, C, hT, ST, cwT, vecT, half, shared, oT, levels, w_in, state_gdn, new_gdn)
                stage(merge, bank, hT, oT, yT, mT, w_in, w_gdn_out, w_ssd_out)
            x1d = nc.dram_tensor("x1d", [T, D], F32, kind="Internal").ap()
            tail = ExitStack()
            with tail:
                idx = sb("idx", [P, NX], U32, tail)
                slots = sb("slots", [P, NT, 2], U32, tail)
                wts = sb("wts", [P, NT, 2], F32, tail)
                more = sb("more", [P, NMORE + 1], U32, tail)
                stage(route, bank, C, cols, half, mT, ada, pos, x_prompt, x_sample, w_o, ln1_g, ln1_b, w_router_group,
                      b_router_group, w_router_expert, b_router_expert, h2d, x1d, lists, yd, idx, slots, wts, more)
                stage(experts, bank, C, idx, more, lists, h2d, yd, w_exp_gate, w_exp_up, w_exp_down)
                stage(combine, half, slots, wts, yd, x1d, ada, ln2_g, ln2_b, y_prompt, y_sample)


def condition(nc, sb, sem, bank, cst, C, cols, hT, ada, modT, cwT, vecT, half, x_prompt, x_sample, c,
              c_ctx, w_ada, b_ada, gdn_conv_w, gdn_conv_b, gdn_norm_w, ssd_conv_w, ssd_conv_b, ssd_norm_w, const, small, pos):
    NCH = 6 * D // 512
    own = ExitStack()
    with own:
        S = lambda name, shape, dt=F32: sb(name, shape, dt, own)
        x = S("x", [P, NT, D])
        crow = S("crow", [2 * KD, P])
        cth = S("cth", [2 * KD, P])
        csil = S("csil", [2 * KD, P])
        cT = S("cT", [P, 2, KD])
        cwrow = S("cwrow", [TAPS * 24, 2, P])
        vrow = S("vrow", [65, P])
        aw = S("aw", [P, 2, KD, 512])
        brow = S("brow", [2, 6 * D])
        arow = S("arow", [2, 6 * D])
        post = S("post", [P, NT - 1, D])
        xn = S("xn", [P, NT, D])
        bn = S("bn", [P, NT, 2, 6])
        mv = S("mv", [P, NT, 2])
        rstd = S("rstd", [P, NT])
        ve = S("ve", [P, NT])
        const_in, c_in, rows_in, b_in = sem("const_in"), sem("c_in"), sem("rows_in"), sem("b_in")
        x_in = [sem(f"x_in{t}") for t in range(NT)]
        pos_in = sem("pos_in")
        aw_in = [sem("aw_in0"), sem("aw_in1")]
        c_tanh, c_silu, c_turned, c_ready = sem("c_tanh"), sem("c_silu"), sem("c_turned"), sem("c_ready")
        half_ready, stats_ready, rstd_ready = sem("half_ready"), sem("stats_ready"), sem("rstd_ready")
        ada_done, ada_kept = sem("ada_done"), sem("ada_kept")
        rows_turned, rows_kept = sem("rows_turned"), sem("rows_kept")
        ada_out = sem("ada_out")
        mods_turned, mods_ready = sem("mods_turned"), sem("mods_ready")
        x_turned, h_dve, h_act = sem("x_turned"), sem("h_dve"), sem("h_act")
        xn_ready = sem("xn_ready")
        own_dve = sem("own_dve1")

        with nc.Block() as block:
            @block.sync
            def _(sp):
                sp.dma_start(crow[0:KD, :], c_ctx.rearrange("(k p) -> k p", p=P)).then_inc(c_in, 16)
                sp.dma_start(crow[KD:2 * KD, :], c.rearrange("a (k p) -> (a k) p", p=P)).then_inc(c_in, 16)
                sp.dma_start(cst[:, :, :], const).then_inc(const_in, 16)
                sp.dma_start(cols[:, :], small).then_inc(const_in, 16)

                def load(n, par):
                    src = w_ada[0, :, bass.ds(n * 512, 512)].rearrange("(k p) n -> p k n", p=P)
                    sp.dma_start(aw[:, par, :, :], src).then_inc(aw_in[par], 16)

                load(0, 0)
                load(1, 1)
                with sp.Fori(0, NCH // 2 - 1) as i:
                    for par in range(2):
                        sp.wait_ge(ada_done, 2 * i + par + 1)
                        load(2 * i + par + 2, par)
                sp.wait_ge(ada_out, 16)

            @block.scalar
            def _(act):
                act.dma_start(brow[:, :], b_ada[0, :].partition_broadcast(2)).then_inc(b_in, 16)
                act.dma_start(x[:, 0, :], x_prompt[0]).then_inc(x_in[0], 16)
                for t in range(1, NT):
                    act.dma_start(x[:, t, :], x_sample[0, (t - 1) * P:t * P, :]).then_inc(x_in[t], 16)
                act.dma_start(post[:, :, :], pos.rearrange("(t p) d -> p t d", p=P)).then_inc(pos_in, 16)
                act.dma_start(cwrow[:, 0, :], gdn_conv_w[0].rearrange("k (n p) -> (k n) p", p=P)).then_inc(rows_in, 16)
                act.dma_start(cwrow[:, 1, :], ssd_conv_w[0].rearrange("k (n p) -> (k n) p", p=P)).then_inc(rows_in, 16)
                act.dma_start(vrow[0:24, :], gdn_conv_b[0].rearrange("(n p) -> n p", p=P)).then_inc(rows_in, 16)
                act.dma_start(vrow[24:48, :], ssd_conv_b[0].rearrange("(n p) -> n p", p=P)).then_inc(rows_in, 16)
                act.dma_start(vrow[48:49, :], gdn_norm_w).then_inc(rows_in, 16)
                act.dma_start(vrow[49:65, :], ssd_norm_w[0].rearrange("(n p) -> n p", p=P)).then_inc(rows_in, 16)
                act.wait_ge(c_in, 32)
                act.activation(cth[:, :], crow[:, :], ACT.Tanh, scale=0.5).then_inc(c_tanh, 1)
                act.wait_ge(ada_kept, NCH)
                act.dma_start(ada, arow[:, :]).then_inc(ada_out, 16)
                act.wait_ge(mods_ready, 1)
                for t in range(NT):
                    cond = min(t, 1)
                    act.wait_ge(x_turned, 2 * t + 2)
                    for k in range(4, 8):
                        last = act.activation(hT[:, k, t * P:(t + 1) * P], bank[(2 * t + 1) % 8][:, (k - 4) * P:(k - 3) * P],
                                              ACT.Identity, bias=modT[:, 0, k, cond:cond + 1],
                                              scale=modT[:, 1, k, cond:cond + 1])
                    last.then_inc(h_act, 1)

            @block.gpsimd
            def _(pool):
                nc.gpsimd.memset(half[:, :], -0.5).then_inc(half_ready, 1)
                pool.wait_ge(half_ready, 1)
                for t in range(NT):
                    pool.wait_ge(stats_ready, t + 1)
                    pool.tensor_tensor(out=rstd[:, t:t + 1], in0=ve[:, t:t + 1], in1=half[:, 0:1],
                                       op=ALU.pow).then_inc(rstd_ready, 1)

            @block.vector
            def _(dve):
                st = Steps(dve, own_dve)
                dve.wait_ge(c_tanh, 1)
                st.link(dve.scalar_tensor_tensor(out=csil[:, :], in0=cth[:, :], scalar=1.0, in1=crow[:, :],
                                                 op0=ALU.add, op1=ALU.mult))
                dve.tensor_scalar(out=csil[:, :], in0=csil[:, :], scalar1=0.5, scalar2=None, op0=ALU.mult).then_inc(c_silu, 1)
                dve.wait_ge(c_turned, 1)
                dve.tensor_copy(cT[:, :, :], bank[0][:, 0:2 * KD].rearrange("p (a k) -> p a k", a=2)).then_inc(c_ready, 1)
                dve.wait_ge(rows_turned, 1)
                dve.tensor_copy(cwT[:, :, :, :], bank[1][:, 0:240].rearrange("p (a k n) -> p a k n", a=2, k=TAPS))
                dve.tensor_copy(vecT[:, :], bank[1][:, 256:256 + 65]).then_inc(rows_kept, 1)
                dve.wait_ge(pos_in, 16)
                for t in range(NT):
                    dve.wait_ge(x_in[t], 16)
                    if t > 0:
                        st.link(dve.tensor_tensor(out=x[:, t, :], in0=x[:, t, :], in1=post[:, t - 1, :], op=ALU.add))
                    dve.bn_stats(bn[:, t, 0, :], x[:, t, 0:512])
                    st.link(dve.bn_stats(bn[:, t, 1, :], x[:, t, 512:1024]))
                    st.link(dve.bn_aggr(mv[:, t, :], bn[:, t, :, :]))
                    dve.tensor_scalar(out=ve[:, t:t + 1], in0=mv[:, t, 1:2], scalar1=EPS, scalar2=None,
                                      op0=ALU.add).then_inc(stats_ready, 1)
                for t in range(NT):
                    dve.wait_ge(rstd_ready, t + 1)
                    dve.tensor_scalar(out=xn[:, t, :], in0=x[:, t, :], scalar1=mv[:, t, 0:1], scalar2=rstd[:, t:t + 1],
                                      op0=ALU.subtract, op1=ALU.mult).then_inc(xn_ready, 1)
                dve.wait_ge(b_in, 16)

                def keep(n, par):
                    dve.wait_ge(ada_done, n + 1)
                    dve.tensor_tensor(out=arow[:, bass.ds(n * 512, 512)], in0=bank[2 + par][0:2, :],
                                      in1=brow[:, bass.ds(n * 512, 512)], op=ALU.add).then_inc(ada_kept, 1)

                with dve.Fori(0, NCH // 2) as i:
                    for par in range(2):
                        keep(2 * i + par, par)
                dve.wait_ge(mods_turned, 1)
                for m in range(2):
                    last = dve.tensor_scalar(out=modT[:, m, :, :], in0=bank[0][:, m * 16:(m + 1) * 16],
                                             scalar1=float(m % 2), scalar2=None, op0=ALU.add)
                last.then_inc(mods_ready, 1)
                dve.wait_ge(mods_ready, 1)
                for t in range(NT):
                    cond = min(t, 1)
                    dve.wait_ge(x_turned, 2 * t + 1)
                    for k in range(4):
                        last = dve.tensor_scalar(out=hT[:, k, t * P:(t + 1) * P], in0=bank[2 * t % 8][:, k * P:(k + 1) * P],
                                                 scalar1=modT[:, 1, k, cond:cond + 1], scalar2=modT[:, 0, k, cond:cond + 1],
                                                 op0=ALU.mult, op1=ALU.add)
                    last.then_inc(h_dve, 1)

            @block.tensor
            def _(pe):
                pe.wait_ge(const_in, 32)
                pe.wait_ge(c_silu, 1)
                pe.transpose(bank[0][:, 0:2 * KD], csil[:, :], cst[0:2 * KD, C_ID, 0:2 * KD]).then_inc(c_turned, 1)
                pe.wait_ge(rows_in, 96)
                for a in range(2):
                    pe.transpose(bank[1][:, a * 120:(a + 1) * 120], cwrow[:, a, :], cst[0:120, C_ID, 0:120])
                pe.transpose(bank[1][:, 256:256 + 65], vrow[:, :], cst[0:65, C_ID, 0:65]).then_inc(rows_turned, 1)
                pe.wait_ge(c_ready, 1)

                def chunk(i, par, first):
                    pe.wait_ge(aw_in[par], 16 * (i + 1))
                    if not first:
                        pe.wait_ge(ada_kept, 2 * i + par - 1)
                    for k in range(KD):
                        last = pe.matmul(bank[2 + par][0:2, :], cT[:, :, k], aw[:, par, k, :], start=(k == 0), stop=(k == KD - 1))
                    last.then_inc(ada_done, 1)

                chunk(0, 0, True)
                chunk(0, 1, True)
                with pe.Fori(1, NCH // 2) as i:
                    for par in range(2):
                        chunk(i, par, False)
                pe.wait_ge(ada_kept, NCH)
                pe.wait_ge(rows_kept, 1)
                for m, at in enumerate((0, 1)):
                    for k in range(KD):
                        last = pe.transpose(bank[0][:, m * 16 + 2 * k:m * 16 + 2 * k + 2],
                                            arow[:, at * D + k * P:at * D + (k + 1) * P], cst[0:2, C_ID, 0:2])
                last.then_inc(mods_turned, 1)
                pe.wait_ge(mods_ready, 1)
                for t in range(NT):
                    pe.wait_ge(xn_ready, t + 1)
                    for h in range(2):
                        if t == NT - 1:
                            pe.wait_ge((h_dve, h_act)[h], 1)
                        for k in range(4):
                            last = pe.transpose(bank[(2 * t + h) % 8][:, k * P:(k + 1) * P],
                                                xn[:, t, (4 * h + k) * P:(4 * h + k + 1) * P], C(C_ID))
                        last.then_inc(x_turned, 1)


def statistics(nc, sb, sem, bank, cst, C, hT, ST, w_in, gdn_a_log, gdn_dt_bias, ssd_a_log, ssd_dt_bias):
    own = ExitStack()
    with own:
        S = lambda name, shape, dt=F32: sb(name, shape, dt, own)
        NS = 2 * GH + NST
        ws = S("ws", [P, KD, NS])
        bias = S("bias", [P, NST])
        alog = S("alog", [P, NST])
        aexp = S("aexp", [P, NST])
        raw = S("raw", [P, NT, NS])
        z = S("z", [P, NT, NST])
        m = S("m", [P, NT, NST])
        e = S("e", [P, NT, NST])
        u = S("u", [P, NT, NST])
        d = S("d", [P, NT, NST])
        isz = S("isz", [P, NT, NST])
        lu = S("lu", [P, NT, NST])
        eb = S("eb", [P, NT, 2 * GH])
        ws_in, small_in = sem("ws_in"), sem("small_in")
        raw_done, aexp_ready, neg_ready, exp_ready, u_ready, ln_ready = (sem(n) for n in (
            "raw_done", "aexp_ready", "neg_ready", "exp_ready", "u_ready", "ln_ready"))
        beta_exp, raw_kept, g_ready, sums_done, sums_kept = (sem(n) for n in (
            "beta_exp", "raw_kept", "g_ready", "sums_done", "sums_kept"))
        own_dve = sem("own_dve2")
        flat = lambda t: t[:, :, :].rearrange("p t n -> p (t n)")
        with nc.Block() as block:
            @block.sync
            def _(sp):
                wv = w_in[0].rearrange("(k p) n -> p k n", p=P)
                sp.dma_start(ws[:, :, 0:4 * GH], wv[:, :, O_BETA:O_BETA + 4 * GH]).then_inc(ws_in, 16)
                sp.dma_start(ws[:, :, 4 * GH:NS], wv[:, :, O_DT:O_DT + 2 * SH]).then_inc(ws_in, 16)
                for dst, g, s in ((bias, gdn_dt_bias, ssd_dt_bias), (alog, gdn_a_log, ssd_a_log)):
                    sp.dma_start(dst[:, 0:2 * GH], g[0].rearrange("a h -> (a h)").partition_broadcast(P)).then_inc(small_in, 16)
                    sp.dma_start(dst[:, 2 * GH:NST], s[0].rearrange("a h -> (a h)").partition_broadcast(P)).then_inc(small_in, 16)

            @block.tensor
            def _(pe):
                pe.wait_ge(ws_in, 32)
                for t in range(NT):
                    for k in range(KD):
                        last = pe.matmul(bank[t][:, 0:NS], hT[:, k, t * P:(t + 1) * P], ws[:, k, :], start=(k == 0), stop=(k == KD - 1))
                    last.then_inc(raw_done, 1)
                pe.wait_ge(raw_kept, 1)
                pe.wait_ge(g_ready, 1)
                for n, mask in enumerate((C_LE, C_GE, C_GT, C_LT, C_ONE)):
                    pe.matmul(bank[n][:, 0:NT * NST], C(mask), ST[:, 0, :, :].rearrange("p t n -> p (t n)"),
                              start=True, stop=True).then_inc(sums_done, 1)

            @block.scalar
            def _(act):
                act.wait_ge(small_in, 64)
                act.activation(aexp[:, :], alog[:, :], ACT.Exp).then_inc(aexp_ready, 1)
                act.wait_ge(raw_kept, 1)
                act.activation(eb[:, :, :], raw[:, :, 0:2 * GH], ACT.Exp, scale=-1.0).then_inc(beta_exp, 1)
                act.wait_ge(neg_ready, 1)
                act.activation(flat(e), flat(m), ACT.Exp).then_inc(exp_ready, 1)
                act.wait_ge(u_ready, 1)
                act.activation(flat(lu), flat(u), ACT.Ln).then_inc(ln_ready, 1)
                for n in range(5):
                    act.wait_ge(sums_done, n + 1)
                    sums = bank[n][:, 0:NT * NST].rearrange("p (t n) -> p t n", n=NST)
                    if n == 4:
                        act.activation(ST[:, 3, :, :], sums, ACT.Exp)
                        continue
                    kind, dr = 1 + n // 2, n % 2
                    for at, w in ((dr * GH, GH), (2 * GH + dr * SH, SH)):
                        act.activation(ST[:, kind, :, at:at + w], sums[:, :, at:at + w], ACT.Exp)

            @block.vector
            def _(dve):
                st = Steps(dve, own_dve)
                TT, TS = dve.tensor_tensor, dve.tensor_scalar
                for t in range(NT):
                    dve.wait_ge(raw_done, t + 1)
                    last = dve.tensor_copy(raw[:, t, :], bank[t][:, 0:NS])
                last.then_inc(raw_kept, 1)
                dve.wait_ge(raw_kept, 1)
                dve.wait_ge(small_in, 64)
                st.link(TT(out=z[:, :, :], in0=raw[:, :, 2 * GH:NS], in1=bias[:, :].unsqueeze(1).broadcast_to([P, NT, NST]), op=ALU.add))
                st.link(TS(out=flat(m), in0=flat(z), scalar1=-1.0, scalar2=None, op0=ALU.mult))
                TT(out=flat(m), in0=flat(m), in1=flat(z), op=ALU.min).then_inc(neg_ready, 1)
                dve.wait_ge(beta_exp, 1)
                st.link(TS(out=eb[:, :, :], in0=eb[:, :, :], scalar1=1.0, scalar2=None, op0=ALU.add))
                dve.reciprocal(ST[:, 4, :, 0:2 * GH], eb[:, :, :])
                dve.wait_ge(exp_ready, 1)
                TS(out=flat(u), in0=flat(e), scalar1=1.0, scalar2=None, op0=ALU.add).then_inc(u_ready, 1)
                dve.wait_ge(u_ready, 1)
                st.link(TS(out=flat(d), in0=flat(u), scalar1=-1.0, scalar2=None, op0=ALU.add))
                st.link(TS(out=flat(isz), in0=flat(d), scalar1=0.0, scalar2=None, op0=ALU.is_equal))
                st.link(TT(out=flat(d), in0=flat(d), in1=flat(isz), op=ALU.add))
                st.link(dve.reciprocal(flat(d), flat(d)))
                st.link(TT(out=flat(d), in0=flat(d), in1=flat(e), op=ALU.mult))
                dve.wait_ge(ln_ready, 1)
                st.link(TT(out=flat(d), in0=flat(d), in1=flat(lu), op=ALU.mult))
                st.link(TT(out=flat(isz), in0=flat(isz), in1=flat(e), op=ALU.mult))
                st.link(TT(out=flat(d), in0=flat(d), in1=flat(isz), op=ALU.add))
                st.link(dve.scalar_tensor_tensor(out=flat(z), in0=flat(z), scalar=0.0, in1=flat(d), op0=ALU.max, op1=ALU.add))
                dve.tensor_copy(ST[:, 4, :, 2 * GH:NST], z[:, :, 2 * GH:NST])
                dve.wait_ge(aexp_ready, 1)
                dve.scalar_tensor_tensor(out=ST[:, 0, :, :], in0=z[:, :, :], scalar=-1.0,
                                         in1=aexp[:, :].unsqueeze(1).broadcast_to([P, NT, NST]),
                                         op0=ALU.mult, op1=ALU.mult).then_inc(g_ready, 1)


def deltanet(nc, sb, sem, bank, cst, C, hT, ST, cwT, vecT, half, shared, oT, levels, w_in, state_gdn, new_gdn):
    own = ExitStack()
    with own:
        S = lambda name, shape, dt=F32: sb(name, shape, dt, own)
        NU = 2 * NT
        FW, BW = 0, 1
        negm = S("negm", [P, LEVELS, 2, P])
        w4 = shared[:, 0:4 * KD * P].rearrange("p (c k n) -> p c k n", c=4, k=KD)
        cw = S("cw", [P, TAPS, 3])
        cb = S("cb", [P, 3])
        cur = S("cur", [P, 5, NT, 2])
        padded = S("padded", [P, 3, PADW])
        conv = S("conv", [P, 3, CW])
        th = S("th", [P, 3, CW])
        zth = S("zth", [P, T])
        zg = S("zg", [P, T])
        vT = S("vT", [P, NT, P])
        kraw = S("kraw", [P, NT, P])
        kq = shared[:, 4 * KD * P:4 * KD * P + 2 * T].rearrange("p (t a n) -> p t a n", t=NT, a=2)
        sq = S("sq", [P, 2, NT, P])
        ssum = S("ssum", [P, 2, NT])
        rn = S("rn", [P, 2, NT])
        kn = shared[:, 4 * KD * P + 2 * T:4 * KD * P + 3 * T].rearrange("p (t n) -> p t n", t=NT)
        vt = S("vt", [P, NT, P])
        gm = S("gm", [P, 2, NT, P])
        bm = S("bm", [P, 2, NT, P])
        dec = S("dec", [P, 2, NT, P])
        di = S("di", [P, 2, NT, P])
        att = S("att", [P, 2, NT, P])
        MT = S("MT", [P, NU, P])
        D_ = S("D_", [P, NU, P])
        DT = S("DT", [P, NU, P])
        convf = conv[:, :, :].rearrange("p c n -> p (c n)")
        thf = th[:, :, :].rearrange("p c n -> p (c n)")
        X = convf[:, 0:NU * P].rearrange("p (u n) -> p u n", n=P)
        state = S("state", [P, 2, 2, P])
        neg = S("neg", [P, NT, 2])
        ber = S("ber", [P, NT, 2])
        pair = lambda ap: ap.rearrange("p (d n) -> p d n", d=2)
        R = pair(convf[:, NU * P:(NU + 2) * P])
        vn = pair(convf[:, (NU + 2) * P:(NU + 4) * P])
        vd = pair(zth[:, 0:2 * P])
        qs = pair(zth[:, 2 * P:4 * P])
        osum, osq, on = (thf[:, n * T:(n + 1) * T].rearrange("p (t n) -> p t n", n=P) for n in range(3))
        oss = S("oss", [P, NT])
        osc = S("osc", [P, NT])
        unit = lambda d, t: 4 * d + t if t < 4 else 8 + d
        GROUPS = [(0, 4), (4, 4), (8, 2)]
        XB = (0, 3, 6)
        DTB = (1, 4, 7)
        DB = (2, 5, 7)
        dtv = lambda g, n: bank[DTB[g]][:, 0:n * P]
        dv = lambda g, n: bank[DB[g]][:, 256 * (g == 2):256 * (g == 2) + n * P]
        CHAIN = [(0, 0)] + [(1 + s, 4 - s) for s in range(4)]

        names = ("gl_in", "gw_in", "gs_in", "gs_out", "g_proj", "g_raw", "g_conv", "g_tanh", "g_ztanh", "g_silu", "g_sq", "g_sums",
                 "g_kturn", "g_vturn", "g_ssum", "g_rn", "g_kn", "g_v", "g_knturn", "g_knT", "g_cur", "g_gm", "g_seg",
                 "g_dec", "g_KQ", "g_M", "g_D2", "g_init", "g_Dkept", "g_X", "g_Xkept", "g_DT", "g_DTkept", "g_KS", "g_QS",
                 "g_R", "g_qs", "g_vnew", "g_vn", "g_vd", "g_O", "g_SU", "g_state", "g_osum", "g_oz", "g_oss", "g_osc",
                 "g_on", "g_oturn", "g_head", "g_dve", "g_zg", "g_pad", "g_pool", "g_qsadd", "g_di", "g_own_act")
        s = {n: sem(n) for n in names}
        DVE_STEPS, POOL_STEPS = 40, 8

        with nc.Block() as block:
            @block.sync
            def _(sp):
                sp.dma_start(negm[:, :, :, :], levels.rearrange("p (l a) n -> p l a n", a=2)).then_inc(s["gl_in"], 16)
                with sp.Fori(0, GH) as h:
                    sp.wait_ge(s["g_head"], h + 1)
                    for n, at in enumerate((O_QKV, O_QKV + D, O_QKV + 2 * D, O_ZG)):
                        src = w_in[0, :, bass.ds(h * P + at, P)].rearrange("(k p) n -> p k n", p=P)
                        sp.dma_start(w4[:, n, :, :], src).then_inc(s["gw_in"], 16)
                    for d in range(2):
                        sp.dma_start(state[:, 1, d, :], state_gdn[0, 0, d, bass.ds(h, 1), :, :].rearrange("a k v -> k (a v)")).then_inc(s["gs_in"], 16)
                    sp.wait_ge(s["g_state"], 10 * h + 2)
                    for d in range(2):
                        sp.dma_start(new_gdn[0, 0, d, bass.ds(h, 1), :, :].rearrange("a k v -> k (a v)"), state[:, 0, d, :]).then_inc(s["gs_out"], 16)
                sp.wait_ge(s["gs_out"], 32 * GH)

            @block.tensor
            def _(pe):
                pe.wait_ge(s["gl_in"], 16)
                with pe.Fori(0, GH) as h:
                    pe.wait_ge(s["g_head"], h + 1)
                    for n in range(4):
                        if n == 0:
                            pe.wait_ge(s["gw_in"], 64 * h + 64)
                        for k in range(KD):
                            pe.matmul(bank[2 * n][:, :], w4[:, n, k, :], hT[:, k, SEQ:T], start=(k == 0), stop=(k == KD - 1))
                        for k in range(KD):
                            last = pe.matmul(bank[2 * n + 1][:, 0:SEQ], w4[:, n, k, :], hT[:, k, 0:SEQ], start=(k == 0), stop=(k == KD - 1))
                        last.then_inc(s["g_proj"], 1)
                    pe.wait_ge(s["g_silu"], 3 * h + 2)
                    for t in range(NT):
                        last = pe.transpose(bank[1 + t // 4][:, t % 4 * P:t % 4 * P + P], kraw[:, t, :], C(C_ID))
                    last.then_inc(s["g_kturn"], 1)
                    pe.wait_ge(s["g_sq"], 2 * h + 2)
                    for n in range(2):
                        for t in range(NT):
                            last = pe.matmul(bank[0][:, n * NT + t:n * NT + t + 1], sq[:, n, t, :], cst[:, C_ONE, 0:1], start=True, stop=True)
                    last.then_inc(s["g_sums"], 1)
                    pe.wait_ge(s["g_silu"], 3 * h + 3)
                    for t in range(NT):
                        last = pe.transpose(bank[3 + t // 4][:, t % 4 * P:t % 4 * P + P], vT[:, t, :], C(C_ID))
                    last.then_inc(s["g_vturn"], 1)
                    pe.wait_ge(s["g_zg"], h + 1)
                    pe.wait_ge(s["g_gm"], 2 * h + 1)
                    pe.matmul(bank[6][:, :], C(C_GT), gm[:, FW, 0:4, :].rearrange("p t n -> p (t n)"), start=True, stop=True)
                    pe.matmul(bank[7][:, 0:P], C(C_GT), gm[:, FW, 4, :], start=True, stop=True).then_inc(s["g_seg"], 1)
                    pe.wait_ge(s["g_kn"], h + 1)
                    for t in range(NT):
                        last = pe.transpose(bank[5 if t < 4 else 0][:, t % 4 * P:t % 4 * P + P], kn[:, t, :], C(C_ID))
                    last.then_inc(s["g_knturn"], 1)
                    pe.wait_ge(s["g_knT"], h + 1)
                    pe.wait_ge(s["g_v"], h + 1)
                    for t in range(NT):
                        last = pe.matmul(bank[1 + t // 2][:, t % 2 * 256:t % 2 * 256 + 256], kq[:, t, 0, :],
                                         kq[:, t, :, :].rearrange("p a n -> p (a n)"), start=True, stop=True)
                    last.then_inc(s["g_KQ"], 1)
                    pe.wait_ge(s["g_gm"], 2 * h + 2)
                    pe.matmul(bank[4][:, :], C(C_LT), gm[:, BW, 0:4, :].rearrange("p t n -> p (t n)"), start=True, stop=True)
                    pe.matmul(bank[5][:, 0:P], C(C_LT), gm[:, BW, 4, :], start=True, stop=True).then_inc(s["g_seg"], 1)
                    pe.wait_ge(s["g_dec"], 2 * h + 2)
                    for g, (u0, n) in enumerate(GROUPS):
                        pe.wait_ge(s["g_D2"], 3 * h + g + 1)
                        pe.matmul(dtv(g, n), C(C_ID), DT[:, u0:u0 + n, :].rearrange("p u n -> p (u n)"), start=True, stop=False, skip_group_check=True)
                        for u in range(n):
                            last = pe.matmul(dv(g, n)[:, u * P:(u + 1) * P], DT[:, u0 + u, :], C(C_ID), start=(u == 0 and g < 2), stop=False, skip_group_check=True)
                        last.then_inc(s["g_init"], 1)
                    for l in range(LEVELS):
                        for g, (u0, n) in enumerate(GROUPS):
                            pe.wait_ge(s["g_Dkept"], 3 * 6 * h + 3 * l + g + 1)
                            for u in range(n):
                                last = pe.matmul(bank[XB[g]][:, u * P:(u + 1) * P], MT[:, u0 + u, :], D_[:, u0 + u, :], start=True, stop=True)
                            last.then_inc(s["g_X"], 1)
                        for g, (u0, n) in enumerate(GROUPS):
                            pe.wait_ge(s["g_Xkept"], 3 * 6 * h + 3 * l + g + 1)
                            for u in range(n):
                                last = pe.matmul(dtv(g, n)[:, u * P:(u + 1) * P], X[:, u0 + u, :], DT[:, u0 + u, :], start=False, stop=(l == LEVELS - 1), skip_group_check=True)
                            if l < LEVELS - 1:
                                for u in range(n):
                                    last = pe.matmul(dv(g, n)[:, u * P:(u + 1) * P], DT[:, u0 + u, :], X[:, u0 + u, :], start=False, stop=(l == LEVELS - 2), skip_group_check=True)
                            last.then_inc(s["g_DT"], 1)
                    pe.wait_ge(s["gs_in"], 32 * h + 32)
                    for p, tiles in enumerate(CHAIN):
                        q = int(p > 0)
                        if p > 0:
                            if p == 1:
                                pe.wait_ge(s["g_Dkept"], 18 * h + 18)
                            pe.wait_ge(s["g_state"], 10 * h + 2 * p)
                            for d, t in enumerate(tiles):
                                last = pe.matmul(bank[0][:, d * P:(d + 1) * P], kq[:, t, 0, :], state[:, q, d, :], start=True, stop=True)
                            last.then_inc(s["g_KS"], 1)
                            if p > 1:
                                pe.wait_ge(s["g_qs"], 4 * h + p - 1)
                            for d, t in enumerate(tiles):
                                last = pe.matmul(bank[1][:, d * P:(d + 1) * P], kq[:, t, 1, :], state[:, q, d, :], start=True, stop=True)
                            last.then_inc(s["g_QS"], 1)
                        else:
                            pe.wait_ge(s["g_DTkept"], 18 * h + 18)
                        pe.wait_ge(s["g_R"], 5 * h + p + 1)
                        for d, t in enumerate(tiles):
                            last = pe.matmul(bank[2][:, d * P:(d + 1) * P], DT[:, unit(d, t), :], R[:, d, :], start=True, stop=True)
                        last.then_inc(s["g_vnew"], 1)
                        pe.wait_ge(s["g_vd"], 5 * h + p + 1)
                        for d, t in enumerate(tiles):
                            last = pe.matmul(bank[4][:, d * P:(d + 1) * P], kn[:, t, :], vd[:, d, :], start=True, stop=True)
                        last.then_inc(s["g_SU"], 1)
                        pe.wait_ge(s["g_vn"], 5 * h + p + 1)
                        if p > 0:
                            pe.wait_ge(s["g_osum"], 5 * h + p)
                        for d, t in enumerate(tiles):
                            last = pe.matmul(bank[3][:, d * P:(d + 1) * P], att[:, d, t, :], vn[:, d, :], start=True, stop=True)
                        last.then_inc(s["g_O"], 1)
                    pe.wait_ge(s["g_on"], h + 1)
                    for t in range(NT):
                        last = pe.transpose(bank[5 + t // 4][:, t % 4 * P:t % 4 * P + P], on[:, t, :], C(C_ID))
                    last.then_inc(s["g_oturn"], 1)

            @block.scalar
            def _(act):
                with act.Fori(0, GH) as h:
                    for n in range(3):
                        act.wait_ge(s["g_proj"], 4 * h + n + 1)
                        if n == 0:
                            act.wait_ge(s["g_pad"], 1)
                        act.copy(padded[:, n, 2:2 + SEQ], bank[2 * n + 1][:, 0:SEQ])
                        act.copy(padded[:, n, 6 + SEQ:6 + T], bank[2 * n][:, :]).then_inc(s["g_raw"], 1)
                        if n > 0:
                            act.wait_ge(s["g_conv"], 3 * h + n)
                            act.activation(th[:, n - 1, :], conv[:, n - 1, :], ACT.Tanh, scale=0.5).then_inc(s["g_tanh"], 1)
                    act.wait_ge(s["g_proj"], 4 * h + 4)
                    act.activation(zth[:, 0:SEQ], bank[7][:, 0:SEQ], ACT.Tanh, scale=0.5)
                    act.activation(zth[:, SEQ:T], bank[6][:, :], ACT.Tanh, scale=0.5).then_inc(s["g_ztanh"], 1)
                    act.wait_ge(s["g_conv"], 3 * h + 3)
                    act.activation(th[:, 2, :], conv[:, 2, :], ACT.Tanh, scale=0.5).then_inc(s["g_tanh"], 1)
                    for n in range(2):
                        act.wait_ge(s["g_silu"], 3 * h + n + 1)
                        act.activation(sq[:, n, :, :], kq[:, :, 1, :] if n == 0 else kraw[:, :, :], ACT.Square, scale=0.5).then_inc(s["g_sq"], 1)
                    act.wait_ge(s["g_vturn"], h + 1)
                    act.mul(vt[:, 0:4, :], bank[3][:, :].rearrange("p (t n) -> p t n", n=P), 0.5)
                    act.mul(vt[:, 4, :], bank[4][:, 0:P], 0.5).then_inc(s["g_v"], 1)
                    act.wait_ge(s["g_seg"], 2 * h + 1)
                    act.activation(dec[:, FW, 0:4, :], bank[6][:, :].rearrange("p (t n) -> p t n", n=P), ACT.Exp)
                    act.activation(dec[:, FW, 4, :], bank[7][:, 0:P], ACT.Exp).then_inc(s["g_dec"], 1)
                    act.wait_ge(s["g_knturn"], h + 1)
                    act.copy(kq[:, 0:4, 0, :], bank[5][:, :].rearrange("p (t n) -> p t n", n=P))
                    act.copy(kq[:, 4, 0, :], bank[0][:, 0:P]).then_inc(s["g_knT"], 1)
                    act.wait_ge(s["g_seg"], 2 * h + 2)
                    act.activation(dec[:, BW, 0:4, :], bank[4][:, :].rearrange("p (t n) -> p t n", n=P), ACT.Exp)
                    act.activation(dec[:, BW, 4, :], bank[5][:, 0:P], ACT.Exp).then_inc(s["g_dec"], 1)
                    for g, (u0, n) in enumerate(GROUPS):
                        act.wait_ge(s["g_init"], 3 * h + g + 1)
                        act.copy(D_[:, u0:u0 + n, :], dv(g, n).rearrange("p (u n) -> p u n", n=P)).then_inc(s["g_Dkept"], 1)
                    for l in range(LEVELS):
                        for g, (u0, n) in enumerate(GROUPS):
                            act.wait_ge(s["g_DT"], 18 * h + 3 * l + g + 1)
                            act.copy(DT[:, u0:u0 + n, :], dtv(g, n).rearrange("p (u n) -> p u n", n=P)).then_inc(s["g_DTkept"], 1)
                            if l < LEVELS - 1:
                                act.copy(D_[:, u0:u0 + n, :], dv(g, n).rearrange("p (u n) -> p u n", n=P)).then_inc(s["g_Dkept"], 1)
                    for p, tiles in enumerate(CHAIN):
                        if p > 0:
                            act.wait_ge(s["g_QS"], 4 * h + p)
                            if p > 1:
                                act.wait_ge(s["g_qsadd"], 4 * h + p - 1)
                            for d, t in enumerate(tiles):
                                last = act.activation(qs[:, d, :], bank[1][:, d * P:(d + 1) * P], ACT.Copy, scale=cur[:, 1, t, d:d + 1])
                            last.then_inc(s["g_qs"], 1)
                        act.wait_ge(s["g_vd"], 5 * h + p + 1)
                        if p > 0:
                            act.wait_ge(s["g_O"], 5 * h + p)
                        for d, t in enumerate(tiles):
                            last = act.activation(vn[:, d, :], bank[2][:, d * P:(d + 1) * P], ACT.Copy, scale=cur[:, 4, t, d:d + 1])
                        last.then_inc(s["g_vn"], 1)
                    act.wait_ge(s["g_osum"], 5 * h + 5)
                    for t in range(NT):
                        last = act.activation(osq[:, t, :], osum[:, t, :], ACT.Square, accum_out=oss[:, t:t + 1])
                    last.then_inc(s["g_oss"], 1)

            @block.gpsimd
            def _(pool):
                pool.memset(padded[:, :, :], 0.0).then_inc(s["g_pad"], 1)
                with pool.Fori(0, GH) as h:
                    st = Steps(pool, s["g_pool"], h * POOL_STEPS, held=True)
                    TT = pool.tensor_tensor
                    pool.wait_ge(s["g_cur"], h + 1)
                    for d, mask in ((FW, C_LE), (BW, C_GE)):
                        TT(out=gm[:, d, :, :], in0=C(mask).unsqueeze(1).broadcast_to([P, NT, P]),
                           in1=cur[:, 0, :, d:d + 1].broadcast_to([P, NT, P]), op=ALU.mult).then_inc(s["g_gm"], 1)
                    for d, mask in ((FW, C_LT), (BW, C_GT)):
                        st.add(TT(out=bm[:, d, :, :], in0=C(mask).unsqueeze(1).broadcast_to([P, NT, P]),
                                  in1=cur[:, 4, :, d:d + 1].broadcast_to([P, NT, P]), op=ALU.mult))
                    st.add(TT(out=ber[:, :, :], in0=cur[:, 4, :, :], in1=cur[:, 2, :, :], op=ALU.mult))
                    pool.wait_ge(s["g_ssum"], h + 1)
                    TT(out=rn[:, :, :].rearrange("p a t -> p (a t)"), in0=ssum[:, :, :].rearrange("p a t -> p (a t)"),
                       in1=half[:, 0:2 * NT], op=ALU.pow).then_inc(s["g_rn"], 1)
                    for p in range(1, 5):
                        pool.wait_ge(s["g_qs"], 4 * h + p)
                        hold(pool, s["g_osum"], 5 * h + p)
                        for d, t in enumerate(CHAIN[p]):
                            if p <= 2:
                                last = pool.tensor_copy(osum[:, t, :], qs[:, d, :])
                            else:
                                last = TT(out=osum[:, t, :], in0=osum[:, t, :], in1=qs[:, d, :], op=ALU.add)
                        last.then_inc(s["g_qsadd"], 1)
                    hold(pool, s["g_oss"], h + 1)
                    st.link(pool.tensor_scalar(out=rn[:, 0, :], in0=rn[:, 0, :], scalar1=0.5 * P ** -0.5, scalar2=None, op0=ALU.mult))
                    st.link(TT(out=osc[:, :], in0=rn[:, 0, :], in1=rn[:, 0, :], op=ALU.mult))
                    st.link(TT(out=osc[:, :], in0=osc[:, :], in1=oss[:, :], op=ALU.mult))
                    st.link(pool.tensor_scalar(out=osc[:, :], in0=osc[:, :], scalar1=1.0 / P, scalar2=EPS, op0=ALU.mult, op1=ALU.add))
                    st.link(TT(out=osc[:, :], in0=osc[:, :], in1=half[:, 0:NT], op=ALU.pow))
                    TT(out=osc[:, :], in0=osc[:, :], in1=rn[:, 0, :], op=ALU.mult).then_inc(s["g_osc"], 1)
                    assert st.n == POOL_STEPS, st.n

            @block.vector
            def _(dve):
                dve.drain().then_inc(s["g_head"], 1)
                TT, TS, STT = dve.tensor_tensor, dve.tensor_scalar, dve.scalar_tensor_tensor
                dve.wait_ge(s["gl_in"], 16)
                with dve.Fori(0, GH) as h:
                    st = Steps(dve, s["g_dve"], h * DVE_STEPS)
                    for d in range(2):
                        st.add(dve.tensor_copy(cur[:, :, :, d:d + 1], ST[:, :, :, bass.ds(h + d * GH, 1)]))
                    for n in range(3):
                        st.add(dve.tensor_copy(cw[:, :, n:n + 1], cwT[:, 0, :, bass.ds(h + n * GH, 1)]))
                    for n in range(3):
                        st.add(dve.tensor_copy(cb[:, n:n + 1], vecT[:, bass.ds(h + n * GH, 1)]))
                    st.wait()
                    TS(out=neg[:, :, :], in0=cur[:, 1, :, :], scalar1=-1.0, scalar2=None, op0=ALU.mult).then_inc(s["g_cur"], 1)

                    def silu(n):
                        dve.wait_ge(s["g_tanh"], 3 * h + n + 1)
                        to = (kq[:, :, 1, :], kraw[:, :, :], vT[:, :, :])[n]
                        STT(out=to[:, 0, :], in0=th[:, n, 0:SEQ], scalar=1.0, in1=conv[:, n, 0:SEQ], op0=ALU.add, op1=ALU.mult)
                        STT(out=to[:, 1:NT, :], in0=th[:, n, LAT:CW].rearrange("p (t n) -> p t n", n=P), scalar=1.0,
                            in1=conv[:, n, LAT:CW].rearrange("p (t n) -> p t n", n=P),
                            op0=ALU.add, op1=ALU.mult).then_inc(s["g_silu"], 1)

                    for n in range(3):
                        dve.wait_ge(s["g_raw"], 3 * h + n + 1)
                        st.link(TS(out=conv[:, n, :], in0=padded[:, n, 0:CW], scalar1=cw[:, 0, n:n + 1], scalar2=cb[:, n:n + 1], op0=ALU.mult, op1=ALU.add))
                        for k in range(1, TAPS):
                            ins = STT(out=conv[:, n, :], in0=padded[:, n, k:k + CW], scalar=cw[:, k, n:n + 1], in1=conv[:, n, :], op0=ALU.mult, op1=ALU.add)
                            if k < TAPS - 1:
                                st.link(ins)
                            else:
                                ins.then_inc(s["g_conv"], 1)
                        if n > 0:
                            silu(n - 1)
                    dve.wait_ge(s["g_ztanh"], h + 1)
                    STT(out=zg[:, 0:SEQ], in0=zth[:, 0:SEQ], scalar=1.0, in1=bank[7][:, 0:SEQ], op0=ALU.add, op1=ALU.mult)
                    STT(out=zg[:, SEQ:T], in0=zth[:, SEQ:T], scalar=1.0, in1=bank[6][:, :], op0=ALU.add, op1=ALU.mult).then_inc(s["g_zg"], 1)
                    silu(2)
                    dve.wait_ge(s["g_sums"], h + 1)
                    TS(out=ssum[:, :, :], in0=bank[0][:, 0:2 * NT].rearrange("p (a t) -> p a t", a=2), scalar1=EPS, scalar2=None, op0=ALU.add).then_inc(s["g_ssum"], 1)
                    dve.wait_ge(s["g_rn"], h + 1)
                    dve.wait_ge(s["g_kturn"], h + 1)
                    for t in range(NT):
                        last = TS(out=kn[:, t, :], in0=bank[1 + t // 4][:, t % 4 * P:t % 4 * P + P], scalar1=rn[:, 1, t:t + 1], scalar2=0.5, op0=ALU.mult, op1=ALU.mult)
                    last.then_inc(s["g_kn"], 1)
                    for d in range(2):
                        dve.wait_ge(s["g_dec"], 2 * h + d + 1)
                        st.add(TT(out=di[:, d, :, :], in0=dec[:, d, :, :], in1=C((C_LE, C_GE)[d]).unsqueeze(1).broadcast_to([P, NT, P]), op=ALU.mult))
                        if d == 0:
                            dve.wait_ge(s["g_pool"], POOL_STEPS * h + 3)
                        st.link(TT(out=dec[:, d, :, :], in0=dec[:, d, :, :], in1=bm[:, d, :, :], op=ALU.mult))
                        if d == 0:
                            dve.wait_ge(s["g_KQ"], h + 1)
                        for b, (t0, n) in enumerate(((0, 2), (2, 2), (4, 1))):
                            v = bank[1 + b][:, 0:n * 256].rearrange("p (t a n) -> p t a n", a=2, n=P)
                            u0 = unit(d, t0)
                            st.add(TT(out=MT[:, u0:u0 + n, :], in0=v[:, :, 0, :], in1=dec[:, d, t0:t0 + n, :], op=ALU.mult))
                            st.add(TT(out=att[:, d, t0:t0 + n, :], in0=v[:, :, 1, :], in1=di[:, d, t0:t0 + n, :], op=ALU.mult))
                    st.wait()
                    for g, (u0, n) in enumerate(GROUPS):
                        m = cst[:, C_N1F + g:C_N1F + g + 1, :].broadcast_to([P, n, P]) if g < 2 else cst[:, C_N1F:C_N1F + 2, :]
                        st.add(TT(out=DT[:, u0:u0 + n, :], in0=MT[:, u0:u0 + n, :], in1=m, op=ALU.mult))
                    for g, (u0, n) in enumerate(GROUPS):
                        st.wait(2 - g if g == 0 else 2 - g)
                        TT(out=DT[:, u0:u0 + n, :], in0=DT[:, u0:u0 + n, :], in1=cst[:, C_ID:C_ID + 1, :].broadcast_to([P, n, P]), op=ALU.add).then_inc(s["g_D2"], 1)
                    for l in range(LEVELS):
                        for g, (u0, n) in enumerate(GROUPS):
                            dve.wait_ge(s["g_X"], 18 * h + 3 * l + g + 1)
                            m = negm[:, l, g:g + 1, :].broadcast_to([P, n, P]) if g < 2 else negm[:, l, :, :]
                            TT(out=X[:, u0:u0 + n, :], in0=bank[XB[g]][:, 0:n * P].rearrange("p (u n) -> p u n", n=P), in1=m, op=ALU.mult).then_inc(s["g_Xkept"], 1)
                    dve.wait_ge(s["gs_in"], 32 * h + 32)
                    for p, tiles in enumerate(CHAIN):
                        q = int(p > 0)
                        if p > 0:
                            dve.wait_ge(s["g_KS"], 4 * h + p)
                        for d, t in enumerate(tiles):
                            if p == 0:
                                last = dve.tensor_copy(R[:, d, :], vt[:, t, :])
                            else:
                                last = STT(out=R[:, d, :], in0=bank[0][:, d * P:(d + 1) * P], scalar=neg[:, t, d:d + 1], in1=vt[:, t, :], op0=ALU.mult, op1=ALU.add)
                        last.then_inc(s["g_R"], 1)
                        dve.wait_ge(s["g_vnew"], 5 * h + p + 1)
                        for d, t in enumerate(tiles):
                            last = TS(out=vd[:, d, :], in0=bank[2][:, d * P:(d + 1) * P], scalar1=ber[:, t, d:d + 1], scalar2=None, op0=ALU.mult)
                        last.then_inc(s["g_vd"], 1)
                        dve.wait_ge(s["g_SU"], 5 * h + p + 1)
                        for d, t in enumerate(tiles):
                            if p == 0:
                                dve.tensor_copy(state[:, q, d, :], bank[4][:, d * P:(d + 1) * P]).then_inc(s["g_state"], 1)
                            else:
                                STT(out=state[:, q, d, :], in0=state[:, q, d, :], scalar=cur[:, 3, t, d:d + 1], in1=bank[4][:, d * P:(d + 1) * P], op0=ALU.mult, op1=ALU.add).then_inc(s["g_state"], 1)
                        dve.wait_ge(s["g_O"], 5 * h + p + 1)
                        if p > 0:
                            dve.wait_ge(s["g_qsadd"], 4 * h + p)
                        if p == 0:
                            st.link(dve.tensor_copy(osum[:, 0, :], bank[3][:, 0:P]))
                            TT(out=osum[:, 0, :], in0=osum[:, 0, :], in1=bank[3][:, P:2 * P], op=ALU.add).then_inc(s["g_osum"], 1)
                        else:
                            for d, t in enumerate(tiles):
                                last = TT(out=osum[:, t, :], in0=osum[:, t, :], in1=bank[3][:, d * P:(d + 1) * P], op=ALU.add)
                            last.then_inc(s["g_osum"], 1)
                    dve.wait_ge(s["g_osc"], h + 1)
                    for t in range(NT):
                        last = TS(out=on[:, t, :], in0=osum[:, t, :], scalar1=osc[:, t:t + 1], scalar2=0.5, op0=ALU.mult, op1=ALU.mult)
                    last.then_inc(s["g_on"], 1)
                    dve.wait_ge(s["g_oturn"], h + 1)
                    STT(out=oT[:, bass.ds(h, 1), SEQ - P:4 * P], in0=bank[5][:, :].unsqueeze(1), scalar=vecT[:, 48:49], in1=zg[:, 0:4 * P].unsqueeze(1), op0=ALU.mult, op1=ALU.mult)
                    STT(out=oT[:, bass.ds(h, 1), 4 * P:T], in0=bank[6][:, 0:P].unsqueeze(1), scalar=vecT[:, 48:49], in1=zg[:, 4 * P:T].unsqueeze(1), op0=ALU.mult, op1=ALU.mult).then_inc(s["g_head"], 1)
                    assert st.n == DVE_STEPS, st.n


def ssd(nc, sb, sem, bank, cst, C, hT, ST, cwT, vecT, half, shared, yT, w_in, ssd_d, state_ssd, new_ssd):
    own = ExitStack()
    with own:
        S = lambda name, shape, dt=F32: sb(name, shape, dt, own)
        FW, BW = 0, 1
        GW = HG * SP_
        NQ = GW // P
        NJ = 2 + NQ
        w6 = shared[:, :].rearrange("p (c k n) -> p c k n", c=NJ, k=KD)
        wz = w6[:, 0:NQ, :, :].rearrange("p a b c -> p (a b c)").rearrange("p (k n) -> p k n", k=KD)
        dskip = S("dskip", [P, SH])
        cw = S("scw", [P, TAPS, NJ])
        cb = S("scb", [P, NJ])
        cur = S("scur", [P, 5, NT, 2, HG])
        dter = S("dter", [P, NT, 2, HG])
        dg = S("dg", [P, HG])
        padded = S("spadded", [P, 3, PADW])
        room = S("sroom", [P, 2, 3 * CW])
        flat_room = room[:, :, :].rearrange("p a n -> p (a n)")
        conv = room[:, 0, :].rearrange("p (c n) -> p c n", c=3)
        th = room[:, 1, :].rearrange("p (c n) -> p c n", c=3)
        xe = flat_room[:, 0:4 * GW].rearrange("p (a d n) -> p a d n", a=2, d=2)
        state = flat_room[:, 4 * GW:6 * GW].rearrange("p (d n) -> p d n", d=2)
        BT = S("BT", [P, NT, P])
        CT = S("CT", [P, NT, P])
        xT = S("xT", [P, 3, NT, P])
        dtx = xT[:, :, :, :].rearrange("p a t n -> p (a t n)")[:, 0:2 * GW].rearrange("p (d n) -> p d n", d=2)
        tmp = dtx
        Bt = S("Bt", [P, NT, P])
        xt = S("xt", [P, NT, GW])
        am = S("am", [P, 2, HG, P])
        dec = S("sdec", [P, 2, HG, P])
        M = S("M", [P, 2, HG, P])
        cbm = S("cbm", [P, 2, 2, P])
        srow = S("srow", [P, 2, NQ, P])
        ysum = S("ysum", [P, NT, GW])
        yss = S("yss", [P, NT])
        ysc = S("ysc", [P, NT])
        decf = dec[:, :, :, :].rearrange("p a h n -> p (a h n)")
        Mf = M[:, :, :, :].rearrange("p a h n -> p (a h n)")
        zs = lambda t: Mf[:, t * GW:(t + 1) * GW] if t < 4 else decf[:, 0:GW]
        zth = lambda t: decf[:, (1 + t % 2) * GW:(2 + t % 2) * GW]
        CHAIN = [(0, 0)] + [(1 + s, 4 - s) for s in range(4)]
        names = ("s_win", "s_wzin", "s_din", "s_stin", "s_stout", "s_proj", "s_raw", "s_conv", "s_tanh", "s_silu", "s_turn",
                 "s_turnkept", "s_cur", "s_am", "s_seg", "s_cb", "s_dec", "s_M", "s_dx", "s_y", "s_ykept", "s_xe", "s_st",
                 "s_state", "s_yoff", "s_yoffkept", "s_outturn", "s_outkept", "s_initturn", "s_init", "s_z", "s_zth", "s_zs",
                 "s_yz", "s_yss", "s_ysc", "s_yn", "s_yturn", "s_group", "s_pad", "s_dve", "s_pool")
        s = {n: sem(n) for n in names}
        DVE_STEPS, POOL_STEPS = 69, 3
        hv = lambda ap: ap.rearrange("p (h e) -> p h e", e=SP_)

        with nc.Block() as block:
            @block.sync
            def _(sp):
                sp.dma_start(dskip[:, :], ssd_d[0].partition_broadcast(P)).then_inc(s["s_din"], 16)
                with sp.Fori(0, SG) as g:
                    hold(sp, s["s_group"], g + 1)
                    for n in range(NJ):
                        at = g * P + (O_XBC + SH * SP_ + (0, SG * SN)[n]) if n < 2 else g * GW + (O_XBC + (n - 2) * P)
                        src = w_in[0, :, bass.ds(at, P)].rearrange("(k p) n -> p k n", p=P)
                        sp.dma_start(w6[:, n, :, :], src).then_inc(s["s_win"], 16)
                    for d in range(2):
                        src = state_ssd[0, 0, d, bass.ds(g * HG, HG), :, :].rearrange("h e n -> (h e) n").rearrange("(q p) n -> p q n", p=P)
                        sp.dma_start(srow[:, d, :, :], src).then_inc(s["s_stin"], 16)
                    sp.wait_ge(s["s_proj"], NJ * g + NJ)
                    src = w_in[0, :, bass.ds(g * GW + O_ZS, GW)].rearrange("(k p) n -> p k n", p=P)
                    sp.dma_start(wz, src).then_inc(s["s_wzin"], 16)
                    sp.wait_ge(s["s_outkept"], g + 1)
                    for d in range(2):
                        dst = new_ssd[0, 0, d, bass.ds(g * HG, HG), :, :].rearrange("h e n -> (h e) n").rearrange("(q p) n -> p q n", p=P)
                        sp.dma_start(dst, srow[:, d, :, :]).then_inc(s["s_stout"], 16)
                    hold(sp, s["s_stout"], 32 * g + 32)

            @block.tensor
            def _(pe):
                with pe.Fori(0, SG) as g:
                    pe.wait_ge(s["s_group"], g + 1)

                    def turn(n, m):
                        pe.wait_ge(s["s_silu"], NJ * g + n + 1)
                        if m > 0:
                            pe.wait_ge(s["s_turnkept"], 5 * g + m)
                        src = BT if n == 0 else xT[:, (n - 2) % 3, :, :]
                        for t in range(NT):
                            last = pe.transpose(bank[6 + t // 4][:, t % 4 * P:t % 4 * P + P], src[:, t, :], C(C_ID))
                        last.then_inc(s["s_turn"], 1)

                    for n in range(NJ):
                        pe.wait_ge(s["s_win"], 16 * NJ * g + 16 * NJ)
                        if n >= 3:
                            pe.wait_ge(s["s_raw"], NJ * g + n - 2)
                        b = 2 * (n % 3)
                        for k in range(KD):
                            pe.matmul(bank[b][:, :], w6[:, n, k, :], hT[:, k, SEQ:T], start=(k == 0), stop=(k == KD - 1))
                        for k in range(KD):
                            last = pe.matmul(bank[b + 1][:, 0:SEQ], w6[:, n, k, :], hT[:, k, 0:SEQ], start=(k == 0), stop=(k == KD - 1))
                        last.then_inc(s["s_proj"], 1)
                        if n == 2:
                            turn(0, 0)
                        if n > 2:
                            turn(n - 1, n - 2)

                    def cbs(t):
                        if t >= 2:
                            pe.wait_ge(s["s_M"], 10 * g + 2 * t - 3)
                        pe.matmul(bank[4 + t % 2][:, 0:P], BT[:, t, :], CT[:, t, :], start=True, stop=True).then_inc(s["s_cb"], 1)

                    def seg(u):
                        pe.wait_ge(s["s_am"], 10 * g + u + 1)
                        if u >= 2:
                            pe.wait_ge(s["s_dec"], 10 * g + u - 1)
                        for half_ in range(2):
                            last = pe.matmul(bank[2 * (u % 2) + half_][:, :], C((C_GT, C_LT)[u % 2]),
                                             am[:, u % 2, 4 * half_:4 * half_ + 4, :].rearrange("p h n -> p (h n)"), start=True, stop=True)
                        last.then_inc(s["s_seg"], 1)

                    pe.wait_ge(s["s_raw"], NJ * g + NJ)
                    cbs(0)
                    seg(0)
                    turn(5, 4)
                    for u in range(2 * NT):
                        t, d = u // 2, u % 2
                        if u + 1 < 2 * NT:
                            if (u + 1) % 2 == 0:
                                cbs((u + 1) // 2)
                            seg(u + 1)
                        if u == 0:
                            pe.wait_ge(s["s_turnkept"], 5 * g + 5)
                        if d == 0 and t >= 2:
                            pe.wait_ge(s["s_ykept"], 5 * g + t - 1)
                        pe.wait_ge(s["s_M"], 10 * g + u + 1)
                        for h in range(HG):
                            last = pe.matmul(bank[6 + t % 2][:, h * SP_:(h + 1) * SP_], M[:, u % 2, h, :], dtx[:, u % 2, h * SP_:(h + 1) * SP_],
                                             start=(d == 0 and h == 0), stop=(d == 1), skip_group_check=True)
                        last.then_inc(s["s_y"], 1)
                    pe.wait_ge(s["s_dec"], 10 * g + 10)

                    def states(p):
                        pe.wait_ge(s["s_xe"], 5 * g + p + 1)
                        for d, t in enumerate(CHAIN[p]):
                            last = pe.matmul(bank[2 + d][:, :], Bt[:, t, :], xe[:, p % 2, d, :], start=True, stop=True)
                        last.then_inc(s["s_st"], 1)

                    def zproj(t):
                        if t == 0:
                            pe.wait_ge(s["s_wzin"], 16 * g + 16)
                        if t == 4:
                            pe.wait_ge(s["s_zs"], 5 * g + 1)
                        for k in range(KD):
                            last = pe.matmul(bank[4 + t % 4][:, :], hT[:, k, t * P:(t + 1) * P], wz[:, k, :], start=(k == 0), stop=(k == KD - 1))
                        last.then_inc(s["s_z"], 1)

                    states(0)
                    pe.wait_ge(s["s_ykept"], 5 * g + 5)
                    pe.wait_ge(s["s_stin"], 32 * g + 32)
                    for d in range(2):
                        for q in range(NQ):
                            last = pe.transpose(bank[6 + d][:, q * P:(q + 1) * P], srow[:, d, q, :], C(C_ID))
                    last.then_inc(s["s_initturn"], 1)
                    pe.wait_ge(s["s_state"], 10 * g + 2)
                    for d in range(2):
                        for q in range(NQ):
                            last = pe.transpose(bank[4 + d][:, q * P:(q + 1) * P], state[:, d, q * P:(q + 1) * P], C(C_ID))
                    last.then_inc(s["s_outturn"], 1)
                    for p in range(1, 5):
                        if p == 1:
                            pe.wait_ge(s["s_init"], g + 1)
                        else:
                            pe.wait_ge(s["s_state"], 10 * g + 2 * p)
                            pe.wait_ge(s["s_yoffkept"], 4 * g + p - 1)
                        for d, t in enumerate(CHAIN[p]):
                            last = pe.matmul(bank[d][:, :], CT[:, t, :], state[:, d, :], start=True, stop=True)
                        last.then_inc(s["s_yoff"], 1)
                        states(p)
                        if p == 1:
                            pe.wait_ge(s["s_outkept"], g + 1)
                        zproj(p - 1)
                    zproj(4)
                    for t in range(NT):
                        pe.wait_ge(s["s_yn"], 5 * g + t + 1)
                        for q in range(NQ):
                            to = bank[q][:, t * P:(t + 1) * P] if t < 4 else bank[4][:, q * P:(q + 1) * P]
                            last = pe.transpose(to, ysum[:, t, q * P:(q + 1) * P], C(C_ID))
                    last.then_inc(s["s_yturn"], 1)

            @block.scalar
            def _(act):
                with act.Fori(0, SG) as g:
                    def keep_turn(m):
                        act.wait_ge(s["s_turn"], 5 * g + m + 1)
                        to = Bt[:, :, :] if m == 0 else xt[:, :, (m - 1) * P:m * P]
                        act.copy(to[:, 0:4, :], bank[6][:, :].rearrange("p (t n) -> p t n", n=P))
                        act.copy(to[:, 4, :], bank[7][:, 0:P]).then_inc(s["s_turnkept"], 1)

                    for n in range(NJ + 1):
                        if n < NJ:
                            act.wait_ge(s["s_proj"], NJ * g + n + 1)
                            if n == 0:
                                act.wait_ge(s["s_pad"], 1)
                            if n >= 3:
                                act.wait_ge(s["s_conv"], NJ * g + n - 2)
                            b = 2 * (n % 3)
                            act.copy(padded[:, n % 3, 2:2 + SEQ], bank[b + 1][:, 0:SEQ])
                            act.copy(padded[:, n % 3, 6 + SEQ:6 + T], bank[b][:, :]).then_inc(s["s_raw"], 1)
                        if n > 0:
                            act.wait_ge(s["s_conv"], NJ * g + n)
                            if n >= 4:
                                act.wait_ge(s["s_silu"], NJ * g + n - 3)
                            act.activation(th[:, (n - 1) % 3, :], conv[:, (n - 1) % 3, :], ACT.Tanh).then_inc(s["s_tanh"], 1)
                        if n >= 3:
                            keep_turn(n - 3)
                    for u in range(2 * NT):
                        if u == 1:
                            keep_turn(4)
                        act.wait_ge(s["s_seg"], 10 * g + u + 1)
                        if u >= 2:
                            act.wait_ge(s["s_M"], 10 * g + u - 1)
                        for half_ in range(2):
                            last = act.activation(dec[:, u % 2, 4 * half_:4 * half_ + 4, :], bank[2 * (u % 2) + half_][:, :].rearrange("p (h n) -> p h n", n=P), ACT.Exp)
                        last.then_inc(s["s_dec"], 1)
                    act.wait_ge(s["s_outturn"], g + 1)
                    for d in range(2):
                        last = act.copy(srow[:, d, :, :], bank[4 + d][:, :].rearrange("p (q n) -> p q n", n=P))
                    last.then_inc(s["s_outkept"], 1)
                    for d in range(2):
                        last = act.copy(state[:, d, :], bank[6 + d][:, :])
                    last.then_inc(s["s_init"], 1)
                    for t in range(NT):
                        act.wait_ge(s["s_z"], 5 * g + t + 1)
                        if t == 0:
                            act.wait_ge(s["s_M"], 10 * g + 10)
                        if t >= 2:
                            act.wait_ge(s["s_zs"], 5 * g + t - 1)
                        act.activation(zth(t), bank[4 + t % 4][:, :], ACT.Tanh, scale=0.5).then_inc(s["s_zth"], 1)
                    for t in range(NT):
                        act.wait_ge(s["s_yz"], 5 * g + t + 1)
                        act.activation(xt[:, t, :], ysum[:, t, :], ACT.Square, scale=0.5, accum_out=yss[:, t:t + 1]).then_inc(s["s_yss"], 1)
                    act.wait_ge(s["s_yturn"], g + 1)
                    for q in range(NQ):
                        w = vecT[:, bass.ds(g * NQ + (49 + q), 1)]
                        act.activation(yT[:, bass.ds(g * NQ + q, 1), 0:4 * P], bank[q][:, :].unsqueeze(1), ACT.Copy, scale=w)
                        last = act.activation(yT[:, bass.ds(g * NQ + q, 1), 4 * P:T], bank[4][:, q * P:(q + 1) * P].unsqueeze(1), ACT.Copy, scale=w)
                    last.then_inc(s["s_group"], 1)

            @block.gpsimd
            def _(pool):
                pool.memset(padded[:, :, :], 0.0).then_inc(s["s_pad"], 1)
                pool.wait_ge(s["s_din"], 16)
                with pool.Fori(0, SG) as g:
                    st = Steps(pool, s["s_pool"], g * POOL_STEPS, held=True)
                    TT = pool.tensor_tensor
                    pool.wait_ge(s["s_cur"], g + 1)
                    st.add(TT(out=dter[:, :, :, :], in0=cur[:, 4, :, :, :], in1=cur[:, 2, :, :, :], op=ALU.mult))
                    for u in range(2 * NT):
                        t, d = u // 2, u % 2
                        if u >= 2:
                            pool.wait_ge(s["s_seg"], 10 * g + u - 1)
                        TT(out=am[:, d, :, :], in0=C((C_LE, C_GE)[d]).unsqueeze(1).broadcast_to([P, HG, P]),
                           in1=cur[:, 0, t, d, :].unsqueeze(2).broadcast_to([P, HG, P]), op=ALU.mult).then_inc(s["s_am"], 1)
                        if u >= 3 and d == 1 or u == 2 * NT - 1:
                            for tt in ([t - 1] if u < 2 * NT - 1 else [t - 1, t]):
                                if tt == 0:
                                    continue
                                skip(pool, s, TT, g, tt, ysum, xt, dg, hv)
                        if u == 1:
                            pool.wait_ge(s["s_turnkept"], 5 * g + 5)
                            skip(pool, s, TT, g, 0, ysum, xt, dg, hv)
                    st.wait()
                    for p, tiles in enumerate(CHAIN):
                        if p >= 2:
                            pool.wait_ge(s["s_st"], 5 * g + p - 1)
                        for d, t in enumerate(tiles):
                            last = TT(out=hv(xe[:, p % 2, d, :]), in0=hv(xt[:, t, :]), in1=dter[:, t, d, :].unsqueeze(2).broadcast_to([P, HG, SP_]), op=ALU.mult)
                        last.then_inc(s["s_xe"], 1)
                    hold(pool, s["s_yss"], 5 * g + 5)
                    st.link(pool.tensor_scalar(out=ysc[:, :], in0=yss[:, :], scalar1=1.0 / GW, scalar2=EPS, op0=ALU.mult, op1=ALU.add))
                    st.link(TT(out=ysc[:, :], in0=ysc[:, :], in1=half[:, 0:NT], op=ALU.pow))
                    pool.tensor_scalar(out=ysc[:, :], in0=ysc[:, :], scalar1=0.5, scalar2=None, op0=ALU.mult).then_inc(s["s_ysc"], 1)
                    assert st.n == POOL_STEPS, st.n

            @block.vector
            def _(dve):
                dve.drain().then_inc(s["s_group"], 1)
                TT, TS, STT = dve.tensor_tensor, dve.tensor_scalar, dve.scalar_tensor_tensor
                with dve.Fori(0, SG) as g:
                    st = Steps(dve, s["s_dve"], g * DVE_STEPS)
                    if True:
                        dve.wait_ge(s["s_group"], g + 1)
                    for d in range(2):
                        st.add(dve.tensor_copy(cur[:, :, :, d, :], ST[:, :, :, bass.ds(g * HG + (2 * GH + d * SH), HG)]))
                    for n in range(NJ):
                        at = g + (16, 20)[n] if n < 2 else g * NQ + (n - 2)
                        st.add(TS(out=cw[:, :, n:n + 1], in0=cwT[:, 1, :, bass.ds(at, 1)], scalar1=0.5, scalar2=None, op0=ALU.mult))
                        at = g + (40, 44)[n] if n < 2 else g * NQ + (24 + n - 2)
                        st.add(TS(out=cb[:, n:n + 1], in0=vecT[:, bass.ds(at, 1)], scalar1=0.5, scalar2=None, op0=ALU.mult))
                    dve.wait_ge(s["s_din"], 16)
                    st.add(dve.tensor_copy(dg[:, :], dskip[:, bass.ds(g * HG, HG)]))
                    hold(dve, s["s_dve"], st.base + st.n)
                    dve.engine_nop().then_inc(s["s_cur"], 1)

                    def silu(n):
                        dve.wait_ge(s["s_tanh"], NJ * g + n + 1)
                        if n >= 5:
                            dve.wait_ge(s["s_turn"], 5 * g + n - 3)
                        to = (BT, CT)[n] if n < 2 else xT[:, (n - 2) % 3, :, :]
                        STT(out=to[:, 0, :], in0=th[:, n % 3, 0:SEQ], scalar=1.0, in1=conv[:, n % 3, 0:SEQ], op0=ALU.add, op1=ALU.mult)
                        STT(out=to[:, 1:NT, :], in0=th[:, n % 3, LAT:CW].rearrange("p (t n) -> p t n", n=P), scalar=1.0,
                            in1=conv[:, n % 3, LAT:CW].rearrange("p (t n) -> p t n", n=P),
                            op0=ALU.add, op1=ALU.mult).then_inc(s["s_silu"], 1)

                    for n in range(NJ):
                        dve.wait_ge(s["s_raw"], NJ * g + n + 1)
                        c3 = conv[:, n % 3, :]
                        st.link(TS(out=c3, in0=padded[:, n % 3, 0:CW], scalar1=cw[:, 0, n:n + 1], scalar2=cb[:, n:n + 1], op0=ALU.mult, op1=ALU.add))
                        for k in range(1, TAPS):
                            ins = STT(out=c3, in0=padded[:, n % 3, k:k + CW], scalar=cw[:, k, n:n + 1], in1=c3, op0=ALU.mult, op1=ALU.add)
                            if k < TAPS - 1:
                                st.link(ins)
                            else:
                                ins.then_inc(s["s_conv"], 1)
                        if n > 0:
                            silu(n - 1)
                    silu(NJ - 1)

                    def keep_y(t):
                        dve.wait_ge(s["s_y"], 10 * g + 2 * t + 2)
                        dve.wait_ge(s["s_dx"], 5 * g + t + 1)
                        TT(out=ysum[:, t, :], in0=ysum[:, t, :], in1=bank[6 + t % 2][:, :], op=ALU.add).then_inc(s["s_ykept"], 1)

                    dve.wait_ge(s["s_turnkept"], 5 * g + 5)
                    for u in range(2 * NT):
                        t, d = u // 2, u % 2
                        if d == 0:
                            dve.wait_ge(s["s_cb"], 5 * g + t + 1)
                            for e in range(2):
                                st.add(TT(out=cbm[:, t % 2, e, :], in0=bank[4 + t % 2][:, 0:P], in1=C((C_LE, C_GE)[e]), op=ALU.mult))
                        if u >= 2:
                            dve.wait_ge(s["s_y"], 10 * g + u - 1)
                        TT(out=hv(dtx[:, d, :]), in0=hv(xt[:, t, :]), in1=cur[:, 4, t, d, :].unsqueeze(2).broadcast_to([P, HG, SP_]), op=ALU.mult)
                        if d == 0:
                            st.wait()
                        dve.wait_ge(s["s_dec"], 10 * g + u + 1)
                        TT(out=M[:, d, :, :], in0=dec[:, d, :, :], in1=cbm[:, t % 2, d:d + 1, :].broadcast_to([P, HG, P]), op=ALU.mult).then_inc(s["s_M"], 1)
                        if d == 1 and t >= 1:
                            keep_y(t - 1)
                    keep_y(NT - 1)

                    def gate(t):
                        dve.wait_ge(s["s_zth"], 5 * g + t + 1)
                        STT(out=zs(t), in0=zth(t), scalar=1.0, in1=bank[4 + t % 4][:, :], op0=ALU.add, op1=ALU.mult).then_inc(s["s_zs"], 1)

                    for p, tiles in enumerate(CHAIN):
                        if p == 1:
                            dve.wait_ge(s["s_init"], g + 1)
                            dve.wait_ge(s["s_outturn"], g + 1)
                        if p > 0:
                            dve.wait_ge(s["s_yoff"], 4 * g + p)
                            for d, t in enumerate(tiles):
                                st.add(TT(out=hv(state[:, d, :]), in0=hv(state[:, d, :]), in1=cur[:, 3, t, d, :].unsqueeze(2).broadcast_to([P, HG, SP_]), op=ALU.mult))
                            st.wait()
                        dve.wait_ge(s["s_st"], 5 * g + p + 1)
                        for d, t in enumerate(tiles):
                            if p == 0:
                                dve.tensor_copy(state[:, d, :], bank[2 + d][:, :]).then_inc(s["s_state"], 1)
                            else:
                                TT(out=state[:, d, :], in0=state[:, d, :], in1=bank[2 + d][:, :], op=ALU.add).then_inc(s["s_state"], 1)
                        if p > 0:
                            for d, t in enumerate(tiles):
                                ins = TT(out=hv(tmp[:, d, :]), in0=hv(bank[d][:, :]), in1=cur[:, 1, t, d, :].unsqueeze(2).broadcast_to([P, HG, SP_]), op=ALU.mult)
                                st.add(ins) if d == 0 else ins.then_inc(s["s_yoffkept"], 1)
                            dve.wait_ge(s["s_yoffkept"], 4 * g + p)
                            for d, t in enumerate(tiles):
                                st.add(TT(out=ysum[:, t, :], in0=ysum[:, t, :], in1=tmp[:, d, :], op=ALU.add))
                            st.wait()
                            gate(p - 1)
                    gate(4)
                    dve.wait_ge(s["s_zs"], 5 * g + 5)
                    for t in range(NT):
                        TT(out=ysum[:, t, :], in0=ysum[:, t, :], in1=zs(t), op=ALU.mult).then_inc(s["s_yz"], 1)
                    dve.wait_ge(s["s_ysc"], g + 1)
                    for t in range(NT):
                        TS(out=ysum[:, t, :], in0=ysum[:, t, :], scalar1=ysc[:, t:t + 1], scalar2=None, op0=ALU.mult).then_inc(s["s_yn"], 1)
                    assert st.n == DVE_STEPS, st.n


def skip(pool, s, TT, g, t, ysum, xt, dg, hv):
    TT(out=hv(ysum[:, t, :]), in0=hv(xt[:, t, :]), in1=dg[:, :].unsqueeze(2).broadcast_to([P, HG, SP_]), op=ALU.mult).then_inc(s["s_dx"], 1)


def merge(nc, sb, sem, bank, hT, oT, yT, mT, w_in, w_gdn_out, w_ssd_out):
    own = ExitStack()
    with own:
        S = lambda name, shape, dt=F32: sb(name, shape, dt, own)
        KS = SH * SP_ // P
        wm = S("wm", [P, 2, 3 * KD + KS, P])
        gth = S("gth", [P, 2, T])
        prod = S("prod", [P, 2, T])
        SRC = ((0, KD, hT), (KD, KD, hT), (2 * KD, KD, oT), (3 * KD, KS, yT))
        wm_in = [sem("wm_in0"), sem("wm_in1")]
        wm_used, m_done, m_tanh, m_prod, m_kept, m_free = (sem(n) for n in ("wm_used", "m_done", "m_tanh", "m_prod", "m_kept", "m_free"))
        with nc.Block() as block:
            @block.sync
            def _(sp):
                def load(n, par):
                    for at, w, off in ((0, w_in[0], O_GATE), (KD, w_in[0], O_GATE + D), (2 * KD, w_gdn_out[0], 0), (3 * KD, w_ssd_out[0], 0)):
                        kk = KS if at == 3 * KD else KD
                        sp.dma_start(wm[:, par, at:at + kk, :], w[:, bass.ds(n * P + off, P)].rearrange("(k p) n -> p k n", p=P)).then_inc(wm_in[par], 16)

                load(0, 0)
                load(1, 1)
                with sp.Fori(0, KD // 2 - 1) as i:
                    for par in range(2):
                        sp.wait_ge(m_done, 5 * (2 * i + par) + 5)
                        load(2 * i + par + 2, par)

            @block.tensor
            def _(pe):
                def turn(i, par, first):
                    n = 2 * i + par
                    pe.wait_ge(wm_in[par], 64 * (i + 1))
                    for j, (at, kk, src) in enumerate(SRC):
                        if not first:
                            if j < 2:
                                pe.wait_ge(m_tanh, 3 * (n - 1) + j + 1)
                                pe.wait_ge(m_kept, n)
                            else:
                                pe.wait_ge(m_kept, n)
                        for k in range(kk):
                            last = pe.matmul(bank[j][:, :], wm[:, par, at + k, :], src[:, k, SEQ:T], start=(k == 0), stop=(k == kk - 1))
                        last.then_inc(m_done, 1)
                    for j, (at, kk, src) in enumerate(SRC):
                        for k in range(kk):
                            last = pe.matmul(bank[4][:, j * P:(j + 1) * P], wm[:, par, at + k, :], src[:, k, 0:SEQ], start=(k == 0), stop=(k == kk - 1))
                    last.then_inc(m_done, 1)

                turn(0, 0, True)
                turn(0, 1, False)
                with pe.Fori(1, KD // 2) as i:
                    for par in range(2):
                        turn(i, par, False)

            @block.scalar
            def _(act):
                act.wait_ge(m_free, 1)
                with act.Fori(0, KD) as n:
                    act.wait_ge(m_free, n + 1)
                    for j in range(2):
                        act.wait_ge(m_done, 5 * n + j + 1)
                        act.activation(gth[:, j, SEQ:T], bank[j][:, :], ACT.Tanh, scale=0.5).then_inc(m_tanh, 1)
                    act.wait_ge(m_done, 5 * n + 5)
                    act.activation(gth[:, :, 0:SEQ], bank[4][:, 0:2 * P].rearrange("p (j n) -> p j n", j=2), ACT.Tanh, scale=0.5).then_inc(m_tanh, 1)

            @block.vector
            def _(dve):
                dve.drain().then_inc(m_free, 1)
                with dve.Fori(0, KD) as n:
                    for j in range(2):
                        dve.wait_ge(m_tanh, 3 * n + j + 1)
                        dve.wait_ge(m_done, 5 * n + j + 3)
                        dve.scalar_tensor_tensor(out=prod[:, j, SEQ:T], in0=gth[:, j, SEQ:T], scalar=1.0, in1=bank[2 + j][:, :], op0=ALU.add, op1=ALU.mult).then_inc(m_prod, 1)
                    dve.wait_ge(m_tanh, 3 * n + 3)
                    dve.scalar_tensor_tensor(out=prod[:, :, 0:SEQ], in0=gth[:, :, 0:SEQ], scalar=1.0,
                                             in1=bank[4][:, 2 * P:4 * P].rearrange("p (j n) -> p j n", j=2), op0=ALU.add, op1=ALU.mult).then_inc(m_kept, 1)
                    dve.wait_ge(m_prod, 2 * n + 2)
                    dve.wait_ge(m_kept, n + 1)
                    dve.tensor_tensor(out=mT[:, bass.ds(n, 1), :], in0=prod[:, 0:1, :], in1=prod[:, 1:2, :], op=ALU.add).then_inc(m_free, 1)


def route(nc, sb, sem, bank, C, cols, half, mT, ada, pos, x_prompt, x_sample, w_o, ln1_g, ln1_b, w_router_group,
          b_router_group, w_router_expert, b_router_expert, h2d, x1d, lists, yd, idx, slots, wts, more):
    own = ExitStack()
    with own:
        S = lambda name, shape, dt=F32: sb(name, shape, dt, own)
        NR = XG + NX
        wo = S("wo", [P, KD, D])
        wr = S("wr", [P, KD, NR])
        br = S("br", [P, NR])
        x = S("rx", [P, NT, D])
        pt = S("rpos", [P, NT - 1, D])
        g1 = S("g1", [P, 2, D])
        sc2 = S("sc2", [P, 2, D])
        sh2 = S("sh2", [P, 2, D])
        lg = S("lg", [P, D])
        lb = S("lb", [P, D])
        tmp = S("rtmp", [P, D])
        bn = S("rbn", [P, 2, 6])
        mv = S("rmv", [P, 2])
        ve = S("rve", [P, 2, NT])
        rs = S("rrs", [P, 2, NT])
        h2 = S("h2", [P, 2, D])
        h2T = S("h2T", [P, KD, P])
        lo = S("lo", [P, NT, NR])
        gmax = S("gmax", [P, NT, 1])
        gsh = S("gsh", [P, NT, XG])
        gex = S("gex", [P, NT, XG])
        gsum = S("gsum", [P, NT, 1])
        eq = S("eq", [P, NT, XG])
        rank = S("rank", [P, NT, 1])
        lsel = S("lsel", [P, NT, XG, XE])
        les = S("les", [P, NT, XE])
        top = S("top8", [P, NT, 8])
        topi = S("topi", [P, NT, 8], U32)
        eid = S("eid", [P, NT, 2])
        gidx = S("gidx", [P, NT, 1])
        dif = S("dif", [P, NT, 1])
        tex = S("tex", [P, NT, 1])
        oh = S("oh", [P, 2, NT, NX])
        both = S("both", [P, NT, NX])
        place = S("place", [P, NT, NX])
        pick = S("pick", [P, 2, NT, NX])
        slotf = S("slotf", [P, 2, NT, 1])
        nmore = S("nmore", [P, NX])
        upto = S("upto", [P, NX])
        far = S("far", [P, NX])
        past = S("past", [P, NT, NX])
        later = S("later", [P, NMORE, NX])
        whose = S("whose", [P, NMORE + 1])
        zero = S("zero", [P, D])
        rows_ = S("rows_", [NX, P])
        x_in, wo_in, wr_in, row_in, pos_in = (sem(n) for n in ("r_x", "r_wo", "r_wr", "r_row", "r_pos"))
        mixed, x1_done, ve_ready, rs_ready, h2_ready, x1_out = (sem(n) for n in (
            "r_mixed", "r_x1", "r_ve", "r_rs", "r_h2", "r_x1out"))
        h2_out = [sem("r_h2out0"), sem("r_h2out1")]
        h2_turned, h2_kept, logits, lo_kept, z_out, gs_ready, gex_ready, dif_ready, tex_ready = (sem(n) for n in (
            "r_turned", "r_kept", "r_logits", "r_lokept", "r_zout", "r_gs", "r_gex", "r_dif", "r_tex"))
        both_ready, counted, slots_ready, scattered, rows_in, rows_turned, own_dve, sq_kept = (sem(n) for n in (
            "r_both", "r_counted", "r_slots", "r_scattered", "r_rowsin", "r_rowsturned", "r_dve", "r_free"))
        zero_ready, yz_out = sem("r_zero"), sem("r_yz")
        rows = lambda ap: ap.partition_broadcast(P)
        with nc.Block() as block:
            @block.sync
            def _(sp):
                sp.dma_start(wo[:, :, :], w_o[0].rearrange("(k p) n -> p k n", p=P)).then_inc(wo_in, 16)
                sp.dma_start(x[:, 0, :], x_prompt[0]).then_inc(x_in, 16)
                sp.dma_start(x[:, 1:NT, :], x_sample[0].rearrange("(t p) n -> p t n", p=P)).then_inc(x_in, 16)
                for cond in range(2):
                    sp.dma_start(g1[:, cond, :], rows(ada[cond, 2 * D:3 * D])).then_inc(row_in, 16)
                    sp.dma_start(sh2[:, cond, :], rows(ada[cond, 3 * D:4 * D])).then_inc(row_in, 16)
                    sp.dma_start(sc2[:, cond, :], rows(ada[cond, 4 * D:5 * D])).then_inc(row_in, 16)
                sp.dma_start(lg[:, :], rows(ln1_g[0])).then_inc(row_in, 16)
                sp.dma_start(lb[:, :], rows(ln1_b[0])).then_inc(row_in, 16)
                sp.dma_start(wr[:, :, 0:XG], w_router_group[0].rearrange("(k p) n -> p k n", p=P)).then_inc(wr_in, 16)
                sp.dma_start(wr[:, :, XG:NR], w_router_expert[0].rearrange("(k p) n -> p k n", p=P)).then_inc(wr_in, 16)
                sp.dma_start(br[:, 0:XG], rows(b_router_group[0])).then_inc(wr_in, 16)
                sp.dma_start(br[:, XG:NR], rows(b_router_expert[0])).then_inc(wr_in, 16)
                sp.wait_ge(zero_ready, 1)
                sp.dma_start(lists.rearrange("(p n) a -> p (n a)", p=P), zero[:, 0:NPLACE // P]).then_inc(z_out, 16)
                sp.dma_start(yd[NX * P:NPLACE, :].rearrange("(b p) n -> p b n", p=P), zero[:, :].unsqueeze(1).broadcast_to([P, NMORE, D])).then_inc(yz_out, 16)
                for t in range(NT):
                    sp.wait_ge(x1_done, t + 1)
                    sp.dma_start(x1d[t * P:(t + 1) * P, :], x[:, t, :]).then_inc(x1_out, 16)
                    sp.wait_ge(h2_ready, t + 1)
                    sp.dma_start(h2d[t * P:(t + 1) * P, :], h2[:, t % 2, :]).then_inc(h2_out[t % 2], 16)
                sp.wait_ge(scattered, 16 * 2 * NT)
                sp.dma_start(rows_[:, :], lists[0:NX * P, :].rearrange("(e n) a -> e (n a)", e=NX)).then_inc(rows_in, 16)
                sp.wait_ge(x1_out, 16 * NT)
                sp.wait_ge(yz_out, 16)
                sp.wait_ge(h2_out[0], 16 * 3)
                sp.wait_ge(h2_out[1], 16 * 2)

            @block.scalar
            def _(act):
                act.dma_start(pt[:, :, :], pos.rearrange("(t p) n -> p t n", p=P)).then_inc(pos_in, 16)
                for t in range(NT):
                    act.wait_ge(h2_turned, t + 1)
                    if t > 0:
                        act.wait_ge(logits, t)
                    for h in range(2):
                        last = act.copy(h2T[:, 4 * h:4 * h + 4, :], bank[4 + h][:, :].rearrange("p (k n) -> p k n", n=P))
                    last.then_inc(h2_kept, 1)
                act.wait_ge(gs_ready, 1)
                act.activation(gex[:, :, :], gsh[:, :, :], ACT.Exp).then_inc(gex_ready, 1)
                act.wait_ge(dif_ready, 1)
                act.activation(tex[:, :, :], dif[:, :, :], ACT.Exp).then_inc(tex_ready, 1)

            @block.tensor
            def _(pe):
                pe.wait_ge(wo_in, 16)
                def mix(t):
                    if t >= 2:
                        pe.wait_ge(sq_kept, t - 1)
                    for h in range(2):
                        for k in range(KD):
                            last = pe.matmul(bank[2 * (t % 2) + h][:, :], mT[:, k, t * P:(t + 1) * P], wo[:, k, h * 512:(h + 1) * 512], start=(k == 0), stop=(k == KD - 1))
                    last.then_inc(mixed, 1)

                def router(t):
                    pe.wait_ge(h2_ready, t + 1)
                    if t > 0:
                        pe.wait_ge(h2_kept, t)
                    for k in range(KD):
                        last = pe.transpose(bank[4 + k // 4][:, k % 4 * P:k % 4 * P + P], h2[:, t % 2, k * P:(k + 1) * P], C(C_ID))
                    last.then_inc(h2_turned, 1)
                    pe.wait_ge(h2_kept, t + 1)
                    if t == 0:
                        pe.wait_ge(wr_in, 64)
                    else:
                        pe.wait_ge(lo_kept, t)
                    for k in range(KD):
                        last = pe.matmul(bank[6][:, 0:NR], h2T[:, k, :], wr[:, k, :], start=(k == 0), stop=(k == KD - 1))
                    last.then_inc(logits, 1)

                mix(0)
                mix(1)
                for t in range(NT):
                    if t + 2 < NT:
                        mix(t + 2)
                    router(t)
                pe.wait_ge(both_ready, 1)
                for t in range(NT):
                    for e in range(t):
                        pe.matmul(bank[7][:, t * NX:(t + 1) * NX], C(C_ONE), both[:, e, :], start=(e == 0), stop=False)
                    pe.matmul(bank[7][:, t * NX:(t + 1) * NX], C(C_LT), both[:, t, :], start=(t == 0), stop=True)
                for t in range(NT):
                    last = pe.matmul(bank[7][:, NT * NX:(NT + 1) * NX], C(C_ONE), both[:, t, :], start=(t == 0), stop=(t == NT - 1))
                last.then_inc(counted, 1)
                pe.wait_ge(rows_in, 16)
                pe.transpose(bank[4][:, 0:NX], rows_[:, :], C(C_ID)[0:NX, 0:NX]).then_inc(rows_turned, 1)

            @block.gpsimd
            def _(pool):
                pool.memset(zero[:, :], 0.0).then_inc(zero_ready, 1)
                for t in range(NT):
                    for n in range(2):
                        pool.wait_ge(ve_ready, 2 * t + n + 1)
                        pool.tensor_tensor(out=rs[:, n, t:t + 1], in0=ve[:, n, t:t + 1], in1=half[:, 0:1], op=ALU.pow).then_inc(rs_ready, 1)
                pool.wait_ge(z_out, 16)
                pool.wait_ge(slots_ready, 1)
                for t in range(NT):
                    for n in range(2):
                        pool.indirect_dma_start(out=lists, out_offset=bass.IndirectOffsetOnAxis(ap=slots[:, t, n:n + 1], axis=0),
                                                in_=cols[:, S_TOK + t:S_TOK + t + 1], in_offset=None).then_inc(scattered, 16)
                pool.wait_ge(scattered, 16 * 2 * NT)

            @block.vector
            def _(dve):
                st = Steps(dve, own_dve)
                TT, TS, STT = dve.tensor_tensor, dve.tensor_scalar, dve.scalar_tensor_tensor
                cst_one = C(C_ONE)[:, 0:NX]
                dve.wait_ge(row_in, 128)
                for cond in range(2):
                    TS(out=g1[:, cond, :], in0=g1[:, cond, :], scalar1=0.5, scalar2=None, op0=ALU.mult)
                    st.add(TS(out=sc2[:, cond, :], in0=sc2[:, cond, :], scalar1=1.0, scalar2=None, op0=ALU.add))
                st.wait()
                dve.wait_ge(x_in, 32)

                def norm(t, n):
                    dve.bn_stats(bn[:, 0, :], x[:, t, 0:512])
                    st.link(dve.bn_stats(bn[:, 1, :], x[:, t, 512:D]))
                    st.link(dve.bn_aggr(mv[:, :], bn[:, :, :]))
                    TS(out=ve[:, n, t:t + 1], in0=mv[:, 1:2], scalar1=EPS, scalar2=None, op0=ALU.add).then_inc(ve_ready, 1)
                    dve.wait_ge(rs_ready, 2 * t + n + 1)
                    st.link(TS(out=tmp[:, :], in0=x[:, t, :], scalar1=mv[:, 0:1], scalar2=rs[:, n, t:t + 1], op0=ALU.subtract, op1=ALU.mult))

                for t in range(NT):
                    cond = min(t, 1)
                    if t > 0:
                        dve.wait_ge(pos_in, 16)
                        st.link(TT(out=x[:, t, :], in0=x[:, t, :], in1=pt[:, t - 1, :], op=ALU.add))
                    dve.wait_ge(mixed, t + 1)
                    if t > 0:
                        dve.wait_ge(h2_ready, t)
                    for h in range(2):
                        ins = TT(out=tmp[:, h * 512:(h + 1) * 512], in0=bank[2 * (t % 2) + h][:, :], in1=g1[:, cond, h * 512:(h + 1) * 512], op=ALU.mult)
                    ins.then_inc(sq_kept, 1)
                    dve.wait_ge(sq_kept, t + 1)
                    st.link(STT(out=x[:, t, :], in0=x[:, t, :], scalar=ALPHA, in1=tmp[:, :], op0=ALU.mult, op1=ALU.add))
                    norm(t, 0)
                    st.link(TT(out=tmp[:, :], in0=tmp[:, :], in1=lg[:, :], op=ALU.mult))
                    TT(out=x[:, t, :], in0=tmp[:, :], in1=lb[:, :], op=ALU.add).then_inc(x1_done, 1)
                    dve.wait_ge(x1_done, t + 1)
                    norm(t, 1)
                    if t >= 2:
                        dve.wait_ge(h2_out[t % 2], 16 * (t // 2))
                        dve.wait_ge(h2_turned, t - 1)
                    st.link(TT(out=tmp[:, :], in0=tmp[:, :], in1=sc2[:, cond, :], op=ALU.mult))
                    TT(out=h2[:, t % 2, :], in0=tmp[:, :], in1=sh2[:, cond, :], op=ALU.add).then_inc(h2_ready, 1)
                    if t > 0:
                        dve.wait_ge(logits, t)
                        TT(out=lo[:, t - 1, :], in0=bank[6][:, 0:NR], in1=br[:, :], op=ALU.add).then_inc(lo_kept, 1)
                dve.wait_ge(logits, NT)
                TT(out=lo[:, NT - 1, :], in0=bank[6][:, 0:NR], in1=br[:, :], op=ALU.add).then_inc(lo_kept, 1)
                dve.wait_ge(lo_kept, NT)
                st.link(dve.tensor_reduce(out=gmax[:, :, :], in_=lo[:, :, 0:XG], axis=AX.X, op=ALU.max))
                TT(out=gsh[:, :, :], in0=lo[:, :, 0:XG], in1=gmax[:, :, :].broadcast_to([P, NT, XG]), op=ALU.subtract).then_inc(gs_ready, 1)
                st.link(TT(out=eq[:, :, :], in0=lo[:, :, 0:XG], in1=gmax[:, :, :].broadcast_to([P, NT, XG]), op=ALU.is_equal))
                grp = cols[:, S_GRP:S_GRP + XG].unsqueeze(1).broadcast_to([P, NT, XG])
                st.link(TT(out=eq[:, :, :], in0=eq[:, :, :], in1=grp, op=ALU.mult))
                st.link(dve.tensor_reduce(out=rank[:, :, :], in_=eq[:, :, :], axis=AX.X, op=ALU.max))
                st.link(TT(out=eq[:, :, :], in0=grp, in1=rank[:, :, :].broadcast_to([P, NT, XG]), op=ALU.is_equal))
                st.link(TS(out=gidx[:, :, :], in0=rank[:, :, :], scalar1=-float(XE), scalar2=float(XE * XG), op0=ALU.mult, op1=ALU.add))
                for t in range(NT):
                    ins = TT(out=lsel[:, t, :, :], in0=lo[:, t, XG:NR].rearrange("p (g e) -> p g e", g=XG),
                             in1=eq[:, t, :].unsqueeze(2).broadcast_to([P, XG, XE]), op=ALU.mult)
                st.link(ins)
                for t in range(NT):
                    ins = dve.tensor_reduce(out=les[:, t, :], in_=lsel[:, t, :, :].rearrange("p g e -> p e g"), axis=AX.X, op=ALU.add)
                st.link(ins)
                for t in range(NT):
                    ins = dve.max(top[:, t, :], les[:, t, :])
                st.link(ins)
                for t in range(NT):
                    ins = dve.max_index(topi[:, t, :], top[:, t, :], les[:, t, :])
                st.link(ins)
                TT(out=dif[:, :, :], in0=top[:, :, 1:2], in1=top[:, :, 0:1], op=ALU.subtract).then_inc(dif_ready, 1)
                st.link(dve.tensor_copy(eid[:, :, :], topi[:, :, 0:2]))
                st.link(TT(out=eid[:, :, :], in0=eid[:, :, :], in1=gidx[:, :, :].broadcast_to([P, NT, 2]), op=ALU.add))
                for n in range(2):
                    ins = TT(out=oh[:, n, :, :], in0=cols[:, S_E:S_E + NX].unsqueeze(1).broadcast_to([P, NT, NX]),
                             in1=eid[:, :, n:n + 1].broadcast_to([P, NT, NX]), op=ALU.is_equal)
                st.link(ins)
                TT(out=both[:, :, :], in0=oh[:, 0, :, :], in1=oh[:, 1, :, :], op=ALU.add).then_inc(both_ready, 1)
                dve.wait_ge(gex_ready, 1)
                dve.wait_ge(tex_ready, 1)
                st.link(dve.tensor_reduce(out=gsum[:, :, :], in_=gex[:, :, :], axis=AX.X, op=ALU.add))
                st.link(TS(out=wts[:, :, 0:1], in0=tex[:, :, :], scalar1=1.0, scalar2=2.0, op0=ALU.add, op1=ALU.mult))
                st.link(TT(out=wts[:, :, 0:1], in0=wts[:, :, 0:1], in1=gsum[:, :, :], op=ALU.mult))
                st.link(dve.reciprocal(wts[:, :, 0:1], wts[:, :, 0:1]))
                st.link(TT(out=wts[:, :, 1:2], in0=wts[:, :, 0:1], in1=tex[:, :, :], op=ALU.mult))
                dve.wait_ge(counted, 1)
                count = bank[7][:, NT * NX:(NT + 1) * NX]
                st.link(TS(out=nmore[:, :], in0=count, scalar1=float(P), scalar2=None, op0=ALU.is_gt))
                for b in range(2, T // P):
                    st.link(STT(out=nmore[:, :], in0=count, scalar=float(b * P), in1=nmore[:, :], op0=ALU.is_gt, op1=ALU.add))
                st.link(dve.tensor_tensor_scan(out=upto[:, :], data0=cst_one, data1=nmore[:, :], initial=0.0, op0=ALU.mult, op1=ALU.add))
                st.link(TT(out=far[:, :], in0=upto[:, :], in1=nmore[:, :], op=ALU.subtract))
                st.link(STT(out=far[:, :], in0=far[:, :], scalar=float(P), in1=cols[:, S_FAR:S_FAR + NX], op0=ALU.mult, op1=ALU.add))
                places = bank[7][:, 0:NT * NX].rearrange("p (t e) -> p t e", e=NX)
                st.link(TS(out=past[:, :, :], in0=places, scalar1=float(P), scalar2=None, op0=ALU.is_ge))
                st.link(TT(out=past[:, :, :], in0=past[:, :, :], in1=far[:, :].unsqueeze(1).broadcast_to([P, NT, NX]), op=ALU.mult))
                st.link(TT(out=place[:, :, :], in0=places, in1=cols[:, S_LIST:S_LIST + NX].unsqueeze(1).broadcast_to([P, NT, NX]), op=ALU.add))
                st.link(TT(out=place[:, :, :], in0=place[:, :, :], in1=past[:, :, :], op=ALU.add))
                for n in range(2):
                    ins = TT(out=pick[:, n, :, :], in0=oh[:, n, :, :], in1=place[:, :, :], op=ALU.mult)
                st.link(ins)
                st.link(dve.tensor_reduce(out=slotf[:, :, :, :], in_=pick[:, :, :, :], axis=AX.X, op=ALU.add))
                dve.tensor_copy(slots[:, :, :], slotf[:, :, :, 0].rearrange("p n t -> p t n")).then_inc(slots_ready, 1)
                st.link(TT(out=later[:, :, :], in0=upto[:, :].unsqueeze(1).broadcast_to([P, NMORE, NX]),
                           in1=cols[:, S_MORE:S_MORE + NMORE].unsqueeze(2).broadcast_to([P, NMORE, NX]), op=ALU.is_le))
                st.link(dve.tensor_reduce(out=whose[:, 0:NMORE].unsqueeze(2), in_=later[:, :, :], axis=AX.X, op=ALU.add))
                st.link(dve.tensor_copy(whose[:, NMORE:NMORE + 1], upto[:, NX - 1:NX]))
                st.link(dve.tensor_copy(more[:, :], whose[:, :]))
                dve.wait_ge(rows_turned, 1)
                st.link(dve.tensor_copy(idx[:, :], bank[4][:, 0:NX]))


def experts(nc, sb, sem, bank, C, idx, more, lists, h2d, yd, w_exp_gate, w_exp_up, w_exp_down):
    own = ExitStack()
    with own:
        S = lambda name, shape, dt=F32: sb(name, shape, dt, own)
        NB = 4
        NF = FX // P
        wgu = S("wgu", [P, NB, KD, 2, FX])
        wdn = S("wdn", [P, NB, NF, D])
        idxs = S("idxs", [P, NB], U32)
        xg = S("xg", [P, NB, D])
        xgT = S("xgT", [P, 2, KD, P])
        eth = S("eth", [P, 2, FX])
        eh = S("eh", [P, FX])
        hid = S("hid", [P, 2, FX])
        hidT = S("hidT", [P, NF, P])
        ysb = S("ysb", [P, 2, D])
        idf = S("idf", [P, 1])
        w_in_ = [sem(f"e_w{n}") for n in range(NB)]
        got = [sem(f"e_got{n}") for n in range(NB)]
        y_out = [sem("e_yout0"), sem("e_yout1")]
        (x_turned, x_kept, gu_done, th_ready, a_ready, hid_ready, ht_turned, ht_kept, dn_done, y_dve, y_act,
         idx_ready) = (sem("e_" + n) for n in ("xturned", "xkept", "gu", "th", "a", "hid", "htturned", "htkept", "dn",
                                               "ydve", "yact", "idx"))
        V = lambda ap: ap.rearrange("(p k) f -> p k f", p=P)

        def load(sp, e, par):
            one = lambda w: w[0, bass.ds(e, 1), :, :].rearrange("a d f -> (a d) f")
            sp.dma_start(wgu[:, par, :, 0, :], V(one(w_exp_gate))).then_inc(w_in_[par], 16)
            sp.dma_start(wgu[:, par, :, 1, :], V(one(w_exp_up))).then_inc(w_in_[par], 16)
            sp.dma_start(wdn[:, par, :, :], V(one(w_exp_down))).then_inc(w_in_[par], 16)

        def turn_x(pe, par):
            for k in range(KD):
                last = pe.transpose(bank[k // 4][:, k % 4 * P:k % 4 * P + P], xg[:, par, k:D:KD], C(C_ID))
            return last

        def gate_up(pe, par, slot, to):
            for k in range(KD):
                last = pe.matmul(to[:, :], xgT[:, slot, k, :], wgu[:, par, k, :, :].rearrange("p a f -> p (a f)"), start=(k == 0), stop=(k == KD - 1))
            return last

        def turn_h(pe, slot):
            for j in range(NF):
                last = pe.transpose(bank[4][:, j * P:(j + 1) * P], hid[:, slot, j:FX:NF], C(C_ID))
            return last

        def down(pe, par):
            for h in range(2):
                for j in range(NF):
                    last = pe.matmul(bank[5 + h][:, :], hidT[:, j, :], wdn[:, par, j, h * 512:(h + 1) * 512], start=(j == 0), stop=(j == NF - 1))
            return last

        def turns(body):
            def run(eng):
                with eng.Fori(0, NX // NB - 1) as i:
                    for par in range(NB):
                        body(i * NB + par, i, par, True, True)
                for par in range(NB):
                    body(NX - NB + par, NX // NB - 1, par, par < NB - 1, par < NB - 2)
            return run

        with nc.Block() as block:
            @block.sync
            def _(sp):
                for par in range(NB):
                    load(sp, par, par)
                with sp.Fori(0, NX // NB - 1) as i:
                    for par in range(NB):
                        sp.wait_ge(dn_done, i * NB + par + 1)
                        load(sp, i * NB + par + NB, par)

            @block.gpsimd
            def _(pool):
                def gather(e, par):
                    pool.tensor_copy(idxs[:, par:par + 1], idx[:, bass.ds(e, 1)]).then_inc(idx_ready, 1)
                    hold(pool, idx_ready, e + 1)
                    pool.indirect_dma_start(out=xg[:, par, :], out_offset=None, in_=h2d,
                                            in_offset=bass.IndirectOffsetOnAxis(ap=idxs[:, par:par + 1], axis=0)).then_inc(got[par], 16)

                for par in range(NB):
                    gather(par, par)
                with pool.Fori(0, NX // NB - 1) as i:
                    for par in range(NB):
                        pool.wait_ge(x_turned, i * NB + par + 1)
                        pool.wait_ge(got[par], i * 16 + 16)
                        gather(i * NB + par + NB, par)

            @block.tensor
            def _(pe):
                pe.wait_ge(got[0], 16)
                turn_x(pe, 0).then_inc(x_turned, 1)
                pe.wait_ge(got[1], 16)
                pe.wait_ge(x_kept, 1)
                turn_x(pe, 1).then_inc(x_turned, 1)
                pe.wait_ge(w_in_[0], 48)
                gate_up(pe, 0, 0, bank[2]).then_inc(gu_done, 1)

                def body(e, i, par, one, two):
                    if one:
                        p1, i1 = (par + 1) % NB, i + (par + 1) // NB
                        pe.wait_ge(w_in_[p1], i1 * 48 + 48)
                        pe.wait_ge(x_kept, e + 2)
                        gate_up(pe, p1, p1 % 2, bank[2 + p1 % 2]).then_inc(gu_done, 1)
                    if two:
                        p2, i2 = (par + 2) % NB, i + (par + 2) // NB
                        pe.wait_ge(got[p2], i2 * 16 + 16)
                        turn_x(pe, p2).then_inc(x_turned, 1)
                    pe.wait_ge(hid_ready, e + 1)
                    turn_h(pe, par % 2).then_inc(ht_turned, 1)
                    pe.wait_ge(ht_kept, e + 1)
                    pe.wait_ge(y_dve, e + 1)
                    pe.wait_ge(y_act, e + 1)
                    down(pe, par).then_inc(dn_done, 1)

                turns(body)(pe)

            @block.scalar
            def _(act):
                act.drain().then_inc(y_act, 1)

                def keep_x(e, slot, wait):
                    act.wait_ge(x_turned, e + 1)
                    if wait:
                        act.wait_ge(gu_done, e - 1)
                    for h in range(2):
                        last = act.copy(xgT[:, slot, 4 * h:4 * h + 4, :], bank[h][:, :].rearrange("p (k n) -> p k n", n=P))
                    last.then_inc(x_kept, 1)

                def tanh(e, slot):
                    act.wait_ge(gu_done, e + 1)
                    act.activation(eth[:, slot, :], bank[2 + slot][:, 0:FX], ACT.Tanh, scale=0.5).then_inc(th_ready, 1)

                keep_x(0, 0, False)
                keep_x(1, 1, False)
                tanh(0, 0)

                def body(e, i, par, one, two):
                    if one:
                        tanh(e + 1, (par + 1) % 2)
                    if two:
                        keep_x(e + 2, par % 2, True)
                    act.wait_ge(ht_turned, e + 1)
                    act.copy(hidT[:, :, :], bank[4][:, 0:FX].rearrange("p (j n) -> p j n", n=P)).then_inc(ht_kept, 1)
                    act.wait_ge(dn_done, e + 1)
                    act.wait_ge(y_out[par % 2], (i * 2 + par // 2) * 16 + 16)
                    act.copy(ysb[:, par % 2, 512:D], bank[6][:, :]).then_inc(y_act, 1)
                    act.wait_ge(y_act, e + 2)
                    act.wait_ge(y_dve, e + 2)
                    act.dma_start(yd[bass.ds(e * P, P), :], ysb[:, par % 2, :]).then_inc(y_out[par % 2], 16)

                for o in y_out:
                    act.drain().then_inc(o, 16)
                turns(body)(act)
                for o in y_out:
                    act.wait_ge(o, (NX // 2 + 1) * 16)

            @block.vector
            def _(dve):
                dve.drain().then_inc(y_dve, 1)

                def hidden(e, slot):
                    dve.wait_ge(th_ready, e + 1)
                    dve.scalar_tensor_tensor(out=eh[:, :], in0=eth[:, slot, :], scalar=1.0, in1=bank[2 + slot][:, 0:FX], op0=ALU.add, op1=ALU.mult).then_inc(a_ready, 1)
                    dve.wait_ge(a_ready, e + 1)
                    dve.tensor_tensor(out=hid[:, slot, :], in0=eh[:, :], in1=bank[2 + slot][:, FX:2 * FX], op=ALU.mult).then_inc(hid_ready, 1)

                hidden(0, 0)

                def body(e, i, par, one, two):
                    if one:
                        dve.wait_ge(hid_ready, e + 1)
                        hidden(e + 1, (par + 1) % 2)
                    dve.wait_ge(dn_done, e + 1)
                    dve.wait_ge(y_out[par % 2], (i * 2 + par // 2) * 16 + 16)
                    dve.tensor_copy(ysb[:, par % 2, 0:512], bank[5][:, :]).then_inc(y_dve, 1)

                turns(body)(dve)

        (o_w, o_idx, o_int, o_x, o_xt, o_xk, o_gu, o_th, o_a, o_h, o_ht, o_hk, o_dn, o_y, o_out) = (
            sem("o_" + n) for n in ("w", "idx", "int", "x", "xt", "xk", "gu", "th", "a", "h", "ht", "hk", "dn", "y", "out"))

        def further(body):
            def run(eng):
                blocks = eng.value_load(more[0:1, NMORE:NMORE + 1], min_val=0, max_val=NMORE)
                with eng.If(blocks > 0):
                    with eng.Fori(0, blocks) as n:
                        body(eng, n, n * P + NX * P)
            return run

        with nc.Block() as block:
            def sp_body(sp, n, at):
                e = sp.value_load(more[0:1, bass.ds(n, 1)], min_val=0, max_val=NX - 1)
                one = lambda w: w[0, bass.ds(e, 1), :, :].rearrange("a d f -> (a d) f")
                sp.dma_start(wgu[:, 0, :, 0, :], V(one(w_exp_gate))).then_inc(o_w, 16)
                sp.dma_start(wgu[:, 0, :, 1, :], V(one(w_exp_up))).then_inc(o_w, 16)
                sp.dma_start(wdn[:, 0, :, :], V(one(w_exp_down))).then_inc(o_w, 16)
                sp.dma_start(idf[:, :], lists[bass.ds(at, P), :]).then_inc(o_idx, 16)
                sp.wait_ge(o_y, 2 * n + 2)
                sp.dma_start(yd[bass.ds(at, P), :], ysb[:, 0, :]).then_inc(o_out, 16)
                hold(sp, o_out, 16 * n + 16)

            def pool_body(pool, n, at):
                hold(pool, o_idx, 16 * n + 16)
                pool.tensor_copy(idxs[:, 0:1], idf[:, :]).then_inc(o_int, 1)
                hold(pool, o_int, n + 1)
                pool.indirect_dma_start(out=xg[:, 0, :], out_offset=None, in_=h2d,
                                        in_offset=bass.IndirectOffsetOnAxis(ap=idxs[:, 0:1], axis=0)).then_inc(o_x, 16)
                pool.wait_ge(o_x, 16 * n + 16)

            def pe_body(pe, n, at):
                pe.wait_ge(o_x, 16 * n + 16)
                turn_x(pe, 0).then_inc(o_xt, 1)
                pe.wait_ge(o_xk, n + 1)
                pe.wait_ge(o_w, 48 * n + 48)
                gate_up(pe, 0, 0, bank[2]).then_inc(o_gu, 1)
                pe.wait_ge(o_h, n + 1)
                turn_h(pe, 0).then_inc(o_ht, 1)
                pe.wait_ge(o_hk, n + 1)
                down(pe, 0).then_inc(o_dn, 1)

            def act_body(act, n, at):
                act.wait_ge(o_xt, n + 1)
                for h in range(2):
                    last = act.copy(xgT[:, 0, 4 * h:4 * h + 4, :], bank[h][:, :].rearrange("p (k n) -> p k n", n=P))
                last.then_inc(o_xk, 1)
                act.wait_ge(o_gu, n + 1)
                act.activation(eth[:, 0, :], bank[2][:, 0:FX], ACT.Tanh, scale=0.5).then_inc(o_th, 1)
                act.wait_ge(o_ht, n + 1)
                act.copy(hidT[:, :, :], bank[4][:, 0:FX].rearrange("p (j n) -> p j n", n=P)).then_inc(o_hk, 1)
                act.wait_ge(o_dn, n + 1)
                act.copy(ysb[:, 0, 512:D], bank[6][:, :]).then_inc(o_y, 1)
                act.wait_ge(o_y, 2 * n + 2)

            def dve_body(dve, n, at):
                dve.wait_ge(o_th, n + 1)
                dve.scalar_tensor_tensor(out=eh[:, :], in0=eth[:, 0, :], scalar=1.0, in1=bank[2][:, 0:FX], op0=ALU.add, op1=ALU.mult).then_inc(o_a, 1)
                dve.wait_ge(o_a, n + 1)
                dve.tensor_tensor(out=hid[:, 0, :], in0=eh[:, :], in1=bank[2][:, FX:2 * FX], op=ALU.mult).then_inc(o_h, 1)
                dve.wait_ge(o_dn, n + 1)
                dve.tensor_copy(ysb[:, 0, 0:512], bank[5][:, :]).then_inc(o_y, 1)
                dve.wait_ge(o_y, 2 * n + 2)

            block.sync(further(sp_body))
            block.gpsimd(further(pool_body))
            block.tensor(further(pe_body))
            block.scalar(further(act_body))
            block.vector(further(dve_body))


def combine(nc, sb, sem, half, slots, wts, yd, x1d, ada, ln2_g, ln2_b, y_prompt, y_sample):
    own = ExitStack()
    with own:
        S = lambda name, shape, dt=F32: sb(name, shape, dt, own)
        yg = S("yg", [P, NT, 2, D])
        x1 = S("x1", [P, NT, D])
        g2 = S("g2", [P, 2, D])
        lg = S("lg2", [P, D])
        lb = S("lb2", [P, D])
        bn = S("cbn", [P, NT, 2, 6])
        mv = S("cmv", [P, NT, 2])
        ve = S("cve", [P, NT])
        rs = S("crs", [P, NT])
        nb = S("cnb", [P, NT])
        got = [sem(f"c_got{t}") for t in range(NT)]
        row_in, x_in, scaled, summed, ve_ready, rs_ready, nb_ready, normed, weighed, out_ready, out_done, own_dve = (sem("c_" + n) for n in (
            "row", "x", "scaled", "summed", "ve", "rs", "nb", "normed", "weighed", "ready", "out", "dve"))
        rows = lambda ap: ap.partition_broadcast(P)
        with nc.Block() as block:
            @block.sync
            def _(sp):
                sp.dma_start(x1[:, :, :], x1d.rearrange("(t p) n -> p t n", p=P)).then_inc(x_in, 16)
                for cond in range(2):
                    sp.dma_start(g2[:, cond, :], rows(ada[cond, 5 * D:6 * D])).then_inc(row_in, 16)
                sp.dma_start(lg[:, :], rows(ln2_g[0])).then_inc(row_in, 16)
                sp.dma_start(lb[:, :], rows(ln2_b[0])).then_inc(row_in, 16)
                for t in range(NT):
                    sp.wait_ge(out_ready, t + 1)
                    to = y_prompt[0] if t == 0 else y_sample[0, (t - 1) * P:t * P, :]
                    sp.dma_start(to, x1[:, t, :]).then_inc(out_done, 16)
                sp.wait_ge(out_done, 16 * NT)

            @block.scalar
            def _(act):
                for t in range(NT):
                    act.wait_ge(got[t], 32)
                    act.activation(yg[:, t, 0, :], yg[:, t, 0, :], ACT.Copy, scale=wts[:, t, 0:1]).then_inc(scaled, 1)
                for t in range(NT):
                    act.wait_ge(nb_ready, t + 1)
                    act.activation(yg[:, t, 1, :], x1[:, t, :], ACT.Identity, bias=nb[:, t:t + 1], scale=rs[:, t:t + 1]).then_inc(normed, 1)

            @block.gpsimd
            def _(pool):
                for t in range(NT):
                    for n in range(2):
                        pool.indirect_dma_start(out=yg[:, t, n, :], out_offset=None, in_=yd,
                                                in_offset=bass.IndirectOffsetOnAxis(ap=slots[:, t, n:n + 1], axis=0)).then_inc(got[t], 16)
                for t in range(NT):
                    pool.wait_ge(ve_ready, t + 1)
                    pool.tensor_tensor(out=rs[:, t:t + 1], in0=ve[:, t:t + 1], in1=half[:, 0:1], op=ALU.pow).then_inc(rs_ready, 1)

            @block.vector
            def _(dve):
                st = Steps(dve, own_dve)
                TT, TS, STT = dve.tensor_tensor, dve.tensor_scalar, dve.scalar_tensor_tensor
                dve.wait_ge(row_in, 64)
                dve.wait_ge(x_in, 16)

                def front(t):
                    cond = min(t, 1)
                    a = yg[:, t, 0, :]
                    dve.wait_ge(scaled, t + 1)
                    st.link(STT(out=a, in0=yg[:, t, 1, :], scalar=wts[:, t, 1:2], in1=a, op0=ALU.mult, op1=ALU.add))
                    st.link(TT(out=a, in0=a, in1=g2[:, cond, :], op=ALU.mult))
                    st.link(STT(out=x1[:, t, :], in0=x1[:, t, :], scalar=ALPHA, in1=a, op0=ALU.mult, op1=ALU.add))
                    dve.bn_stats(bn[:, t, 0, :], x1[:, t, 0:512])
                    st.link(dve.bn_stats(bn[:, t, 1, :], x1[:, t, 512:D]))
                    st.link(dve.bn_aggr(mv[:, t, :], bn[:, t, :, :]))
                    TS(out=ve[:, t:t + 1], in0=mv[:, t, 1:2], scalar1=EPS, scalar2=None, op0=ALU.add).then_inc(ve_ready, 1)
                    dve.wait_ge(rs_ready, t + 1)
                    TS(out=nb[:, t:t + 1], in0=mv[:, t, 0:1], scalar1=rs[:, t:t + 1], scalar2=-1.0, op0=ALU.mult, op1=ALU.mult).then_inc(nb_ready, 1)

                def back(t):
                    a = yg[:, t, 1, :]
                    dve.wait_ge(normed, t + 1)
                    st.link(TT(out=a, in0=a, in1=lg[:, :], op=ALU.mult))
                    TT(out=x1[:, t, :], in0=a, in1=lb[:, :], op=ALU.add).then_inc(out_ready, 1)

                for t in range(NT):
                    front(t)
                    if t > 0:
                        back(t - 1)
                back(NT - 1)


_INS = ["x_prompt", "x_sample", "state_gdn", "state_ssd", "c", "c_ctx", "w_ada", "b_ada", "w_in", "gdn_conv_w",
        "gdn_conv_b", "gdn_a_log", "gdn_dt_bias", "gdn_norm_w", "w_gdn_out", "ssd_conv_w", "ssd_conv_b", "ssd_a_log",
        "ssd_dt_bias", "ssd_d", "ssd_norm_w", "w_ssd_out", "w_o", "ln1_g", "ln1_b", "w_router_group",
        "b_router_group", "w_router_expert", "b_router_expert", "w_exp_gate", "w_exp_up", "w_exp_down", "ln2_g",
        "ln2_b"]
_OUTS = [(1, SEQ, D), (1, DEC, D), (1, 1, 2, GH, P, P), (1, 1, 2, SH, SP_, SN)]


def kernel(**inputs):
    import numpy as _np
    import concourse.bacc as _bacc
    from concourse import mybir as _mybir
    from concourse.bass_utils import run_bass_kernel_spmd as _run

    nc = _bacc.Bacc("TRN2", target_bir_lowering=False, num_devices=1)
    const, levels = constants()
    data = [(name, inputs[name]) for name in _INS]
    data += [("const", const), ("small", small_constants()), ("levels", levels), ("pos", positions())]
    arrays, args = {}, []
    for name, value in data:
        a = _np.ascontiguousarray(value)
        arrays[f"in_{name}_dram"] = a
        args.append(nc.dram_tensor(f"in_{name}_dram", a.shape, _mybir.dt.from_np(a.dtype), kind="ExternalInput").ap())
    for i, shape in enumerate(_OUTS):
        args.append(nc.dram_tensor(f"out_{i}_dram", shape, F32, kind="ExternalOutput").ap())
    build(nc, *args)
    r = _run(nc, [arrays], core_ids=[0])
    return tuple(r.results[0][f"out_{i}_dram"] for i in range(len(_OUTS)))
```

```python
from contextlib import ExitStack

import numpy as np

import concourse.bass as bass
from concourse import mybir

F32 = mybir.dt.float32
I32 = mybir.dt.int32
U32 = mybir.dt.uint32
ACT = mybir.ActivationFunctionType
ALU = mybir.AluOpType
AX = mybir.AxisListType

P = 128
SEQ, DEC = 128, 512
NT = (SEQ + DEC) // P
T = NT * P
D = 1024
KD = D // P
GH = 8
SH, SP_, SG, SN = 32, 64, 4, 128
HG = SH // SG
TAPS = 5
NST = 2 * GH + 2 * SH
O_QKV, O_ZG = 0, 3 * D
O_BETA = O_ZG + D
O_A = O_BETA + 2 * GH
O_XBC = O_A + 2 * GH
O_ZS = O_XBC + SH * SP_ + 2 * SG * SN
O_DT = O_ZS + SH * SP_
O_GATE = O_DT + 2 * SH
NX = 32
XG, XE = 4, 8
FX = 256
ALPHA = 2.0 ** 0.25
EPS = 1e-6
PADW = 2 + SEQ + 2 + 2 + DEC + 2
CW = PADW - 4
LAT = SEQ + 4

(C_ID, C_LE, C_GE, C_GT, C_LT, C_ONE, C_N1F, C_N1B) = range(8)
NC_ = 8
LEVELS = 6


def constants():
    k = np.arange(P)[:, None]
    i = np.arange(P)[None, :]

    def below(s):
        return ((k // s) == (i // s) + 1) & ((i // s) % 2 == 0)

    c = [k == i, k <= i, k >= i, k > i, k < i, np.ones((P, P), bool), below(1).T, below(1)]
    c = [m.astype(np.float32) for m in c]
    c[C_N1F] = -c[C_N1F]
    c[C_N1B] = -c[C_N1B]
    levels = []
    for n in range(LEVELS):
        m = below(2 << n).astype(np.float32)
        levels += [-m, -m.T]
    return np.stack(c, 1), np.stack(levels, 1)


NMORE = (2 * T) // (P + 1)
NPLACE = (NX + NMORE) * P
(S_E, S_LIST, S_GRP, S_TOK, S_MORE, S_FAR) = (0, NX, 2 * NX, 2 * NX + XG, 2 * NX + XG + NT, 2 * NX + XG + NT + NMORE)
NCOL = S_FAR + NX


def small_constants():
    row = np.concatenate([np.arange(NX), np.arange(NX) * P, XG - np.arange(XG)])
    end = np.concatenate([np.arange(NMORE), (NX - 1 - np.arange(NX)) * P])
    tok = np.arange(P)[:, None] + P * np.arange(NT)[None, :]
    return np.concatenate([np.broadcast_to(row, (P, row.size)), tok, np.broadcast_to(end, (P, end.size))], 1).astype(np.float32)


def positions():
    n, q = DEC, D // 4
    rr = (np.arange(n) // 64).astype(np.float32)[:, None]
    cc = (np.arange(n) % 64).astype(np.float32)[:, None]
    f = np.exp((-np.log(np.float32(10000.0)) * np.arange(q, dtype=np.float32) / q).astype(np.float32)).astype(np.float32)
    return np.concatenate([np.sin(rr * f), np.cos(rr * f), np.sin(cc * f), np.cos(cc * f)], -1).astype(np.float32)



class Steps:

    def __init__(self, eng, sem, base=0, held=False):
        self.eng, self.sem, self.base, self.n, self.held = eng, sem, base, 0, held

    def add(self, ins):
        ins.then_inc(self.sem, 1)
        self.n += 1

    def wait(self, back=0):
        if self.held:
            hold(self.eng, self.sem, self.base + (self.n - back))
        else:
            self.eng.wait_ge(self.sem, self.base + (self.n - back))

    def link(self, ins):
        self.add(ins)
        self.wait()


def hold(eng, sem, value):
    value = eng.to_reg(value)
    eng.wait_ge(sem, 1)
    eng.wait_ge(sem, value)


def build(nc, x_prompt, x_sample, state_gdn, state_ssd, c, c_ctx, w_ada, b_ada, w_in, gdn_conv_w, gdn_conv_b,
          gdn_a_log, gdn_dt_bias, gdn_norm_w, w_gdn_out, ssd_conv_w, ssd_conv_b, ssd_a_log, ssd_dt_bias,
          ssd_d, ssd_norm_w, w_ssd_out, w_o, ln1_g, ln1_b, w_router_group, b_router_group,
          w_router_expert, b_router_expert, w_exp_gate, w_exp_up, w_exp_down, ln2_g, ln2_b,
          const, small, levels, pos, y_prompt, y_sample, new_gdn, new_ssd):
    top = ExitStack()
    def sb(name, shape, dt=F32, where=None):
        return (where or top).enter_context(nc.sbuf_tensor(name, shape, dt))

    before = []

    def stage(fn, *args):
        stack, taken = ExitStack(), []

        def sem(name):
            taken.append(stack.enter_context(nc.semaphore(name)))
            return taken[-1]

        fn(nc, sb, sem, *args)
        nums = sorted(one.num for one in taken)
        first = 0
        for n in range(1, len(nums) + 1):
            if n == len(nums) or nums[n] != nums[n - 1] + 1:
                nc.gpsimd.sem_clear(range(nums[first], nums[n - 1] + 1))
                first = n
        if before:
            before.pop().close()
        before.append(stack)

    sem = lambda name: top.enter_context(nc.semaphore(name))

    with top:
        bank = [top.enter_context(nc.psum_tensor(f"bank{i}", [P, 512], F32)) for i in range(8)]
        cst = sb("cst", [P, NC_, P])
        cols = sb("cols", [P, NCOL])
        half = sb("half", [P, 16])
        C = lambda n: cst[:, n, :]
        ada = nc.dram_tensor("ada", [2, 6 * D], F32, kind="Internal").ap()
        h2d = nc.dram_tensor("h2d", [T, D], F32, kind="Internal").ap()
        lists = nc.dram_tensor("lists", [NPLACE, 1], F32, kind="Internal").ap()
        yd = nc.dram_tensor("yd", [NPLACE, D], F32, kind="Internal").ap()
        mix_stack = ExitStack()
        with mix_stack:
            shared = sb("shared", [P, 6 * KD * P], F32, mix_stack)
            mT = shared[:, 0:KD * T].rearrange("p (k t) -> p k t", k=KD)
            bulk = ExitStack()
            with bulk:
                hT = sb("hT", [P, KD, T], F32, bulk)
                modT = sb("modT", [P, 2, KD, 2], F32, bulk)
                cwT = sb("cwT", [P, 2, TAPS, 24], F32, bulk)
                vecT = sb("vecT", [P, 2 * 24 + 1 + 16], F32, bulk)
                ST = sb("ST", [P, 5, NT, NST], F32, bulk)
                early = ExitStack()
                with early:
                    ws = sb("ws", [P, KD, 2 * GH + NST], F32, early)
                    bias = sb("bias", [P, NST], F32, early)
                    alog = sb("alog", [P, NST], F32, early)
                    stage(condition, bank, cst, C, cols, hT, ada, modT, cwT, vecT, half, x_prompt, x_sample, c, c_ctx, w_ada,
                              b_ada, gdn_conv_w, gdn_conv_b, gdn_norm_w, ssd_conv_w, ssd_conv_b, ssd_norm_w, const, small, pos,
                              w_in, gdn_a_log, gdn_dt_bias, ssd_a_log, ssd_dt_bias, ws, bias, alog)
                    stage(statistics, bank, cst, C, hT, ST, ws, bias, alog)
                yT = sb("yT", [P, SH * SP_ // P, T], F32, bulk)
                stage(ssd, bank, cst, C, hT, ST, cwT, vecT, half, shared, yT, w_in, ssd_d, state_ssd, new_ssd)
                oT = sb("oT", [P, KD, T], F32, bulk)
                stage(deltanet, bank, cst, C, hT, ST, cwT, vecT, half, shared, oT, levels, w_in, w_gdn_out, state_gdn, new_gdn)
                stage(merge, bank, hT, oT, yT, mT, shared, w_in, w_gdn_out, w_ssd_out)
            x1d = nc.dram_tensor("x1d", [T, D], F32, kind="Internal").ap()
            tail = ExitStack()
            with tail:
                idx = sb("idx", [P, NX], U32, tail)
                slots = sb("slots", [P, NT, 2], U32, tail)
                wts = sb("wts", [P, NT, 2], F32, tail)
                more = sb("more", [P, NMORE + 1], U32, tail)
                wgu = [sb(f"wgu{n}", [P, KD, 2, FX], F32, tail) for n in range(2)]
                wdn = [sb(f"wdn{n}", [P, FX // P, D], F32, tail) for n in range(2)]
                stage(route, bank, C, cols, half, mT, ada, pos, x_prompt, x_sample, w_o, ln1_g, ln1_b, w_router_group,
                      b_router_group, w_router_expert, b_router_expert, h2d, x1d, lists, yd, idx, slots, wts, more, wgu, wdn, w_exp_gate, w_exp_up, w_exp_down)
                x1 = sb("x1", [P, NT, D], F32, tail)
                g2 = sb("g2", [P, 2, D], F32, tail)
                lg2 = sb("lg2", [P, D], F32, tail)
                lb2 = sb("lb2", [P, D], F32, tail)
                stage(experts, bank, C, idx, more, lists, h2d, yd, w_exp_gate, w_exp_up, w_exp_down, wgu, wdn,
                      x1, g2, lg2, lb2, x1d, ada, ln2_g, ln2_b)
                stage(combine, half, slots, wts, yd, x1, g2, lg2, lb2, y_prompt, y_sample)


def condition(nc, sb, sem, bank, cst, C, cols, hT, ada, modT, cwT, vecT, half, x_prompt, x_sample, c,
              c_ctx, w_ada, b_ada, gdn_conv_w, gdn_conv_b, gdn_norm_w, ssd_conv_w, ssd_conv_b, ssd_norm_w, const, small, pos,
              w_in, gdn_a_log, gdn_dt_bias, ssd_a_log, ssd_dt_bias, ws, bias, alog):
    NCH = 6 * D // 512
    own = ExitStack()
    with own:
        S = lambda name, shape, dt=F32: sb(name, shape, dt, own)
        x = S("x", [P, NT, D])
        crow = S("crow", [2 * KD, P])
        cth = S("cth", [2 * KD, P])
        csil = S("csil", [2 * KD, P])
        cT = S("cT", [P, 2, KD])
        cwrow = S("cwrow", [TAPS * 24, 2, P])
        vrow = S("vrow", [65, P])
        NA = 3
        aw = S("aw", [P, NA, KD, 512])
        brow = S("brow", [2, 6 * D])
        arow = S("arow", [2, 6 * D])
        post = S("post", [P, NT - 1, D])
        xn = x
        bn = S("bn", [P, NT, 2, 6])
        mv = S("mv", [P, NT, 2])
        rstd = S("rstd", [P, NT])
        ve = S("ve", [P, NT])
        const_in, c_in, rows_in, b_in = sem("const_in"), sem("c_in"), sem("rows_in"), sem("b_in")
        x_in = [sem(f"x_in{t}") for t in range(NT)]
        aw_in = [sem(f"aw_in{n}") for n in range(NA)]
        c_tanh, c_silu, c_turned, c_ready = sem("c_tanh"), sem("c_silu"), sem("c_turned"), sem("c_ready")
        half_ready, stats_ready, rstd_ready = sem("half_ready"), sem("stats_ready"), sem("rstd_ready")
        ada_done, ada_kept = sem("ada_done"), sem("ada_kept")
        rows_turned, rows_kept = sem("rows_turned"), sem("rows_kept")
        NM = 2 * D // 512
        ada_out = sem("ada_out")
        mods_turned, mods_ready = sem("mods_turned"), sem("mods_ready")
        x_turned, h_dve, h_act = sem("x_turned"), sem("h_dve"), sem("h_act")
        xn_ready, ws_in = sem("xn_ready"), sem("ws_in")
        own_dve = sem("own_dve1")

        with nc.Block() as block:
            @block.sync
            def _(sp):
                sp.dma_start(crow[0:KD, :], c_ctx.rearrange("(k p) -> k p", p=P)).then_inc(c_in, 16)
                sp.dma_start(crow[KD:2 * KD, :], c.rearrange("a (k p) -> (a k) p", p=P)).then_inc(c_in, 16)
                sp.dma_start(cst[:, :, :], const).then_inc(const_in, 16)
                sp.dma_start(cols[:, :], small).then_inc(const_in, 16)

                def load(n):
                    src = w_ada[0, :, n * 512:(n + 1) * 512].rearrange("(k p) n -> p k n", p=P)
                    sp.dma_start(aw[:, n % NA, :, :], src).then_inc(aw_in[n % NA], 16)

                for n in range(NA):
                    load(n)
                for n in range(NA, NCH):
                    sp.wait_ge(ada_done, n - NA + 1)
                    load(n)
                wv = w_in[0].rearrange("(k p) n -> p k n", p=P)
                sp.dma_start(ws[:, :, 0:4 * GH], wv[:, :, O_BETA:O_BETA + 4 * GH]).then_inc(ws_in, 16)
                sp.dma_start(ws[:, :, 4 * GH:], wv[:, :, O_DT:O_DT + 2 * SH]).then_inc(ws_in, 16)
                for dst, g, s in ((bias, gdn_dt_bias, ssd_dt_bias), (alog, gdn_a_log, ssd_a_log)):
                    sp.dma_start(dst[:, 0:2 * GH], g[0].rearrange("a h -> (a h)").partition_broadcast(P)).then_inc(ws_in, 16)
                    sp.dma_start(dst[:, 2 * GH:NST], s[0].rearrange("a h -> (a h)").partition_broadcast(P)).then_inc(ws_in, 16)
                sp.wait_ge(ada_out, 16)
                sp.wait_ge(ws_in, 96)

            @block.scalar
            def _(act):
                act.dma_start(cwrow[:, 0, :], gdn_conv_w[0].rearrange("k (n p) -> (k n) p", p=P)).then_inc(rows_in, 16)
                act.dma_start(cwrow[:, 1, :], ssd_conv_w[0].rearrange("k (n p) -> (k n) p", p=P)).then_inc(rows_in, 16)
                act.dma_start(vrow[0:24, :], gdn_conv_b[0].rearrange("(n p) -> n p", p=P)).then_inc(rows_in, 16)
                act.dma_start(vrow[24:48, :], ssd_conv_b[0].rearrange("(n p) -> n p", p=P)).then_inc(rows_in, 16)
                act.dma_start(vrow[48:49, :], gdn_norm_w).then_inc(rows_in, 16)
                act.dma_start(vrow[49:65, :], ssd_norm_w[0].rearrange("(n p) -> n p", p=P)).then_inc(rows_in, 16)
                act.dma_start(brow[:, :], b_ada[0, :].partition_broadcast(2)).then_inc(b_in, 16)
                act.wait_ge(c_in, 32)
                act.activation(cth[:, :], crow[:, :], ACT.Tanh, scale=0.5).then_inc(c_tanh, 1)
                act.dma_start(x[:, 0, :], x_prompt[0]).then_inc(x_in[0], 16)
                for t in range(1, NT):
                    act.dma_start(post[:, t - 1, :], pos[(t - 1) * P:t * P, :]).then_inc(x_in[t], 16)
                    act.dma_start(x[:, t, :], x_sample[0, (t - 1) * P:t * P, :]).then_inc(x_in[t], 16)
                act.wait_ge(mods_ready, 1)
                for t in range(NT):
                    cond = min(t, 1)
                    act.wait_ge(x_turned, 2 * t + 2)
                    for k in range(4, 8):
                        last = act.activation(hT[:, k, t * P:(t + 1) * P], bank[4 + (2 * t + 1) % 4][:, (k - 4) * P:(k - 3) * P],
                                              ACT.Identity, bias=modT[:, 0, k, cond:cond + 1],
                                              scale=modT[:, 1, k, cond:cond + 1])
                    last.then_inc(h_act, 1)
                act.wait_ge(ada_kept, NCH)
                act.dma_start(ada, arow[:, :]).then_inc(ada_out, 16)

            @block.gpsimd
            def _(pool):
                nc.gpsimd.memset(half[:, :], -0.5).then_inc(half_ready, 1)
                pool.wait_ge(half_ready, 1)
                for t in range(NT):
                    pool.wait_ge(stats_ready, t + 1)
                    pool.tensor_tensor(out=rstd[:, t:t + 1], in0=ve[:, t:t + 1], in1=half[:, 0:1],
                                       op=ALU.pow).then_inc(rstd_ready, 1)

            @block.vector
            def _(dve):
                st = Steps(dve, own_dve)
                dve.wait_ge(c_tanh, 1)
                st.link(dve.scalar_tensor_tensor(out=csil[:, :], in0=cth[:, :], scalar=1.0, in1=crow[:, :],
                                                 op0=ALU.add, op1=ALU.mult))
                dve.tensor_scalar(out=csil[:, :], in0=csil[:, :], scalar1=0.5, scalar2=None, op0=ALU.mult).then_inc(c_silu, 1)
                dve.wait_ge(c_turned, 1)
                dve.tensor_copy(cT[:, :, :], bank[0][:, 0:2 * KD].rearrange("p (a k) -> p a k", a=2)).then_inc(c_ready, 1)
                dve.wait_ge(rows_turned, 1)
                dve.tensor_copy(cwT[:, :, :, :], bank[1][:, 0:240].rearrange("p (a k n) -> p a k n", a=2, k=TAPS))
                dve.tensor_copy(vecT[:, :], bank[1][:, 256:256 + 65]).then_inc(rows_kept, 1)
                dve.wait_ge(b_in, 16)

                def keep(n):
                    dve.wait_ge(ada_done, n + 1)
                    dve.tensor_tensor(out=arow[:, n * 512:(n + 1) * 512], in0=bank[2 + n % 2][0:2, :],
                                      in1=brow[:, n * 512:(n + 1) * 512], op=ALU.add).then_inc(ada_kept, 1)

                def norm(t):
                    dve.wait_ge(x_in[t], 32 if t > 0 else 16)
                    if t > 0:
                        st.link(dve.tensor_tensor(out=x[:, t, :], in0=x[:, t, :], in1=post[:, t - 1, :], op=ALU.add))
                    dve.bn_stats(bn[:, t, 0, :], x[:, t, 0:512])
                    st.link(dve.bn_stats(bn[:, t, 1, :], x[:, t, 512:1024]))
                    st.link(dve.bn_aggr(mv[:, t, :], bn[:, t, :, :]))
                    dve.tensor_scalar(out=ve[:, t:t + 1], in0=mv[:, t, 1:2], scalar1=EPS, scalar2=None,
                                      op0=ALU.add).then_inc(stats_ready, 1)
                    dve.wait_ge(rstd_ready, t + 1)
                    dve.tensor_scalar(out=xn[:, t, :], in0=x[:, t, :], scalar1=mv[:, t, 0:1], scalar2=rstd[:, t:t + 1],
                                      op0=ALU.subtract, op1=ALU.mult).then_inc(xn_ready, 1)

                def modulate(t):
                    cond = min(t, 1)
                    dve.wait_ge(x_turned, 2 * t + 1)
                    for k in range(4):
                        last = dve.tensor_scalar(out=hT[:, k, t * P:(t + 1) * P], in0=bank[4 + 2 * t % 4][:, k * P:(k + 1) * P],
                                                 scalar1=modT[:, 1, k, cond:cond + 1], scalar2=modT[:, 0, k, cond:cond + 1],
                                                 op0=ALU.mult, op1=ALU.add)
                    last.then_inc(h_dve, 1)

                for n in range(NM):
                    keep(n)
                    if n < NM - 1:
                        norm(n)
                dve.wait_ge(mods_turned, 1)
                for m in range(2):
                    last = dve.tensor_scalar(out=modT[:, m, :, :], in0=bank[0][:, m * 16:(m + 1) * 16],
                                             scalar1=float(m % 2), scalar2=None, op0=ALU.add)
                last.then_inc(mods_ready, 1)
                dve.wait_ge(mods_ready, 1)
                for n in range(NM, NCH):
                    keep(n)
                    t = n - NM
                    if t < NT:
                        modulate(t)
                    if t + NM - 1 < NT:
                        norm(t + NM - 1)

            @block.tensor
            def _(pe):
                pe.wait_ge(const_in, 32)
                pe.wait_ge(c_silu, 1)
                pe.transpose(bank[0][:, 0:2 * KD], csil[:, :], cst[0:2 * KD, C_ID, 0:2 * KD]).then_inc(c_turned, 1)
                pe.wait_ge(rows_in, 96)
                for a in range(2):
                    pe.transpose(bank[1][:, a * 120:(a + 1) * 120], cwrow[:, a, :], cst[0:120, C_ID, 0:120])
                pe.transpose(bank[1][:, 256:256 + 65], vrow[:, :], cst[0:65, C_ID, 0:65]).then_inc(rows_turned, 1)
                pe.wait_ge(c_ready, 1)

                def chunk(n):
                    pe.wait_ge(aw_in[n % NA], 16 * (n // NA + 1))
                    if n >= 2:
                        pe.wait_ge(ada_kept, n - 1)
                    for k in range(KD):
                        last = pe.matmul(bank[2 + n % 2][0:2, :], cT[:, :, k], aw[:, n % NA, k, :], start=(k == 0), stop=(k == KD - 1))
                    last.then_inc(ada_done, 1)

                for n in range(NM):
                    chunk(n)
                for n in range(NM, NCH):
                    chunk(n)
                    if n == NM:
                        pe.wait_ge(ada_kept, NM)
                        pe.wait_ge(rows_kept, 1)
                        for m, at in enumerate((0, 1)):
                            for k in range(KD):
                                last = pe.transpose(bank[0][:, m * 16 + 2 * k:m * 16 + 2 * k + 2],
                                                    arow[:, at * D + k * P:at * D + (k + 1) * P], cst[0:2, C_ID, 0:2])
                        last.then_inc(mods_turned, 1)
                    t = n - NM
                    if t < NT:
                        pe.wait_ge(xn_ready, t + 1)
                        for h in range(2):
                            if t >= 2:
                                pe.wait_ge((h_dve, h_act)[h], t - 1)
                            for k in range(4):
                                last = pe.transpose(bank[4 + (2 * t + h) % 4][:, k * P:(k + 1) * P],
                                                    xn[:, t, (4 * h + k) * P:(4 * h + k + 1) * P], C(C_ID))
                            last.then_inc(x_turned, 1)


def statistics(nc, sb, sem, bank, cst, C, hT, ST, ws, bias, alog):
    own = ExitStack()
    with own:
        S = lambda name, shape, dt=F32: sb(name, shape, dt, own)
        NS = 2 * GH + NST
        aexp = S("aexp", [P, NST])
        raw = S("raw", [P, NT, NS])
        z = S("z", [P, NT, NST])
        m = S("m", [P, NT, NST])
        e = S("e", [P, NT, NST])
        u = S("u", [P, NT, NST])
        d = S("d", [P, NT, NST])
        isz = S("isz", [P, NT, NST])
        lu = S("lu", [P, NT, NST])
        eb = S("eb", [P, NT, 2 * GH])
        raw_done, aexp_ready, neg_ready, exp_ready, u_ready, ln_ready = (sem(n) for n in (
            "raw_done", "aexp_ready", "neg_ready", "exp_ready", "u_ready", "ln_ready"))
        beta_exp, raw_kept, g_ready, sums_done, sums_kept = (sem(n) for n in (
            "beta_exp", "raw_kept", "g_ready", "sums_done", "sums_kept"))
        own_dve = sem("own_dve2")
        flat = lambda t: t[:, :, :].rearrange("p t n -> p (t n)")
        with nc.Block() as block:
            @block.tensor
            def _(pe):
                for t in range(NT):
                    for k in range(KD):
                        last = pe.matmul(bank[t][:, 0:NS], hT[:, k, t * P:(t + 1) * P], ws[:, k, :], start=(k == 0), stop=(k == KD - 1))
                    last.then_inc(raw_done, 1)
                pe.wait_ge(raw_kept, 1)
                pe.wait_ge(g_ready, 1)
                for n, mask in enumerate((C_LE, C_GE, C_GT, C_LT, C_ONE)):
                    pe.matmul(bank[n][:, 0:NT * NST], C(mask), ST[:, 0, :, :].rearrange("p t n -> p (t n)"),
                              start=True, stop=True).then_inc(sums_done, 1)

            @block.scalar
            def _(act):
                act.activation(aexp[:, :], alog[:, :], ACT.Exp).then_inc(aexp_ready, 1)
                act.wait_ge(raw_kept, 1)
                act.activation(eb[:, :, :], raw[:, :, 0:2 * GH], ACT.Exp, scale=-1.0).then_inc(beta_exp, 1)
                act.wait_ge(neg_ready, 1)
                act.activation(flat(e), flat(m), ACT.Exp).then_inc(exp_ready, 1)
                act.wait_ge(u_ready, 1)
                act.activation(flat(lu), flat(u), ACT.Ln).then_inc(ln_ready, 1)
                for n in range(5):
                    act.wait_ge(sums_done, n + 1)
                    sums = bank[n][:, 0:NT * NST].rearrange("p (t n) -> p t n", n=NST)
                    if n == 4:
                        act.activation(ST[:, 3, :, :], sums, ACT.Exp)
                        continue
                    kind, dr = 1 + n // 2, n % 2
                    for at, w in ((dr * GH, GH), (2 * GH + dr * SH, SH)):
                        act.activation(ST[:, kind, :, at:at + w], sums[:, :, at:at + w], ACT.Exp)

            @block.vector
            def _(dve):
                st = Steps(dve, own_dve)
                TT, TS = dve.tensor_tensor, dve.tensor_scalar
                for t in range(NT):
                    dve.wait_ge(raw_done, t + 1)
                    last = dve.tensor_copy(raw[:, t, :], bank[t][:, 0:NS])
                last.then_inc(raw_kept, 1)
                dve.wait_ge(raw_kept, 1)
                st.link(TT(out=z[:, :, :], in0=raw[:, :, 2 * GH:NS], in1=bias[:, :].unsqueeze(1).broadcast_to([P, NT, NST]), op=ALU.add))
                st.link(TS(out=flat(m), in0=flat(z), scalar1=-1.0, scalar2=None, op0=ALU.mult))
                TT(out=flat(m), in0=flat(m), in1=flat(z), op=ALU.min).then_inc(neg_ready, 1)
                dve.wait_ge(beta_exp, 1)
                st.link(TS(out=eb[:, :, :], in0=eb[:, :, :], scalar1=1.0, scalar2=None, op0=ALU.add))
                dve.reciprocal(ST[:, 4, :, 0:2 * GH], eb[:, :, :])
                dve.wait_ge(exp_ready, 1)
                TS(out=flat(u), in0=flat(e), scalar1=1.0, scalar2=None, op0=ALU.add).then_inc(u_ready, 1)
                dve.wait_ge(u_ready, 1)
                st.link(TS(out=flat(d), in0=flat(u), scalar1=-1.0, scalar2=None, op0=ALU.add))
                st.link(TS(out=flat(isz), in0=flat(d), scalar1=0.0, scalar2=None, op0=ALU.is_equal))
                st.link(TT(out=flat(d), in0=flat(d), in1=flat(isz), op=ALU.add))
                st.link(dve.reciprocal(flat(d), flat(d)))
                st.link(TT(out=flat(d), in0=flat(d), in1=flat(e), op=ALU.mult))
                dve.wait_ge(ln_ready, 1)
                st.link(TT(out=flat(d), in0=flat(d), in1=flat(lu), op=ALU.mult))
                st.link(TT(out=flat(isz), in0=flat(isz), in1=flat(e), op=ALU.mult))
                st.link(TT(out=flat(d), in0=flat(d), in1=flat(isz), op=ALU.add))
                st.link(dve.scalar_tensor_tensor(out=flat(z), in0=flat(z), scalar=0.0, in1=flat(d), op0=ALU.max, op1=ALU.add))
                dve.tensor_copy(ST[:, 4, :, 2 * GH:NST], z[:, :, 2 * GH:NST])
                dve.wait_ge(aexp_ready, 1)
                dve.scalar_tensor_tensor(out=ST[:, 0, :, :], in0=z[:, :, :], scalar=-1.0,
                                         in1=aexp[:, :].unsqueeze(1).broadcast_to([P, NT, NST]),
                                         op0=ALU.mult, op1=ALU.mult).then_inc(g_ready, 1)


def deltanet(nc, sb, sem, bank, cst, C, hT, ST, cwT, vecT, half, shared, oT, levels, w_in, w_gdn_out, state_gdn, new_gdn):
    own = ExitStack()
    with own:
        S = lambda name, shape, dt=F32: sb(name, shape, dt, own)
        NU = 2 * NT
        FW, BW = 0, 1
        negm = S("negm", [P, LEVELS, 2, P])
        w4 = shared[:, 0:4 * KD * P].rearrange("p (c k n) -> p c k n", c=4, k=KD)
        cw = S("cw", [P, TAPS, 3])
        cb = S("cb", [P, 3])
        cur = S("cur", [P, 5, NT, 2])
        padded = S("padded", [P, 3, PADW])
        conv = S("conv", [P, 3, CW])
        th = S("th", [P, 3, CW])
        zth = S("zth", [P, T])
        zg = S("zg", [P, T])
        vT = S("vT", [P, NT, P])
        kraw = S("kraw", [P, NT, P])
        kq = shared[:, 4 * KD * P:4 * KD * P + 2 * T].rearrange("p (t a n) -> p t a n", t=NT, a=2)
        sq = S("sq", [P, 2, NT, P])
        ssum = S("ssum", [P, 2, NT])
        rn = S("rn", [P, 2, NT])
        kn = shared[:, 4 * KD * P + 2 * T:4 * KD * P + 3 * T].rearrange("p (t n) -> p t n", t=NT)
        vt = S("vt", [P, NT, P])
        gm = S("gm", [P, 2, NT, P])
        bm = S("bm", [P, 2, NT, P])
        dec = S("dec", [P, 2, NT, P])
        di = S("di", [P, 2, NT, P])
        att = S("att", [P, 2, NT, P])
        MT = S("MT", [P, NU, P])
        D_ = S("D_", [P, NU, P])
        DT = S("DT", [P, NU, P])
        convf = conv[:, :, :].rearrange("p c n -> p (c n)")
        thf = th[:, :, :].rearrange("p c n -> p (c n)")
        X = convf[:, 0:NU * P].rearrange("p (u n) -> p u n", n=P)
        state = S("state", [P, 2, 2, P])
        neg = S("neg", [P, NT, 2])
        ber = S("ber", [P, NT, 2])
        pair = lambda ap: ap.rearrange("p (d n) -> p d n", d=2)
        R = pair(convf[:, NU * P:(NU + 2) * P])
        vn = pair(convf[:, (NU + 2) * P:(NU + 4) * P])
        vd = pair(zth[:, 0:2 * P])
        qs = pair(zth[:, 2 * P:4 * P])
        osum, osq, on = (thf[:, n * T:(n + 1) * T].rearrange("p (t n) -> p t n", n=P) for n in range(3))
        oss = S("oss", [P, NT])
        osc = S("osc", [P, NT])
        unit = lambda d, t: 4 * d + t if t < 4 else 8 + d
        GROUPS = [(0, 4), (4, 4), (8, 2)]
        XB = (0, 3, 6)
        DTB = (1, 4, 7)
        DB = (2, 5, 6)
        dtv = lambda g, n: bank[DTB[g]][:, 0:n * P]
        dv = lambda g, n: bank[DB[g]][:, 256 * (g == 2):256 * (g == 2) + n * P]
        CHAIN = [(0, 0)] + [(1 + s, 4 - s) for s in range(4)]

        names = ("gl_in", "gw_in", "gs_in", "gs_out", "g_proj", "g_raw", "g_conv", "g_tanh", "g_ztanh", "g_silu", "g_sq", "g_sums",
                 "g_kturn", "g_vturn", "g_ssum", "g_rn", "g_kn", "g_v", "g_knturn", "g_knT", "g_cur", "g_gm", "g_seg",
                 "g_dec", "g_KQ", "g_M", "g_D2", "g_init", "g_Dkept", "g_X", "g_Xkept", "g_DT", "g_DTkept", "g_KS", "g_QS",
                 "g_R", "g_qs", "g_vnew", "g_vn", "g_vd", "g_O", "g_SU", "g_state", "g_osum", "g_oz", "g_oss", "g_osc",
                 "g_on", "g_oturn", "g_head", "g_dve", "g_zg", "g_pad", "g_pool", "g_qsadd", "g_KQkept", "g_Dturn", "g_gates")
        s = {n: sem(n) for n in names}
        DVE_STEPS, POOL_STEPS = 36, 8

        with nc.Block() as block:
            @block.sync
            def _(sp):
                sp.dma_start(negm[:, :, :, :], levels.rearrange("p (l a) n -> p l a n", a=2)).then_inc(s["gl_in"], 16)
                def load(h):
                    for n, at in enumerate((O_QKV, O_QKV + D, O_QKV + 2 * D, O_ZG)):
                        src = w_in[0, :, bass.ds(h * P + at, P)].rearrange("(k p) n -> p k n", p=P)
                        sp.dma_start(w4[:, n, :, :], src).then_inc(s["gw_in"], 16)

                def body(h, more):
                    sp.wait_ge(s["g_head"], h + 1)
                    for d in range(2):
                        sp.dma_start(state[:, 1, d, :], state_gdn[0, 0, d, bass.ds(h, 1), :, :].rearrange("a k v -> k (a v)")).then_inc(s["gs_in"], 16)
                    if more:
                        sp.wait_ge(s["g_proj"], 4 * h + 4)
                        load(h + 1)
                    else:
                        sp.wait_ge(s["g_proj"], 4 * h + 4)
                        for n, src in enumerate((w_in[0, :, O_GATE:O_GATE + P], w_in[0, :, O_GATE + D:O_GATE + D + P], w_gdn_out[0, :, 0:P])):
                            sp.dma_start(w4[:, 1 + n, :, :], src.rearrange("(k p) n -> p k n", p=P)).then_inc(s["g_gates"], 16)
                    sp.wait_ge(s["g_state"], 10 * h + 2)
                    for d in range(2):
                        sp.dma_start(new_gdn[0, 0, d, bass.ds(h, 1), :, :].rearrange("a k v -> k (a v)"), state[:, 0, d, :]).then_inc(s["gs_out"], 16)

                with sp.Fori(0, GH - 1) as h:
                    body(h, True)
                body(GH - 1, False)
                sp.wait_ge(s["g_gates"], 48)
                sp.wait_ge(s["gs_out"], 32 * GH)

            @block.tensor
            def _(pe):
                OUT = ((7, 6, P), (0, 1, 0), (4, 3, 0), (6, 7, 0))

                def proj(n, parts):
                    a, b, at = OUT[n]
                    for m in parts:
                        k = m % KD
                        if m < KD:
                            last = pe.matmul(bank[a][:, :], w4[:, n, k, :], hT[:, k, SEQ:T], start=(k == 0), stop=(k == KD - 1), skip_group_check=True)
                        else:
                            last = pe.matmul(bank[b][:, at:at + P], w4[:, n, k, :], hT[:, k, 0:SEQ], start=(k == 0), stop=(k == KD - 1), skip_group_check=True)
                    if 2 * KD - 1 in parts:
                        last.then_inc(s["g_proj"], 1)

                ALL = range(2 * KD)

                def blocks_X(h, l, g):
                    u0, n = GROUPS[g]
                    pe.wait_ge(s["g_Dkept"], 18 * h + 3 * l + g + 1)
                    for u in range(n):
                        last = pe.matmul(bank[XB[g]][:, u * P:(u + 1) * P], MT[:, u0 + u, :], D_[:, u0 + u, :], start=True, stop=True)
                    last.then_inc(s["g_X"], 1)

                def blocks_DT(h, l, g):
                    u0, n = GROUPS[g]
                    pe.wait_ge(s["g_Xkept"], 18 * h + 3 * l + g + 1)
                    for u in range(n):
                        last = pe.matmul(dtv(g, n)[:, u * P:(u + 1) * P], X[:, u0 + u, :], DT[:, u0 + u, :], start=False, stop=(l == LEVELS - 1), skip_group_check=True)
                    last.then_inc(s["g_DT"], 1)

                def turn_D(h, g, l):
                    u0, n = GROUPS[g]
                    if l is not None:
                        pe.wait_ge(s["g_DTkept"], 18 * h + 3 * l + g + 1)
                    for u in range(n):
                        last = pe.transpose(dv(g, n)[:, u * P:(u + 1) * P], DT[:, u0 + u, :], C(C_ID))
                    last.then_inc(s["g_Dturn"], 1)

                def body(h, more):
                    proj(2, range(KD))
                    pe.wait_ge(s["g_head"], h + 1)
                    proj(2, range(KD, 2 * KD))
                    pe.wait_ge(s["g_raw"], 3 * h + 1)
                    proj(3, range(KD - 2))
                    pe.wait_ge(s["g_silu"], 3 * h + 2)
                    for t in range(NT):
                        last = pe.transpose(bank[1 + t // 4][:, t % 4 * P:t % 4 * P + P], kraw[:, t, :], C(C_ID))
                    last.then_inc(s["g_kturn"], 1)
                    pe.wait_ge(s["g_sq"], 2 * h + 2)
                    for n in range(2):
                        for t in range(NT):
                            last = pe.matmul(bank[0][:, n * NT + t:n * NT + t + 1], sq[:, n, t, :], cst[:, C_ONE, 0:1], start=True, stop=True)
                    last.then_inc(s["g_sums"], 1)
                    proj(3, range(KD - 2, 2 * KD))
                    pe.wait_ge(s["g_silu"], 3 * h + 3)
                    for t in range(NT):
                        last = pe.transpose(bank[3 + t // 4][:, t % 4 * P:t % 4 * P + P], vT[:, t, :], C(C_ID))
                    last.then_inc(s["g_vturn"], 1)
                    pe.wait_ge(s["g_zg"], h + 1)
                    pe.wait_ge(s["g_gm"], 2 * h + 1)
                    pe.matmul(bank[6][:, :], C(C_GT), gm[:, FW, 0:4, :].rearrange("p t n -> p (t n)"), start=True, stop=True)
                    pe.matmul(bank[7][:, 0:P], C(C_GT), gm[:, FW, 4, :], start=True, stop=True).then_inc(s["g_seg"], 1)
                    pe.wait_ge(s["g_kn"], h + 1)
                    for t in range(NT):
                        last = pe.transpose(bank[5 if t < 4 else 0][:, t % 4 * P:t % 4 * P + P], kn[:, t, :], C(C_ID))
                    last.then_inc(s["g_knturn"], 1)
                    pe.wait_ge(s["g_knT"], h + 1)
                    pe.wait_ge(s["g_v"], h + 1)
                    pe.wait_ge(s["g_gm"], 2 * h + 2)
                    pe.matmul(bank[4][:, :], C(C_LT), gm[:, BW, 0:4, :].rearrange("p t n -> p (t n)"), start=True, stop=True)
                    pe.matmul(bank[5][:, 0:P], C(C_LT), gm[:, BW, 4, :], start=True, stop=True).then_inc(s["g_seg"], 1)
                    for t in range(NT):
                        last = pe.matmul(bank[1 + t // 2][:, t % 2 * 256:t % 2 * 256 + 256], kq[:, t, 0, :],
                                         kq[:, t, :, :].rearrange("p a n -> p (a n)"), start=True, stop=True)
                    last.then_inc(s["g_KQ"], 1)
                    pe.wait_ge(s["g_dec"], 2 * h + 2)
                    for g, (u0, n) in enumerate(GROUPS):
                        pe.wait_ge(s["g_D2"], 3 * h + g + 1)
                        pe.matmul(dtv(g, n), C(C_ID), DT[:, u0:u0 + n, :].rearrange("p u n -> p (u n)"), start=True, stop=False, skip_group_check=True)
                        turn_D(h, g, None)
                    for g in range(3):
                        blocks_X(h, 0, g)
                    for l in range(LEVELS):
                        blocks_DT(h, l, 0)
                        blocks_DT(h, l, 1)
                        if l < LEVELS - 1:
                            turn_D(h, 0, l)
                        blocks_DT(h, l, 2)
                        if l < LEVELS - 1:
                            turn_D(h, 1, l)
                            blocks_X(h, l + 1, 0)
                            turn_D(h, 2, l)
                            blocks_X(h, l + 1, 1)
                            blocks_X(h, l + 1, 2)
                    pe.wait_ge(s["gs_in"], 32 * h + 32)
                    for p, tiles in enumerate(CHAIN):
                        q = int(p > 0)
                        if p > 0:
                            if p == 1:
                                pe.wait_ge(s["g_Dkept"], 18 * h + 18)
                            pe.wait_ge(s["g_state"], 10 * h + 2 * p)
                            for d, t in enumerate(tiles):
                                last = pe.matmul(bank[0][:, d * P:(d + 1) * P], kq[:, t, 0, :], state[:, q, d, :], start=True, stop=True)
                            last.then_inc(s["g_KS"], 1)
                            if p > 1:
                                pe.wait_ge(s["g_qs"], 4 * h + p - 1)
                            for d, t in enumerate(tiles):
                                last = pe.matmul(bank[1][:, d * P:(d + 1) * P], kq[:, t, 1, :], state[:, q, d, :], start=True, stop=True)
                            last.then_inc(s["g_QS"], 1)
                        else:
                            pe.wait_ge(s["g_DTkept"], 18 * h + 18)
                            if more:
                                pe.wait_ge(s["gw_in"], 64 * h + 64)
                        if more and p < 4:
                            proj(0, [2 * p])
                        pe.wait_ge(s["g_R"], 5 * h + p + 1)
                        for d, t in enumerate(tiles):
                            last = pe.matmul(bank[2][:, d * P:(d + 1) * P], DT[:, unit(d, t), :], R[:, d, :], start=True, stop=True)
                        last.then_inc(s["g_vnew"], 1)
                        if more and p < 4:
                            proj(0, [2 * p + 1])
                        pe.wait_ge(s["g_vd"], 5 * h + p + 1)
                        for d, t in enumerate(tiles):
                            last = pe.matmul(bank[4][:, d * P:(d + 1) * P], kn[:, t, :], vd[:, d, :], start=True, stop=True)
                        last.then_inc(s["g_SU"], 1)
                        if more and p < 4:
                            proj(0, [KD + 2 * p, KD + 2 * p + 1])
                        pe.wait_ge(s["g_vn"], 5 * h + p + 1)
                        if p > 0:
                            pe.wait_ge(s["g_osum"], 5 * h + p)
                        for d, t in enumerate(tiles):
                            last = pe.matmul(bank[3][:, d * P:(d + 1) * P], att[:, d, t, :], vn[:, d, :], start=True, stop=True)
                        last.then_inc(s["g_O"], 1)
                    if more:
                        proj(1, range(KD - 1))
                    pe.wait_ge(s["g_on"], h + 1)
                    for t in range(NT):
                        last = pe.transpose(bank[5 if t < 4 else 3][:, t % 4 * P:t % 4 * P + P], on[:, t, :], C(C_ID))
                    last.then_inc(s["g_oturn"], 1)
                    if more:
                        pe.wait_ge(s["g_qs"], 4 * h + 4)
                        proj(1, range(KD - 1, 2 * KD))

                pe.wait_ge(s["gl_in"], 16)
                proj(0, ALL)
                proj(1, ALL)
                with pe.Fori(0, GH - 1) as h:
                    body(h, True)
                body(GH - 1, False)

            @block.scalar
            def _(act):
                with act.Fori(0, GH) as h:
                    for n in range(3):
                        act.wait_ge(s["g_proj"], 4 * h + n + 1)
                        if n == 0:
                            act.wait_ge(s["g_pad"], 1)
                        lat, ctx, at = ((7, 6, P), (0, 1, 0), (4, 3, 0))[n]
                        act.copy(padded[:, n, 2:2 + SEQ], bank[ctx][:, at:at + SEQ])
                        act.copy(padded[:, n, 6 + SEQ:6 + T], bank[lat][:, :]).then_inc(s["g_raw"], 1)
                        if n > 0:
                            act.wait_ge(s["g_conv"], 3 * h + n)
                            act.activation(th[:, n - 1, :], conv[:, n - 1, :], ACT.Tanh, scale=0.5).then_inc(s["g_tanh"], 1)
                    act.wait_ge(s["g_conv"], 3 * h + 3)
                    act.activation(th[:, 2, :], conv[:, 2, :], ACT.Tanh, scale=0.5).then_inc(s["g_tanh"], 1)
                    for n in range(2):
                        act.wait_ge(s["g_silu"], 3 * h + n + 1)
                        act.activation(sq[:, n, :, :], kq[:, :, 1, :] if n == 0 else kraw[:, :, :], ACT.Square, scale=0.5).then_inc(s["g_sq"], 1)
                    act.wait_ge(s["g_proj"], 4 * h + 4)
                    act.activation(zth[:, 0:SEQ], bank[7][:, 0:SEQ], ACT.Tanh, scale=0.5)
                    act.activation(zth[:, SEQ:T], bank[6][:, :], ACT.Tanh, scale=0.5).then_inc(s["g_ztanh"], 1)
                    act.wait_ge(s["g_vturn"], h + 1)
                    act.mul(vt[:, 0:4, :], bank[3][:, :].rearrange("p (t n) -> p t n", n=P), 0.5)
                    act.mul(vt[:, 4, :], bank[4][:, 0:P], 0.5).then_inc(s["g_v"], 1)
                    act.wait_ge(s["g_seg"], 2 * h + 1)
                    act.activation(dec[:, FW, 0:4, :], bank[6][:, :].rearrange("p (t n) -> p t n", n=P), ACT.Exp)
                    act.activation(dec[:, FW, 4, :], bank[7][:, 0:P], ACT.Exp).then_inc(s["g_dec"], 1)
                    act.wait_ge(s["g_knturn"], h + 1)
                    act.copy(kq[:, 0:4, 0, :], bank[5][:, :].rearrange("p (t n) -> p t n", n=P))
                    act.copy(kq[:, 4, 0, :], bank[0][:, 0:P]).then_inc(s["g_knT"], 1)
                    act.wait_ge(s["g_seg"], 2 * h + 2)
                    act.activation(dec[:, BW, 0:4, :], bank[4][:, :].rearrange("p (t n) -> p t n", n=P), ACT.Exp)
                    act.activation(dec[:, BW, 4, :], bank[5][:, 0:P], ACT.Exp).then_inc(s["g_dec"], 1)
                    def keep_D(turn, g):
                        u0, n = GROUPS[g]
                        act.wait_ge(s["g_Dturn"], 18 * h + turn + 1)
                        act.copy(D_[:, u0:u0 + n, :], dv(g, n).rearrange("p (u n) -> p u n", n=P)).then_inc(s["g_Dkept"], 1)

                    def keep_DT(l, g):
                        u0, n = GROUPS[g]
                        act.wait_ge(s["g_DT"], 18 * h + 3 * l + g + 1)
                        act.copy(DT[:, u0:u0 + n, :], dtv(g, n).rearrange("p (u n) -> p u n", n=P)).then_inc(s["g_DTkept"], 1)

                    act.wait_ge(s["g_KQ"], h + 1)
                    for b, (t0, n) in enumerate(((0, 2), (2, 2), (4, 1))):
                        last = act.copy(att[:, BW, t0:t0 + n, :], bank[1 + b][:, 0:n * 256].rearrange("p (t a n) -> p t a n", a=2, n=P)[:, :, 1, :])
                    last.then_inc(s["g_KQkept"], 1)
                    for g in range(3):
                        keep_D(g, g)
                    for l in range(LEVELS):
                        keep_DT(l, 0)
                        keep_DT(l, 1)
                        if l < LEVELS - 1:
                            keep_D(3 * l + 3, 0)
                        keep_DT(l, 2)
                        if l < LEVELS - 1:
                            keep_D(3 * l + 4, 1)
                            keep_D(3 * l + 5, 2)
                    for p, tiles in enumerate(CHAIN):
                        if p > 0:
                            act.wait_ge(s["g_QS"], 4 * h + p)
                            if p > 1:
                                act.wait_ge(s["g_qsadd"], 4 * h + p - 1)
                            for d, t in enumerate(tiles):
                                last = act.activation(qs[:, d, :], bank[1][:, d * P:(d + 1) * P], ACT.Copy, scale=cur[:, 1, t, d:d + 1])
                            last.then_inc(s["g_qs"], 1)
                        act.wait_ge(s["g_vd"], 5 * h + p + 1)
                        if p > 0:
                            act.wait_ge(s["g_O"], 5 * h + p)
                        for d, t in enumerate(tiles):
                            last = act.activation(vn[:, d, :], bank[2][:, d * P:(d + 1) * P], ACT.Copy, scale=cur[:, 4, t, d:d + 1])
                        last.then_inc(s["g_vn"], 1)
                    act.wait_ge(s["g_osum"], 5 * h + 5)
                    for t in range(NT):
                        last = act.activation(osq[:, t, :], osum[:, t, :], ACT.Square, accum_out=oss[:, t:t + 1])
                    last.then_inc(s["g_oss"], 1)

            @block.gpsimd
            def _(pool):
                pool.memset(padded[:, :, :], 0.0).then_inc(s["g_pad"], 1)
                with pool.Fori(0, GH) as h:
                    st = Steps(pool, s["g_pool"], h * POOL_STEPS, held=True)
                    TT = pool.tensor_tensor
                    pool.wait_ge(s["g_cur"], h + 1)
                    for d, mask in ((FW, C_LE), (BW, C_GE)):
                        TT(out=gm[:, d, :, :], in0=C(mask).unsqueeze(1).broadcast_to([P, NT, P]),
                           in1=cur[:, 0, :, d:d + 1].broadcast_to([P, NT, P]), op=ALU.mult).then_inc(s["g_gm"], 1)
                    for d, mask in ((FW, C_LT), (BW, C_GT)):
                        st.add(TT(out=bm[:, d, :, :], in0=C(mask).unsqueeze(1).broadcast_to([P, NT, P]),
                                  in1=cur[:, 4, :, d:d + 1].broadcast_to([P, NT, P]), op=ALU.mult))
                    st.add(TT(out=ber[:, :, :], in0=cur[:, 4, :, :], in1=cur[:, 2, :, :], op=ALU.mult))
                    pool.wait_ge(s["g_ssum"], h + 1)
                    TT(out=rn[:, :, :].rearrange("p a t -> p (a t)"), in0=ssum[:, :, :].rearrange("p a t -> p (a t)"),
                       in1=half[:, 0:2 * NT], op=ALU.pow).then_inc(s["g_rn"], 1)
                    for p in range(1, 5):
                        pool.wait_ge(s["g_qs"], 4 * h + p)
                        hold(pool, s["g_osum"], 5 * h + p)
                        for d, t in enumerate(CHAIN[p]):
                            if p <= 2:
                                last = pool.tensor_copy(osum[:, t, :], qs[:, d, :])
                            else:
                                last = TT(out=osum[:, t, :], in0=osum[:, t, :], in1=qs[:, d, :], op=ALU.add)
                        last.then_inc(s["g_qsadd"], 1)
                    hold(pool, s["g_oss"], h + 1)
                    st.link(pool.tensor_scalar(out=rn[:, 0, :], in0=rn[:, 0, :], scalar1=0.5 * P ** -0.5, scalar2=None, op0=ALU.mult))
                    st.link(TT(out=osc[:, :], in0=rn[:, 0, :], in1=rn[:, 0, :], op=ALU.mult))
                    st.link(TT(out=osc[:, :], in0=osc[:, :], in1=oss[:, :], op=ALU.mult))
                    st.link(pool.tensor_scalar(out=osc[:, :], in0=osc[:, :], scalar1=1.0 / P, scalar2=EPS, op0=ALU.mult, op1=ALU.add))
                    st.link(TT(out=osc[:, :], in0=osc[:, :], in1=half[:, 0:NT], op=ALU.pow))
                    TT(out=osc[:, :], in0=osc[:, :], in1=rn[:, 0, :], op=ALU.mult).then_inc(s["g_osc"], 1)
                    assert st.n == POOL_STEPS, st.n

            @block.vector
            def _(dve):
                dve.drain().then_inc(s["g_head"], 1)
                TT, TS, STT = dve.tensor_tensor, dve.tensor_scalar, dve.scalar_tensor_tensor
                dve.wait_ge(s["gl_in"], 16)
                with dve.Fori(0, GH) as h:
                    st = Steps(dve, s["g_dve"], h * DVE_STEPS)
                    for d in range(2):
                        st.add(dve.tensor_copy(cur[:, :, :, d:d + 1], ST[:, :, :, bass.ds(h + d * GH, 1)]))
                    for n in range(3):
                        st.add(dve.tensor_copy(cw[:, :, n:n + 1], cwT[:, 0, :, bass.ds(h + n * GH, 1)]))
                    for n in range(3):
                        st.add(dve.tensor_copy(cb[:, n:n + 1], vecT[:, bass.ds(h + n * GH, 1)]))
                    st.wait()
                    TS(out=neg[:, :, :], in0=cur[:, 1, :, :], scalar1=-1.0, scalar2=None, op0=ALU.mult).then_inc(s["g_cur"], 1)

                    def silu(n):
                        dve.wait_ge(s["g_tanh"], 3 * h + n + 1)
                        to = (kq[:, :, 1, :], kraw[:, :, :], vT[:, :, :])[n]
                        STT(out=to[:, 0, :], in0=th[:, n, 0:SEQ], scalar=1.0, in1=conv[:, n, 0:SEQ], op0=ALU.add, op1=ALU.mult)
                        STT(out=to[:, 1:NT, :], in0=th[:, n, LAT:CW].rearrange("p (t n) -> p t n", n=P), scalar=1.0,
                            in1=conv[:, n, LAT:CW].rearrange("p (t n) -> p t n", n=P),
                            op0=ALU.add, op1=ALU.mult).then_inc(s["g_silu"], 1)

                    for n in range(3):
                        dve.wait_ge(s["g_raw"], 3 * h + n + 1)
                        st.link(TS(out=conv[:, n, :], in0=padded[:, n, 0:CW], scalar1=cw[:, 0, n:n + 1], scalar2=cb[:, n:n + 1], op0=ALU.mult, op1=ALU.add))
                        for k in range(1, TAPS):
                            ins = STT(out=conv[:, n, :], in0=padded[:, n, k:k + CW], scalar=cw[:, k, n:n + 1], in1=conv[:, n, :], op0=ALU.mult, op1=ALU.add)
                            if k < TAPS - 1:
                                st.link(ins)
                            else:
                                ins.then_inc(s["g_conv"], 1)
                        if n > 0:
                            silu(n - 1)
                    silu(2)
                    dve.wait_ge(s["g_sums"], h + 1)
                    TS(out=ssum[:, :, :], in0=bank[0][:, 0:2 * NT].rearrange("p (a t) -> p a t", a=2), scalar1=EPS, scalar2=None, op0=ALU.add).then_inc(s["g_ssum"], 1)
                    dve.wait_ge(s["g_rn"], h + 1)
                    dve.wait_ge(s["g_kturn"], h + 1)
                    for t in range(NT):
                        last = TS(out=kn[:, t, :], in0=bank[1 + t // 4][:, t % 4 * P:t % 4 * P + P], scalar1=rn[:, 1, t:t + 1], scalar2=0.5, op0=ALU.mult, op1=ALU.mult)
                    last.then_inc(s["g_kn"], 1)
                    dve.wait_ge(s["g_ztanh"], h + 1)
                    STT(out=zg[:, 0:SEQ], in0=zth[:, 0:SEQ], scalar=1.0, in1=bank[7][:, 0:SEQ], op0=ALU.add, op1=ALU.mult)
                    STT(out=zg[:, SEQ:T], in0=zth[:, SEQ:T], scalar=1.0, in1=bank[6][:, :], op0=ALU.add, op1=ALU.mult).then_inc(s["g_zg"], 1)
                    for d in range(2):
                        dve.wait_ge(s["g_dec"], 2 * h + d + 1)
                        if d == 0:
                            dve.wait_ge(s["g_pool"], POOL_STEPS * h + 3)
                        st.add(TT(out=di[:, d, :, :], in0=dec[:, d, :, :], in1=bm[:, d, :, :], op=ALU.mult))
                    st.wait()
                    dve.wait_ge(s["g_KQkept"], h + 1)
                    for d in range(2):
                        for b, (t0, n) in enumerate(((0, 2), (2, 2), (4, 1))):
                            v = bank[1 + b][:, 0:n * 256].rearrange("p (t a n) -> p t a n", a=2, n=P)
                            u0 = unit(d, t0)
                            st.add(TT(out=MT[:, u0:u0 + n, :], in0=v[:, :, 0, :], in1=di[:, d, t0:t0 + n, :], op=ALU.mult))
                    st.wait()
                    for g, (u0, n) in enumerate(GROUPS):
                        m = cst[:, C_N1F + g:C_N1F + g + 1, :].broadcast_to([P, n, P]) if g < 2 else cst[:, C_N1F:C_N1F + 2, :]
                        st.add(TT(out=DT[:, u0:u0 + n, :], in0=MT[:, u0:u0 + n, :], in1=m, op=ALU.mult))
                    for g, (u0, n) in enumerate(GROUPS):
                        st.wait(2 - g if g == 0 else 2 - g)
                        TT(out=DT[:, u0:u0 + n, :], in0=DT[:, u0:u0 + n, :], in1=cst[:, C_ID:C_ID + 1, :].broadcast_to([P, n, P]), op=ALU.add).then_inc(s["g_D2"], 1)
                    for d in range(2):
                        st.add(TT(out=di[:, d, :, :], in0=dec[:, d, :, :], in1=C((C_LE, C_GE)[d]).unsqueeze(1).broadcast_to([P, NT, P]), op=ALU.mult))
                    st.wait()
                    st.link(TT(out=att[:, FW, :, :], in0=att[:, BW, :, :], in1=di[:, FW, :, :], op=ALU.mult))
                    st.link(TT(out=att[:, BW, :, :], in0=att[:, BW, :, :], in1=di[:, BW, :, :], op=ALU.mult))
                    for l in range(LEVELS):
                        for g, (u0, n) in enumerate(GROUPS):
                            dve.wait_ge(s["g_X"], 18 * h + 3 * l + g + 1)
                            m = negm[:, l, g:g + 1, :].broadcast_to([P, n, P]) if g < 2 else negm[:, l, :, :]
                            TT(out=X[:, u0:u0 + n, :], in0=bank[XB[g]][:, 0:n * P].rearrange("p (u n) -> p u n", n=P), in1=m, op=ALU.mult).then_inc(s["g_Xkept"], 1)
                    dve.wait_ge(s["gs_in"], 32 * h + 32)
                    for p, tiles in enumerate(CHAIN):
                        q = int(p > 0)
                        if p > 0:
                            dve.wait_ge(s["g_KS"], 4 * h + p)
                        for d, t in enumerate(tiles):
                            if p == 0:
                                last = dve.tensor_copy(R[:, d, :], vt[:, t, :])
                            else:
                                last = STT(out=R[:, d, :], in0=bank[0][:, d * P:(d + 1) * P], scalar=neg[:, t, d:d + 1], in1=vt[:, t, :], op0=ALU.mult, op1=ALU.add)
                        last.then_inc(s["g_R"], 1)
                        dve.wait_ge(s["g_vnew"], 5 * h + p + 1)
                        for d, t in enumerate(tiles):
                            last = TS(out=vd[:, d, :], in0=bank[2][:, d * P:(d + 1) * P], scalar1=ber[:, t, d:d + 1], scalar2=None, op0=ALU.mult)
                        last.then_inc(s["g_vd"], 1)
                        dve.wait_ge(s["g_SU"], 5 * h + p + 1)
                        for d, t in enumerate(tiles):
                            if p == 0:
                                dve.tensor_copy(state[:, q, d, :], bank[4][:, d * P:(d + 1) * P]).then_inc(s["g_state"], 1)
                            else:
                                STT(out=state[:, q, d, :], in0=state[:, q, d, :], scalar=cur[:, 3, t, d:d + 1], in1=bank[4][:, d * P:(d + 1) * P], op0=ALU.mult, op1=ALU.add).then_inc(s["g_state"], 1)
                        dve.wait_ge(s["g_O"], 5 * h + p + 1)
                        if p > 0:
                            dve.wait_ge(s["g_qsadd"], 4 * h + p)
                        if p == 0:
                            st.link(dve.tensor_copy(osum[:, 0, :], bank[3][:, 0:P]))
                            TT(out=osum[:, 0, :], in0=osum[:, 0, :], in1=bank[3][:, P:2 * P], op=ALU.add).then_inc(s["g_osum"], 1)
                        else:
                            for d, t in enumerate(tiles):
                                last = TT(out=osum[:, t, :], in0=osum[:, t, :], in1=bank[3][:, d * P:(d + 1) * P], op=ALU.add)
                            last.then_inc(s["g_osum"], 1)
                    dve.wait_ge(s["g_osc"], h + 1)
                    for t in range(NT):
                        last = TS(out=on[:, t, :], in0=osum[:, t, :], scalar1=osc[:, t:t + 1], scalar2=0.5, op0=ALU.mult, op1=ALU.mult)
                    last.then_inc(s["g_on"], 1)
                    dve.wait_ge(s["g_oturn"], h + 1)
                    STT(out=oT[:, bass.ds(h, 1), SEQ - P:4 * P], in0=bank[5][:, :].unsqueeze(1), scalar=vecT[:, 48:49], in1=zg[:, 0:4 * P].unsqueeze(1), op0=ALU.mult, op1=ALU.mult)
                    STT(out=oT[:, bass.ds(h, 1), 4 * P:T], in0=bank[3][:, 0:P].unsqueeze(1), scalar=vecT[:, 48:49], in1=zg[:, 4 * P:T].unsqueeze(1), op0=ALU.mult, op1=ALU.mult).then_inc(s["g_head"], 1)
                    assert st.n == DVE_STEPS, st.n


def ssd(nc, sb, sem, bank, cst, C, hT, ST, cwT, vecT, half, shared, yT, w_in, ssd_d, state_ssd, new_ssd):
    own = ExitStack()
    with own:
        S = lambda name, shape, dt=F32: sb(name, shape, dt, own)
        FW, BW = 0, 1
        GW = HG * SP_
        NQ = GW // P
        NJ = 2 + NQ
        w6 = shared[:, :].rearrange("p (c k n) -> p c k n", c=NJ, k=KD)
        wn = lambda n: w6[:, NQ + n if n < 2 else n - 2, :, :]
        wz = w6[:, 0:NQ, :, :].rearrange("p a b c -> p (a b c)").rearrange("p (k n) -> p k n", k=KD)
        dskip = S("dskip", [P, SH])
        cw = S("scw", [P, TAPS, NJ])
        cb = S("scb", [P, NJ])
        cur = S("scur", [P, 5, NT, 2, HG])
        dter = S("dter", [P, NT, 2, HG])
        dg = S("dg", [P, HG])
        padded = S("spadded", [P, 3, PADW])
        room = S("sroom", [P, 2, 3 * CW])
        flat_room = room[:, :, :].rearrange("p a n -> p (a n)")
        conv = room[:, 0, :].rearrange("p (c n) -> p c n", c=3)
        th = room[:, 1, :].rearrange("p (c n) -> p c n", c=3)
        xe = flat_room[:, 0:4 * GW].rearrange("p (a d n) -> p a d n", a=2, d=2)
        state = flat_room[:, 4 * GW:6 * GW].rearrange("p (d n) -> p d n", d=2)
        BT = S("BT", [P, NT, P])
        CT = S("CT", [P, NT, P])
        xT = S("xT", [P, 3, NT, P])
        dtx = xT[:, :, :, :].rearrange("p a t n -> p (a t n)")[:, 0:2 * GW].rearrange("p (d n) -> p d n", d=2)
        tmp = dtx
        Bt = S("Bt", [P, NT, P])
        xt = S("xt", [P, NT, GW])
        am = S("am", [P, 2, HG, P])
        dec = S("sdec", [P, 2, HG, P])
        M = S("M", [P, 2, HG, P])
        cbm = S("cbm", [P, 2, 2, P])
        srow = S("srow", [P, 2, NQ, P])
        ysum = S("ysum", [P, NT, GW])
        yss = S("yss", [P, NT])
        ysc = S("ysc", [P, NT])
        decf = dec[:, :, :, :].rearrange("p a h n -> p (a h n)")
        Mf = M[:, :, :, :].rearrange("p a h n -> p (a h n)")
        zs = lambda t: Mf[:, t * GW:(t + 1) * GW] if t < 4 else decf[:, 0:GW]
        zth = lambda t: decf[:, (1 + t % 2) * GW:(2 + t % 2) * GW]
        CHAIN = [(0, 0)] + [(1 + s, 4 - s) for s in range(4)]
        names = ("s_win", "s_wzin", "s_bcin", "s_next", "s_din", "s_stin", "s_stout", "s_proj", "s_raw", "s_conv", "s_tanh", "s_silu", "s_turn",
                 "s_turnkept", "s_cur", "s_am", "s_seg", "s_cb", "s_dec", "s_M", "s_dx", "s_y", "s_ykept", "s_xe", "s_st",
                 "s_state", "s_yoff", "s_yoffkept", "s_outturn", "s_outkept", "s_initturn", "s_init", "s_z", "s_zth", "s_zs",
                 "s_yz", "s_yss", "s_ysc", "s_yn", "s_yturn", "s_group", "s_pad", "s_dve", "s_pool")
        s = {n: sem(n) for n in names}
        DVE_STEPS, POOL_STEPS = 69, 3
        OUT = ((6, 7, 0), (5, 7, P), (6, 7, 0), (0, 1, 0), (2, 3, 0), (4, 5, 0))
        hv = lambda ap: ap.rearrange("p (h e) -> p h e", e=SP_)

        with nc.Block() as block:
            @block.sync
            def _(sp):
                sp.dma_start(dskip[:, :], ssd_d[0].partition_broadcast(P)).then_inc(s["s_din"], 16)
                def load_w(g, tiles, signal):
                    for n in tiles:
                        at = g * P + (O_XBC + SH * SP_ + (0, SG * SN)[n]) if n < 2 else g * GW + (O_XBC + (n - 2) * P)
                        src = w_in[0, :, bass.ds(at, P)].rearrange("(k p) n -> p k n", p=P)
                        sp.dma_start(wn(n), src).then_inc(signal, 16)

                def body(g, more):
                    for d in range(2):
                        src = state_ssd[0, 0, d, bass.ds(g * HG, HG), :, :].rearrange("h e n -> (h e) n").rearrange("(q p) n -> p q n", p=P)
                        sp.dma_start(srow[:, d, :, :], src).then_inc(s["s_stin"], 16)
                    sp.wait_ge(s["s_proj"], NJ * g + NJ)
                    src = w_in[0, :, bass.ds(g * GW + O_ZS, GW)].rearrange("(k p) n -> p k n", p=P)
                    sp.dma_start(wz, src).then_inc(s["s_wzin"], 16)
                    if more:
                        load_w(g + 1, (0, 1), s["s_bcin"])
                    sp.wait_ge(s["s_outkept"], g + 1)
                    for d in range(2):
                        dst = new_ssd[0, 0, d, bass.ds(g * HG, HG), :, :].rearrange("h e n -> (h e) n").rearrange("(q p) n -> p q n", p=P)
                        sp.dma_start(dst, srow[:, d, :, :]).then_inc(s["s_stout"], 16)
                    if more:
                        sp.wait_ge(s["s_z"], 5 * g + 5)
                        load_w(g + 1, range(2, NJ), s["s_win"])
                    else:
                        sp.wait_ge(s["s_z"], 5 * g + 5)
                        for n, at in enumerate((O_QKV, O_QKV + D, O_QKV + 2 * D, O_ZG)):
                            sp.dma_start(w6[:, n, :, :], w_in[0, :, at:at + P].rearrange("(k p) n -> p k n", p=P)).then_inc(s["s_next"], 16)
                        sp.wait_ge(s["s_next"], 64)
                    hold(sp, s["s_stout"], 32 * g + 32)

                load_w(0, (0, 1), s["s_bcin"])
                load_w(0, range(2, NJ), s["s_win"])
                with sp.Fori(0, SG - 1) as g:
                    body(g, True)
                body(SG - 1, False)

            @block.tensor
            def _(pe):
                def proj(n):
                    a, b, at = OUT[n]
                    for k in range(KD):
                        pe.matmul(bank[a][:, :], wn(n)[:, k, :], hT[:, k, SEQ:T], start=(k == 0), stop=(k == KD - 1))
                    for k in range(KD):
                        last = pe.matmul(bank[b][:, at:at + P], wn(n)[:, k, :], hT[:, k, 0:SEQ], start=(k == 0), stop=(k == KD - 1))
                    return last

                def body(g, more):
                    def turn(n, m):
                        pe.wait_ge(s["s_silu"], NJ * g + n + 1)
                        if m > 0:
                            pe.wait_ge(s["s_turnkept"], 5 * g + m)
                        src = BT if n == 0 else xT[:, (n - 2) % 3, :, :]
                        for t in range(NT):
                            last = pe.transpose(bank[6 + t // 4][:, t % 4 * P:t % 4 * P + P], src[:, t, :], C(C_ID))
                        last.then_inc(s["s_turn"], 1)

                    pe.wait_ge(s["s_win"], 16 * NQ * g + 16 * NQ)
                    for n in range(2, NJ):
                        if n == 2:
                            pe.wait_ge(s["s_raw"], NJ * g + 2)
                        if n == 3:
                            pe.wait_ge(s["s_group"], g + 1)
                        proj(n).then_inc(s["s_proj"], 1)
                        if n == 3:
                            pe.wait_ge(s["s_raw"], NJ * g + 3)
                            turn(0, 0)
                        if n > 3:
                            turn(n - 2, n - 3)

                    def cbs(t):
                        if t >= 2:
                            pe.wait_ge(s["s_M"], 10 * g + 2 * t - 3)
                        pe.matmul(bank[4 + t % 2][:, 0:P], BT[:, t, :], CT[:, t, :], start=True, stop=True).then_inc(s["s_cb"], 1)

                    def seg(u):
                        pe.wait_ge(s["s_am"], 10 * g + u + 1)
                        if u >= 2:
                            pe.wait_ge(s["s_dec"], 10 * g + u - 1)
                        for half_ in range(2):
                            last = pe.matmul(bank[2 * (u % 2) + half_][:, :], C((C_GT, C_LT)[u % 2]),
                                             am[:, u % 2, 4 * half_:4 * half_ + 4, :].rearrange("p h n -> p (h n)"), start=True, stop=True)
                        last.then_inc(s["s_seg"], 1)

                    pe.wait_ge(s["s_raw"], NJ * g + NJ)
                    cbs(0)
                    seg(0)
                    turn(4, 3)
                    seg(1)
                    turn(5, 4)
                    for u in range(2 * NT):
                        t, d = u // 2, u % 2
                        if 0 < u < 2 * NT - 1:
                            if (u + 1) % 2 == 0:
                                cbs((u + 1) // 2)
                            seg(u + 1)
                        if u == 0:
                            pe.wait_ge(s["s_turnkept"], 5 * g + 5)
                        if d == 0 and t >= 2:
                            pe.wait_ge(s["s_ykept"], 5 * g + t - 1)
                        pe.wait_ge(s["s_M"], 10 * g + u + 1)
                        for h in range(HG):
                            last = pe.matmul(bank[6 + t % 2][:, h * SP_:(h + 1) * SP_], M[:, u % 2, h, :], dtx[:, u % 2, h * SP_:(h + 1) * SP_],
                                             start=(d == 0 and h == 0), stop=(d == 1), skip_group_check=True)
                        last.then_inc(s["s_y"], 1)
                    pe.wait_ge(s["s_dec"], 10 * g + 10)

                    def states(p):
                        pe.wait_ge(s["s_xe"], 5 * g + p + 1)
                        for d, t in enumerate(CHAIN[p]):
                            last = pe.matmul(bank[2 + d][:, :], Bt[:, t, :], xe[:, p % 2, d, :], start=True, stop=True)
                        last.then_inc(s["s_st"], 1)

                    def zproj(t):
                        if t == 0:
                            pe.wait_ge(s["s_wzin"], 16 * g + 16)
                        if t == 4:
                            pe.wait_ge(s["s_zs"], 5 * g + 1)
                        for k in range(KD):
                            last = pe.matmul(bank[4 + t % 4][:, :], hT[:, k, t * P:(t + 1) * P], wz[:, k, :], start=(k == 0), stop=(k == KD - 1))
                        last.then_inc(s["s_z"], 1)

                    states(0)
                    pe.wait_ge(s["s_ykept"], 5 * g + 5)
                    pe.wait_ge(s["s_stin"], 32 * g + 32)
                    for d in range(2):
                        for q in range(NQ):
                            last = pe.transpose(bank[6 + d][:, q * P:(q + 1) * P], srow[:, d, q, :], C(C_ID))
                    last.then_inc(s["s_initturn"], 1)
                    pe.wait_ge(s["s_state"], 10 * g + 2)
                    for d in range(2):
                        for q in range(NQ):
                            last = pe.transpose(bank[4 + d][:, q * P:(q + 1) * P], state[:, d, q * P:(q + 1) * P], C(C_ID))
                    last.then_inc(s["s_outturn"], 1)
                    for p in range(1, 5):
                        if p == 1:
                            pe.wait_ge(s["s_init"], g + 1)
                        else:
                            pe.wait_ge(s["s_state"], 10 * g + 2 * p)
                            pe.wait_ge(s["s_yoffkept"], 4 * g + p - 1)
                        for d, t in enumerate(CHAIN[p]):
                            last = pe.matmul(bank[d][:, :], CT[:, t, :], state[:, d, :], start=True, stop=True)
                        last.then_inc(s["s_yoff"], 1)
                        states(p)
                        if p == 1:
                            pe.wait_ge(s["s_outkept"], g + 1)
                        zproj(p - 1)
                    zproj(4)
                    if more:
                        pe.wait_ge(s["s_bcin"], 32 * g + 64)
                        pe.wait_ge(s["s_zs"], 5 * g + 4)
                        proj(0)
                        proj(1).then_inc(s["s_proj"], 2)
                    for t in range(NT):
                        pe.wait_ge(s["s_yn"], 5 * g + t + 1)
                        for q in range(NQ):
                            to = bank[q][:, t * P:(t + 1) * P] if t < 4 else bank[4][:, q * P:(q + 1) * P]
                            last = pe.transpose(to, ysum[:, t, q * P:(q + 1) * P], C(C_ID))
                    last.then_inc(s["s_yturn"], 1)

                pe.wait_ge(s["s_bcin"], 32)
                proj(0)
                proj(1).then_inc(s["s_proj"], 2)
                with pe.Fori(0, SG - 1) as g:
                    body(g, True)
                body(SG - 1, False)

            @block.scalar
            def _(act):
                def raw(g, n):
                    act.wait_ge(s["s_proj"], NJ * g + n + 1)
                    if n >= 3:
                        act.wait_ge(s["s_conv"], NJ * g + n - 2)
                    a, b, at = OUT[n]
                    act.copy(padded[:, n % 3, 2:2 + SEQ], bank[b][:, at:at + P])
                    act.copy(padded[:, n % 3, 6 + SEQ:6 + T], bank[a][:, :]).then_inc(s["s_raw"], 1)

                def body(g, more):
                    def keep_turn(m):
                        act.wait_ge(s["s_turn"], 5 * g + m + 1)
                        to = Bt[:, :, :] if m == 0 else xt[:, :, (m - 1) * P:m * P]
                        act.copy(to[:, 0:4, :], bank[6][:, :].rearrange("p (t n) -> p t n", n=P))
                        act.copy(to[:, 4, :], bank[7][:, 0:P]).then_inc(s["s_turnkept"], 1)

                    for n in range(NJ):
                        if n >= 2:
                            raw(g, n)
                        act.wait_ge(s["s_conv"], NJ * g + n + 1)
                        if n >= 3:
                            act.wait_ge(s["s_silu"], NJ * g + n - 2)
                        act.activation(th[:, n % 3, :], conv[:, n % 3, :], ACT.Tanh).then_inc(s["s_tanh"], 1)
                        if n >= 3:
                            keep_turn(n - 3)
                    for u in range(2 * NT):
                        if u == 1:
                            keep_turn(3)
                            keep_turn(4)
                        act.wait_ge(s["s_seg"], 10 * g + u + 1)
                        if u >= 2:
                            act.wait_ge(s["s_M"], 10 * g + u - 1)
                        for half_ in range(2):
                            last = act.activation(dec[:, u % 2, 4 * half_:4 * half_ + 4, :], bank[2 * (u % 2) + half_][:, :].rearrange("p (h n) -> p h n", n=P), ACT.Exp)
                        last.then_inc(s["s_dec"], 1)
                    act.wait_ge(s["s_outturn"], g + 1)
                    for d in range(2):
                        last = act.copy(srow[:, d, :, :], bank[4 + d][:, :].rearrange("p (q n) -> p q n", n=P))
                    last.then_inc(s["s_outkept"], 1)
                    for d in range(2):
                        last = act.copy(state[:, d, :], bank[6 + d][:, :])
                    last.then_inc(s["s_init"], 1)
                    for t in range(NT):
                        act.wait_ge(s["s_z"], 5 * g + t + 1)
                        if t == 0:
                            act.wait_ge(s["s_M"], 10 * g + 10)
                        if t >= 2:
                            act.wait_ge(s["s_zs"], 5 * g + t - 1)
                        act.activation(zth(t), bank[4 + t % 4][:, :], ACT.Tanh, scale=0.5).then_inc(s["s_zth"], 1)
                    for t in range(NT):
                        act.wait_ge(s["s_yz"], 5 * g + t + 1)
                        act.activation(xt[:, t, :], ysum[:, t, :], ACT.Square, scale=0.5, accum_out=yss[:, t:t + 1]).then_inc(s["s_yss"], 1)
                    if more:
                        raw(g + 1, 0)
                        raw(g + 1, 1)
                    act.wait_ge(s["s_yturn"], g + 1)
                    for q in range(NQ):
                        w = vecT[:, bass.ds(g * NQ + (49 + q), 1)]
                        act.activation(yT[:, bass.ds(g * NQ + q, 1), 0:4 * P], bank[q][:, :].unsqueeze(1), ACT.Copy, scale=w)
                        last = act.activation(yT[:, bass.ds(g * NQ + q, 1), 4 * P:T], bank[4][:, q * P:(q + 1) * P].unsqueeze(1), ACT.Copy, scale=w)
                    last.then_inc(s["s_group"], 1)

                act.wait_ge(s["s_pad"], 1)
                raw(0, 0)
                raw(0, 1)
                with act.Fori(0, SG - 1) as g:
                    body(g, True)
                body(SG - 1, False)

            @block.gpsimd
            def _(pool):
                pool.memset(padded[:, :, :], 0.0).then_inc(s["s_pad"], 1)
                pool.wait_ge(s["s_din"], 16)
                with pool.Fori(0, SG) as g:
                    st = Steps(pool, s["s_pool"], g * POOL_STEPS, held=True)
                    TT = pool.tensor_tensor
                    pool.wait_ge(s["s_cur"], g + 1)
                    st.add(TT(out=dter[:, :, :, :], in0=cur[:, 4, :, :, :], in1=cur[:, 2, :, :, :], op=ALU.mult))
                    for u in range(2 * NT):
                        t, d = u // 2, u % 2
                        if u >= 2:
                            pool.wait_ge(s["s_seg"], 10 * g + u - 1)
                        TT(out=am[:, d, :, :], in0=C((C_LE, C_GE)[d]).unsqueeze(1).broadcast_to([P, HG, P]),
                           in1=cur[:, 0, t, d, :].unsqueeze(2).broadcast_to([P, HG, P]), op=ALU.mult).then_inc(s["s_am"], 1)
                        if u >= 3 and d == 1 or u == 2 * NT - 1:
                            for tt in ([t - 1] if u < 2 * NT - 1 else [t - 1, t]):
                                if tt == 0:
                                    continue
                                skip(pool, s, TT, g, tt, ysum, xt, dg, hv)
                        if u == 1:
                            pool.wait_ge(s["s_turnkept"], 5 * g + 5)
                            skip(pool, s, TT, g, 0, ysum, xt, dg, hv)
                    st.wait()
                    for p, tiles in enumerate(CHAIN):
                        if p >= 2:
                            pool.wait_ge(s["s_st"], 5 * g + p - 1)
                        for d, t in enumerate(tiles):
                            last = TT(out=hv(xe[:, p % 2, d, :]), in0=hv(xt[:, t, :]), in1=dter[:, t, d, :].unsqueeze(2).broadcast_to([P, HG, SP_]), op=ALU.mult)
                        last.then_inc(s["s_xe"], 1)
                    hold(pool, s["s_yss"], 5 * g + 5)
                    st.link(pool.tensor_scalar(out=ysc[:, :], in0=yss[:, :], scalar1=1.0 / GW, scalar2=EPS, op0=ALU.mult, op1=ALU.add))
                    st.link(TT(out=ysc[:, :], in0=ysc[:, :], in1=half[:, 0:NT], op=ALU.pow))
                    pool.tensor_scalar(out=ysc[:, :], in0=ysc[:, :], scalar1=0.5, scalar2=None, op0=ALU.mult).then_inc(s["s_ysc"], 1)
                    assert st.n == POOL_STEPS, st.n

            @block.vector
            def _(dve):
                dve.drain().then_inc(s["s_group"], 1)
                TT, TS, STT = dve.tensor_tensor, dve.tensor_scalar, dve.scalar_tensor_tensor
                with dve.Fori(0, SG) as g:
                    st = Steps(dve, s["s_dve"], g * DVE_STEPS)
                    dve.wait_ge(s["s_group"], g + 1)
                    for d in range(2):
                        st.add(dve.tensor_copy(cur[:, :, :, d, :], ST[:, :, :, bass.ds(g * HG + (2 * GH + d * SH), HG)]))
                    for n in range(NJ):
                        at = g + (16, 20)[n] if n < 2 else g * NQ + (n - 2)
                        st.add(TS(out=cw[:, :, n:n + 1], in0=cwT[:, 1, :, bass.ds(at, 1)], scalar1=0.5, scalar2=None, op0=ALU.mult))
                        at = g + (40, 44)[n] if n < 2 else g * NQ + (24 + n - 2)
                        st.add(TS(out=cb[:, n:n + 1], in0=vecT[:, bass.ds(at, 1)], scalar1=0.5, scalar2=None, op0=ALU.mult))
                    dve.wait_ge(s["s_din"], 16)
                    st.add(dve.tensor_copy(dg[:, :], dskip[:, bass.ds(g * HG, HG)]))
                    hold(dve, s["s_dve"], st.base + st.n)
                    dve.engine_nop().then_inc(s["s_cur"], 1)

                    def silu(n):
                        dve.wait_ge(s["s_tanh"], NJ * g + n + 1)
                        if n >= 5:
                            dve.wait_ge(s["s_turn"], 5 * g + n - 3)
                        to = (BT, CT)[n] if n < 2 else xT[:, (n - 2) % 3, :, :]
                        STT(out=to[:, 0, :], in0=th[:, n % 3, 0:SEQ], scalar=1.0, in1=conv[:, n % 3, 0:SEQ], op0=ALU.add, op1=ALU.mult)
                        STT(out=to[:, 1:NT, :], in0=th[:, n % 3, LAT:CW].rearrange("p (t n) -> p t n", n=P), scalar=1.0,
                            in1=conv[:, n % 3, LAT:CW].rearrange("p (t n) -> p t n", n=P),
                            op0=ALU.add, op1=ALU.mult).then_inc(s["s_silu"], 1)

                    for n in range(NJ):
                        dve.wait_ge(s["s_raw"], NJ * g + n + 1)
                        c3 = conv[:, n % 3, :]
                        st.link(TS(out=c3, in0=padded[:, n % 3, 0:CW], scalar1=cw[:, 0, n:n + 1], scalar2=cb[:, n:n + 1], op0=ALU.mult, op1=ALU.add))
                        for k in range(1, TAPS):
                            ins = STT(out=c3, in0=padded[:, n % 3, k:k + CW], scalar=cw[:, k, n:n + 1], in1=c3, op0=ALU.mult, op1=ALU.add)
                            if k < TAPS - 1:
                                st.link(ins)
                            else:
                                ins.then_inc(s["s_conv"], 1)
                        silu(n)

                    def keep_y(t):
                        dve.wait_ge(s["s_y"], 10 * g + 2 * t + 2)
                        dve.wait_ge(s["s_dx"], 5 * g + t + 1)
                        TT(out=ysum[:, t, :], in0=ysum[:, t, :], in1=bank[6 + t % 2][:, :], op=ALU.add).then_inc(s["s_ykept"], 1)

                    dve.wait_ge(s["s_turnkept"], 5 * g + 5)
                    for u in range(2 * NT):
                        t, d = u // 2, u % 2
                        if d == 0:
                            dve.wait_ge(s["s_cb"], 5 * g + t + 1)
                            for e in range(2):
                                st.add(TT(out=cbm[:, t % 2, e, :], in0=bank[4 + t % 2][:, 0:P], in1=C((C_LE, C_GE)[e]), op=ALU.mult))
                        if u >= 2:
                            dve.wait_ge(s["s_y"], 10 * g + u - 1)
                        TT(out=hv(dtx[:, d, :]), in0=hv(xt[:, t, :]), in1=cur[:, 4, t, d, :].unsqueeze(2).broadcast_to([P, HG, SP_]), op=ALU.mult)
                        if d == 0:
                            st.wait()
                        dve.wait_ge(s["s_dec"], 10 * g + u + 1)
                        TT(out=M[:, d, :, :], in0=dec[:, d, :, :], in1=cbm[:, t % 2, d:d + 1, :].broadcast_to([P, HG, P]), op=ALU.mult).then_inc(s["s_M"], 1)
                        if d == 1 and t >= 1:
                            keep_y(t - 1)
                    keep_y(NT - 1)

                    def gate(t):
                        dve.wait_ge(s["s_zth"], 5 * g + t + 1)
                        STT(out=zs(t), in0=zth(t), scalar=1.0, in1=bank[4 + t % 4][:, :], op0=ALU.add, op1=ALU.mult).then_inc(s["s_zs"], 1)

                    for p, tiles in enumerate(CHAIN):
                        if p == 1:
                            dve.wait_ge(s["s_init"], g + 1)
                            dve.wait_ge(s["s_outturn"], g + 1)
                        if p > 0:
                            dve.wait_ge(s["s_yoff"], 4 * g + p)
                            for d, t in enumerate(tiles):
                                st.add(TT(out=hv(state[:, d, :]), in0=hv(state[:, d, :]), in1=cur[:, 3, t, d, :].unsqueeze(2).broadcast_to([P, HG, SP_]), op=ALU.mult))
                            st.wait()
                        dve.wait_ge(s["s_st"], 5 * g + p + 1)
                        for d, t in enumerate(tiles):
                            if p == 0:
                                dve.tensor_copy(state[:, d, :], bank[2 + d][:, :]).then_inc(s["s_state"], 1)
                            else:
                                TT(out=state[:, d, :], in0=state[:, d, :], in1=bank[2 + d][:, :], op=ALU.add).then_inc(s["s_state"], 1)
                        if p > 0:
                            for d, t in enumerate(tiles):
                                ins = TT(out=hv(tmp[:, d, :]), in0=hv(bank[d][:, :]), in1=cur[:, 1, t, d, :].unsqueeze(2).broadcast_to([P, HG, SP_]), op=ALU.mult)
                                st.add(ins) if d == 0 else ins.then_inc(s["s_yoffkept"], 1)
                            dve.wait_ge(s["s_yoffkept"], 4 * g + p)
                            for d, t in enumerate(tiles):
                                st.add(TT(out=ysum[:, t, :], in0=ysum[:, t, :], in1=tmp[:, d, :], op=ALU.add))
                            st.wait()
                            gate(p - 1)
                    gate(4)
                    dve.wait_ge(s["s_zs"], 5 * g + 5)
                    for t in range(NT):
                        TT(out=ysum[:, t, :], in0=ysum[:, t, :], in1=zs(t), op=ALU.mult).then_inc(s["s_yz"], 1)
                    dve.wait_ge(s["s_ysc"], g + 1)
                    for t in range(NT):
                        TS(out=ysum[:, t, :], in0=ysum[:, t, :], scalar1=ysc[:, t:t + 1], scalar2=None, op0=ALU.mult).then_inc(s["s_yn"], 1)
                    assert st.n == DVE_STEPS, st.n


def skip(pool, s, TT, g, t, ysum, xt, dg, hv):
    TT(out=hv(ysum[:, t, :]), in0=hv(xt[:, t, :]), in1=dg[:, :].unsqueeze(2).broadcast_to([P, HG, SP_]), op=ALU.mult).then_inc(s["s_dx"], 1)


def merge(nc, sb, sem, bank, hT, oT, yT, mT, shared, w_in, w_gdn_out, w_ssd_out):
    own = ExitStack()
    with own:
        S = lambda name, shape, dt=F32: sb(name, shape, dt, own)
        KS = SH * SP_ // P
        wm = S("wm", [P, 2, 3 * KD + KS, P])
        brought = shared[:, KD * P:4 * KD * P].rearrange("p (k n) -> p k n", n=P)
        gth = S("gth", [P, 2, T])
        prod = S("prod", [P, 2, T])
        SRC = ((0, KD, hT), (KD, KD, hT), (2 * KD, KD, oT), (3 * KD, KS, yT))
        wm_in = [sem("wm_in0"), sem("wm_in1")]
        wm_used, m_done, m_tanh, m_prod, m_kept, m_free = (sem(n) for n in ("wm_used", "m_done", "m_tanh", "m_prod", "m_kept", "m_free"))
        with nc.Block() as block:
            @block.sync
            def _(sp):
                def load(n, par, first=False):
                    for at, w, off in ((0, w_in[0], O_GATE), (KD, w_in[0], O_GATE + D), (2 * KD, w_gdn_out[0], 0), (3 * KD, w_ssd_out[0], 0)):
                        kk = KS if at == 3 * KD else KD
                        if first and at < 3 * KD:
                            continue
                        sp.dma_start(wm[:, par, at:at + kk, :], w[:, bass.ds(n * P + off, P)].rearrange("(k p) n -> p k n", p=P)).then_inc(wm_in[par], 16)

                load(0, 0, True)
                load(1, 1)
                with sp.Fori(0, KD // 2 - 1) as i:
                    for par in range(2):
                        sp.wait_ge(m_done, 5 * (2 * i + par) + 5)
                        load(2 * i + par + 2, par)

            @block.tensor
            def _(pe):
                def turn(i, par, first, brought_first=False):
                    n = 2 * i + par
                    if brought_first:
                        W = lambda at: brought[:, at, :] if at < 3 * KD else wm[:, par, at, :]
                    else:
                        W = lambda at: wm[:, par, at, :]
                        pe.wait_ge(wm_in[par], 64 * i + (64 - 48 * (par == 0)))
                    for j, (at, kk, src) in enumerate(SRC):
                        if brought_first and j == 3:
                            pe.wait_ge(wm_in[par], 16)
                        if not first:
                            if j < 2:
                                pe.wait_ge(m_tanh, 3 * (n - 1) + j + 1)
                                pe.wait_ge(m_kept, n)
                            else:
                                pe.wait_ge(m_kept, n)
                        for k in range(kk):
                            last = pe.matmul(bank[j][:, :], W(at + k), src[:, k, SEQ:T], start=(k == 0), stop=(k == kk - 1))
                        last.then_inc(m_done, 1)
                    for j, (at, kk, src) in enumerate(SRC):
                        for k in range(kk):
                            last = pe.matmul(bank[4][:, j * P:(j + 1) * P], W(at + k), src[:, k, 0:SEQ], start=(k == 0), stop=(k == kk - 1))
                    last.then_inc(m_done, 1)

                turn(0, 0, True, True)
                turn(0, 1, False)
                with pe.Fori(1, KD // 2) as i:
                    for par in range(2):
                        turn(i, par, False)

            @block.scalar
            def _(act):
                act.wait_ge(m_free, 1)
                with act.Fori(0, KD) as n:
                    act.wait_ge(m_free, n + 1)
                    for j in range(2):
                        act.wait_ge(m_done, 5 * n + j + 1)
                        act.activation(gth[:, j, SEQ:T], bank[j][:, :], ACT.Tanh, scale=0.5).then_inc(m_tanh, 1)
                    act.wait_ge(m_done, 5 * n + 5)
                    act.activation(gth[:, :, 0:SEQ], bank[4][:, 0:2 * P].rearrange("p (j n) -> p j n", j=2), ACT.Tanh, scale=0.5).then_inc(m_tanh, 1)

            @block.vector
            def _(dve):
                dve.drain().then_inc(m_free, 1)
                with dve.Fori(0, KD) as n:
                    for j in range(2):
                        dve.wait_ge(m_tanh, 3 * n + j + 1)
                        dve.wait_ge(m_done, 5 * n + j + 3)
                        dve.scalar_tensor_tensor(out=prod[:, j, SEQ:T], in0=gth[:, j, SEQ:T], scalar=1.0, in1=bank[2 + j][:, :], op0=ALU.add, op1=ALU.mult).then_inc(m_prod, 1)
                    dve.wait_ge(m_tanh, 3 * n + 3)
                    dve.scalar_tensor_tensor(out=prod[:, :, 0:SEQ], in0=gth[:, :, 0:SEQ], scalar=1.0,
                                             in1=bank[4][:, 2 * P:4 * P].rearrange("p (j n) -> p j n", j=2), op0=ALU.add, op1=ALU.mult).then_inc(m_kept, 1)
                    dve.wait_ge(m_prod, 2 * n + 2)
                    dve.wait_ge(m_kept, n + 1)
                    dve.tensor_tensor(out=mT[:, bass.ds(n, 1), :], in0=prod[:, 0:1, :], in1=prod[:, 1:2, :], op=ALU.add).then_inc(m_free, 1)


def route(nc, sb, sem, bank, C, cols, half, mT, ada, pos, x_prompt, x_sample, w_o, ln1_g, ln1_b, w_router_group,
          b_router_group, w_router_expert, b_router_expert, h2d, x1d, lists, yd, idx, slots, wts, more, wgu, wdn, w_exp_gate, w_exp_up, w_exp_down):
    own = ExitStack()
    with own:
        S = lambda name, shape, dt=F32: sb(name, shape, dt, own)
        NR = XG + NX
        wo = S("wo", [P, KD, D])
        wr = S("wr", [P, KD, NR])
        br = S("br", [P, NR])
        x = S("rx", [P, NT, D])
        pt = S("rpos", [P, NT - 1, D])
        g1 = S("g1", [P, 2, D])
        sc2 = S("sc2", [P, 2, D])
        sh2 = S("sh2", [P, 2, D])
        lg = S("lg", [P, D])
        lb = S("lb", [P, D])
        tmp = S("rtmp", [P, D])
        bn = S("rbn", [P, 2, 6])
        mv = S("rmv", [P, 2])
        ve = S("rve", [P, 2, NT])
        rs = S("rrs", [P, 2, NT])
        h2 = S("h2", [P, 2, D])
        h2T = S("h2T", [P, KD, P])
        lo = S("lo", [P, NT, NR])
        gmax = S("gmax", [P, NT, 1])
        gsh = S("gsh", [P, NT, XG])
        gex = S("gex", [P, NT, XG])
        gsum = S("gsum", [P, NT, 1])
        eq = S("eq", [P, NT, XG])
        rank = S("rank", [P, NT, 1])
        lsel = S("lsel", [P, NT, XG, XE])
        les = S("les", [P, NT, XE])
        top = S("top8", [P, NT, 8])
        topi = S("topi", [P, NT, 8], U32)
        eid = S("eid", [P, NT, 2])
        gidx = S("gidx", [P, NT, 1])
        dif = S("dif", [P, NT, 1])
        tex = S("tex", [P, NT, 1])
        oh = S("oh", [P, 2, NT, NX])
        both = S("both", [P, NT, NX])
        place = S("place", [P, NT, NX])
        pick = S("pick", [P, 2, NT, NX])
        slotf = S("slotf", [P, 2, NT, 1])
        nmore = S("nmore", [P, NX])
        upto = S("upto", [P, NX])
        far = S("far", [P, NX])
        past = S("past", [P, NT, NX])
        later = S("later", [P, NMORE, NX])
        whose = S("whose", [P, NMORE + 1])
        zero = S("zero", [P, D])
        rows_ = S("rows_", [NX, P])
        x_in, wr_in, row_in, pos_in = (sem(n) for n in ("r_x", "r_wr", "r_row", "r_pos"))
        wo_in = [sem("r_wo0"), sem("r_wo1")]
        mixed, x1_done, ve_ready, rs_ready, h2_ready, x1_out = (sem(n) for n in (
            "r_mixed", "r_x1", "r_ve", "r_rs", "r_h2", "r_x1out"))
        h2_out = [sem("r_h2out0"), sem("r_h2out1")]
        h2_turned, h2_kept, logits, lo_kept, z_out, gs_ready, gex_ready, dif_ready, tex_ready = (sem(n) for n in (
            "r_turned", "r_kept", "r_logits", "r_lokept", "r_zout", "r_gs", "r_gex", "r_dif", "r_tex"))
        both_ready, counted, slots_ready, scattered, rows_in, rows_turned, own_dve, sq_kept = (sem(n) for n in (
            "r_both", "r_counted", "r_slots", "r_scattered", "r_rowsin", "r_rowsturned", "r_dve", "r_free"))
        zero_ready, yz_out, we_in = sem("r_zero"), sem("r_yz"), sem("r_we")
        rows = lambda ap: ap.partition_broadcast(P)
        with nc.Block() as block:
            @block.sync
            def _(sp):
                for h in range(2):
                    sp.dma_start(wo[:, :, h * 512:(h + 1) * 512], w_o[0, :, h * 512:(h + 1) * 512].rearrange("(k p) n -> p k n", p=P)).then_inc(wo_in[h], 16)
                sp.dma_start(x[:, 0, :], x_prompt[0]).then_inc(x_in, 16)
                sp.dma_start(x[:, 1:NT, :], x_sample[0].rearrange("(t p) n -> p t n", p=P)).then_inc(x_in, 16)
                for cond in range(2):
                    sp.dma_start(g1[:, cond, :], rows(ada[cond, 2 * D:3 * D])).then_inc(row_in, 16)
                    sp.dma_start(sh2[:, cond, :], rows(ada[cond, 3 * D:4 * D])).then_inc(row_in, 16)
                    sp.dma_start(sc2[:, cond, :], rows(ada[cond, 4 * D:5 * D])).then_inc(row_in, 16)
                sp.dma_start(lg[:, :], rows(ln1_g[0])).then_inc(row_in, 16)
                sp.dma_start(lb[:, :], rows(ln1_b[0])).then_inc(row_in, 16)
                sp.dma_start(wr[:, :, 0:XG], w_router_group[0].rearrange("(k p) n -> p k n", p=P)).then_inc(wr_in, 16)
                sp.dma_start(wr[:, :, XG:NR], w_router_expert[0].rearrange("(k p) n -> p k n", p=P)).then_inc(wr_in, 16)
                sp.dma_start(br[:, 0:XG], rows(b_router_group[0])).then_inc(wr_in, 16)
                sp.dma_start(br[:, XG:NR], rows(b_router_expert[0])).then_inc(wr_in, 16)
                for e in range(2):
                    load_expert(sp, e, wgu[e], wdn[e], w_exp_gate, w_exp_up, w_exp_down, we_in)
                sp.wait_ge(zero_ready, 1)
                sp.dma_start(lists.rearrange("(p n) a -> p (n a)", p=P), zero[:, 0:NPLACE // P]).then_inc(z_out, 16)
                sp.dma_start(yd[NX * P:NPLACE, :].rearrange("(b p) n -> p b n", p=P), zero[:, :].unsqueeze(1).broadcast_to([P, NMORE, D])).then_inc(yz_out, 16)
                for t in range(NT):
                    sp.wait_ge(x1_done, t + 1)
                    sp.dma_start(x1d[t * P:(t + 1) * P, :], x[:, t, :]).then_inc(x1_out, 16)
                    sp.wait_ge(h2_ready, t + 1)
                    sp.dma_start(h2d[t * P:(t + 1) * P, :], h2[:, t % 2, :]).then_inc(h2_out[t % 2], 16)
                sp.wait_ge(scattered, 16 * 2 * NT)
                sp.dma_start(rows_[:, :], lists[0:NX * P, :].rearrange("(e n) a -> e (n a)", e=NX)).then_inc(rows_in, 16)
                sp.wait_ge(we_in, 96)
                sp.wait_ge(x1_out, 16 * NT)
                sp.wait_ge(yz_out, 16)
                sp.wait_ge(h2_out[0], 16 * 3)
                sp.wait_ge(h2_out[1], 16 * 2)

            @block.scalar
            def _(act):
                act.dma_start(pt[:, :, :], pos.rearrange("(t p) n -> p t n", p=P)).then_inc(pos_in, 16)
                for t in range(NT):
                    act.wait_ge(h2_turned, t + 1)
                    if t > 0:
                        act.wait_ge(logits, t)
                    for h in range(2):
                        last = act.copy(h2T[:, 4 * h:4 * h + 4, :], bank[4 + h][:, :].rearrange("p (k n) -> p k n", n=P))
                    last.then_inc(h2_kept, 1)
                act.wait_ge(gs_ready, 1)
                act.activation(gex[:, :, :], gsh[:, :, :], ACT.Exp).then_inc(gex_ready, 1)
                act.wait_ge(dif_ready, 1)
                act.activation(tex[:, :, :], dif[:, :, :], ACT.Exp).then_inc(tex_ready, 1)

            @block.tensor
            def _(pe):
                def mix(t):
                    if t >= 2:
                        pe.wait_ge(sq_kept, t - 1)
                    for h in range(2):
                        if t == 0:
                            pe.wait_ge(wo_in[h], 16)
                        for k in range(KD):
                            last = pe.matmul(bank[2 * (t % 2) + h][:, :], mT[:, k, t * P:(t + 1) * P], wo[:, k, h * 512:(h + 1) * 512], start=(k == 0), stop=(k == KD - 1))
                    last.then_inc(mixed, 1)

                def router(t):
                    pe.wait_ge(h2_ready, t + 1)
                    if t > 0:
                        pe.wait_ge(h2_kept, t)
                    for k in range(KD):
                        last = pe.transpose(bank[4 + k // 4][:, k % 4 * P:k % 4 * P + P], h2[:, t % 2, k * P:(k + 1) * P], C(C_ID))
                    last.then_inc(h2_turned, 1)
                    pe.wait_ge(h2_kept, t + 1)
                    if t == 0:
                        pe.wait_ge(wr_in, 64)
                    else:
                        pe.wait_ge(lo_kept, t)
                    for k in range(KD):
                        last = pe.matmul(bank[6][:, 0:NR], h2T[:, k, :], wr[:, k, :], start=(k == 0), stop=(k == KD - 1))
                    last.then_inc(logits, 1)

                mix(0)
                mix(1)
                for t in range(NT):
                    if t + 2 < NT:
                        mix(t + 2)
                    router(t)
                pe.wait_ge(both_ready, 1)
                for t in range(NT):
                    for e in range(t):
                        pe.matmul(bank[7][:, t * NX:(t + 1) * NX], C(C_ONE), both[:, e, :], start=(e == 0), stop=False)
                    pe.matmul(bank[7][:, t * NX:(t + 1) * NX], C(C_LT), both[:, t, :], start=(t == 0), stop=True)
                for t in range(NT):
                    last = pe.matmul(bank[7][:, NT * NX:(NT + 1) * NX], C(C_ONE), both[:, t, :], start=(t == 0), stop=(t == NT - 1))
                last.then_inc(counted, 1)
                pe.wait_ge(rows_in, 16)
                pe.transpose(bank[4][:, 0:NX], rows_[:, :], C(C_ID)[0:NX, 0:NX]).then_inc(rows_turned, 1)

            @block.gpsimd
            def _(pool):
                pool.memset(zero[:, :], 0.0).then_inc(zero_ready, 1)
                for t in range(NT):
                    for n in range(2):
                        pool.wait_ge(ve_ready, 2 * t + n + 1)
                        pool.tensor_tensor(out=rs[:, n, t:t + 1], in0=ve[:, n, t:t + 1], in1=half[:, 0:1], op=ALU.pow).then_inc(rs_ready, 1)
                pool.wait_ge(z_out, 16)
                pool.wait_ge(slots_ready, 1)
                for t in range(NT):
                    for n in range(2):
                        pool.indirect_dma_start(out=lists, out_offset=bass.IndirectOffsetOnAxis(ap=slots[:, t, n:n + 1], axis=0),
                                                in_=cols[:, S_TOK + t:S_TOK + t + 1], in_offset=None).then_inc(scattered, 16)
                pool.wait_ge(scattered, 16 * 2 * NT)

            @block.vector
            def _(dve):
                st = Steps(dve, own_dve)
                TT, TS, STT = dve.tensor_tensor, dve.tensor_scalar, dve.scalar_tensor_tensor
                cst_one = C(C_ONE)[:, 0:NX]
                dve.wait_ge(row_in, 128)
                for cond in range(2):
                    TS(out=g1[:, cond, :], in0=g1[:, cond, :], scalar1=0.5, scalar2=None, op0=ALU.mult)
                    st.add(TS(out=sc2[:, cond, :], in0=sc2[:, cond, :], scalar1=1.0, scalar2=None, op0=ALU.add))
                st.wait()
                dve.wait_ge(x_in, 32)

                def norm(t, n):
                    dve.bn_stats(bn[:, 0, :], x[:, t, 0:512])
                    st.link(dve.bn_stats(bn[:, 1, :], x[:, t, 512:D]))
                    st.link(dve.bn_aggr(mv[:, :], bn[:, :, :]))
                    TS(out=ve[:, n, t:t + 1], in0=mv[:, 1:2], scalar1=EPS, scalar2=None, op0=ALU.add).then_inc(ve_ready, 1)
                    dve.wait_ge(rs_ready, 2 * t + n + 1)
                    st.link(TS(out=tmp[:, :], in0=x[:, t, :], scalar1=mv[:, 0:1], scalar2=rs[:, n, t:t + 1], op0=ALU.subtract, op1=ALU.mult))

                for t in range(NT):
                    cond = min(t, 1)
                    if t > 0:
                        dve.wait_ge(pos_in, 16)
                        st.link(TT(out=x[:, t, :], in0=x[:, t, :], in1=pt[:, t - 1, :], op=ALU.add))
                    dve.wait_ge(mixed, t + 1)
                    if t > 0:
                        dve.wait_ge(h2_ready, t)
                    for h in range(2):
                        ins = TT(out=tmp[:, h * 512:(h + 1) * 512], in0=bank[2 * (t % 2) + h][:, :], in1=g1[:, cond, h * 512:(h + 1) * 512], op=ALU.mult)
                    ins.then_inc(sq_kept, 1)
                    dve.wait_ge(sq_kept, t + 1)
                    st.link(STT(out=x[:, t, :], in0=x[:, t, :], scalar=ALPHA, in1=tmp[:, :], op0=ALU.mult, op1=ALU.add))
                    norm(t, 0)
                    st.link(TT(out=tmp[:, :], in0=tmp[:, :], in1=lg[:, :], op=ALU.mult))
                    TT(out=x[:, t, :], in0=tmp[:, :], in1=lb[:, :], op=ALU.add).then_inc(x1_done, 1)
                    dve.wait_ge(x1_done, t + 1)
                    norm(t, 1)
                    if t >= 2:
                        dve.wait_ge(h2_out[t % 2], 16 * (t // 2))
                        dve.wait_ge(h2_turned, t - 1)
                    st.link(TT(out=tmp[:, :], in0=tmp[:, :], in1=sc2[:, cond, :], op=ALU.mult))
                    TT(out=h2[:, t % 2, :], in0=tmp[:, :], in1=sh2[:, cond, :], op=ALU.add).then_inc(h2_ready, 1)
                    if t > 0:
                        dve.wait_ge(logits, t)
                        TT(out=lo[:, t - 1, :], in0=bank[6][:, 0:NR], in1=br[:, :], op=ALU.add).then_inc(lo_kept, 1)
                dve.wait_ge(logits, NT)
                TT(out=lo[:, NT - 1, :], in0=bank[6][:, 0:NR], in1=br[:, :], op=ALU.add).then_inc(lo_kept, 1)
                dve.wait_ge(lo_kept, NT)
                st.link(dve.tensor_reduce(out=gmax[:, :, :], in_=lo[:, :, 0:XG], axis=AX.X, op=ALU.max))
                TT(out=gsh[:, :, :], in0=lo[:, :, 0:XG], in1=gmax[:, :, :].broadcast_to([P, NT, XG]), op=ALU.subtract).then_inc(gs_ready, 1)
                st.link(TT(out=eq[:, :, :], in0=lo[:, :, 0:XG], in1=gmax[:, :, :].broadcast_to([P, NT, XG]), op=ALU.is_equal))
                grp = cols[:, S_GRP:S_GRP + XG].unsqueeze(1).broadcast_to([P, NT, XG])
                st.link(TT(out=eq[:, :, :], in0=eq[:, :, :], in1=grp, op=ALU.mult))
                st.link(dve.tensor_reduce(out=rank[:, :, :], in_=eq[:, :, :], axis=AX.X, op=ALU.max))
                st.link(TT(out=eq[:, :, :], in0=grp, in1=rank[:, :, :].broadcast_to([P, NT, XG]), op=ALU.is_equal))
                st.link(TS(out=gidx[:, :, :], in0=rank[:, :, :], scalar1=-float(XE), scalar2=float(XE * XG), op0=ALU.mult, op1=ALU.add))
                for t in range(NT):
                    ins = TT(out=lsel[:, t, :, :], in0=lo[:, t, XG:NR].rearrange("p (g e) -> p g e", g=XG),
                             in1=eq[:, t, :].unsqueeze(2).broadcast_to([P, XG, XE]), op=ALU.mult)
                st.link(ins)
                for t in range(NT):
                    ins = dve.tensor_reduce(out=les[:, t, :], in_=lsel[:, t, :, :].rearrange("p g e -> p e g"), axis=AX.X, op=ALU.add)
                st.link(ins)
                for t in range(NT):
                    ins = dve.max(top[:, t, :], les[:, t, :])
                st.link(ins)
                for t in range(NT):
                    ins = dve.max_index(topi[:, t, :], top[:, t, :], les[:, t, :])
                st.link(ins)
                TT(out=dif[:, :, :], in0=top[:, :, 1:2], in1=top[:, :, 0:1], op=ALU.subtract).then_inc(dif_ready, 1)
                st.link(dve.tensor_copy(eid[:, :, :], topi[:, :, 0:2]))
                st.link(TT(out=eid[:, :, :], in0=eid[:, :, :], in1=gidx[:, :, :].broadcast_to([P, NT, 2]), op=ALU.add))
                for n in range(2):
                    ins = TT(out=oh[:, n, :, :], in0=cols[:, S_E:S_E + NX].unsqueeze(1).broadcast_to([P, NT, NX]),
                             in1=eid[:, :, n:n + 1].broadcast_to([P, NT, NX]), op=ALU.is_equal)
                st.link(ins)
                TT(out=both[:, :, :], in0=oh[:, 0, :, :], in1=oh[:, 1, :, :], op=ALU.add).then_inc(both_ready, 1)
                dve.wait_ge(gex_ready, 1)
                dve.wait_ge(tex_ready, 1)
                st.link(dve.tensor_reduce(out=gsum[:, :, :], in_=gex[:, :, :], axis=AX.X, op=ALU.add))
                st.link(TS(out=wts[:, :, 0:1], in0=tex[:, :, :], scalar1=1.0, scalar2=2.0, op0=ALU.add, op1=ALU.mult))
                st.link(TT(out=wts[:, :, 0:1], in0=wts[:, :, 0:1], in1=gsum[:, :, :], op=ALU.mult))
                st.link(dve.reciprocal(wts[:, :, 0:1], wts[:, :, 0:1]))
                st.link(TT(out=wts[:, :, 1:2], in0=wts[:, :, 0:1], in1=tex[:, :, :], op=ALU.mult))
                dve.wait_ge(counted, 1)
                count = bank[7][:, NT * NX:(NT + 1) * NX]
                st.link(TS(out=nmore[:, :], in0=count, scalar1=float(P), scalar2=None, op0=ALU.is_gt))
                for b in range(2, T // P):
                    st.link(STT(out=nmore[:, :], in0=count, scalar=float(b * P), in1=nmore[:, :], op0=ALU.is_gt, op1=ALU.add))
                st.link(dve.tensor_tensor_scan(out=upto[:, :], data0=cst_one, data1=nmore[:, :], initial=0.0, op0=ALU.mult, op1=ALU.add))
                st.link(TT(out=far[:, :], in0=upto[:, :], in1=nmore[:, :], op=ALU.subtract))
                st.link(STT(out=far[:, :], in0=far[:, :], scalar=float(P), in1=cols[:, S_FAR:S_FAR + NX], op0=ALU.mult, op1=ALU.add))
                places = bank[7][:, 0:NT * NX].rearrange("p (t e) -> p t e", e=NX)
                st.link(TS(out=past[:, :, :], in0=places, scalar1=float(P), scalar2=None, op0=ALU.is_ge))
                st.link(TT(out=past[:, :, :], in0=past[:, :, :], in1=far[:, :].unsqueeze(1).broadcast_to([P, NT, NX]), op=ALU.mult))
                st.link(TT(out=place[:, :, :], in0=places, in1=cols[:, S_LIST:S_LIST + NX].unsqueeze(1).broadcast_to([P, NT, NX]), op=ALU.add))
                st.link(TT(out=place[:, :, :], in0=place[:, :, :], in1=past[:, :, :], op=ALU.add))
                for n in range(2):
                    ins = TT(out=pick[:, n, :, :], in0=oh[:, n, :, :], in1=place[:, :, :], op=ALU.mult)
                st.link(ins)
                st.link(dve.tensor_reduce(out=slotf[:, :, :, :], in_=pick[:, :, :, :], axis=AX.X, op=ALU.add))
                dve.tensor_copy(slots[:, :, :], slotf[:, :, :, 0].rearrange("p n t -> p t n")).then_inc(slots_ready, 1)
                st.link(TT(out=later[:, :, :], in0=upto[:, :].unsqueeze(1).broadcast_to([P, NMORE, NX]),
                           in1=cols[:, S_MORE:S_MORE + NMORE].unsqueeze(2).broadcast_to([P, NMORE, NX]), op=ALU.is_le))
                st.link(dve.tensor_reduce(out=whose[:, 0:NMORE].unsqueeze(2), in_=later[:, :, :], axis=AX.X, op=ALU.add))
                st.link(dve.tensor_copy(whose[:, NMORE:NMORE + 1], upto[:, NX - 1:NX]))
                st.link(dve.tensor_copy(more[:, :], whose[:, :]))
                dve.wait_ge(rows_turned, 1)
                st.link(dve.tensor_copy(idx[:, :], bank[4][:, 0:NX]))


def load_expert(eng, e, wgu, wdn, w_exp_gate, w_exp_up, w_exp_down, signal):
    for to, w in ((wgu[:, :, 0, :], w_exp_gate), (wgu[:, :, 1, :], w_exp_up), (wdn[:, :, :], w_exp_down)):
        one = w[0, bass.ds(e, 1), :, :].rearrange("a d f -> (a d) f")
        eng.dma_start(to, one.rearrange("(p k) f -> p k f", p=P)).then_inc(signal, 16)


def experts(nc, sb, sem, bank, C, idx, more, lists, h2d, yd, w_exp_gate, w_exp_up, w_exp_down, wgu, wdn,
            x1, g2, lg2, lb2, x1d, ada, ln2_g, ln2_b):
    own = ExitStack()
    with own:
        S = lambda name, shape, dt=F32: sb(name, shape, dt, own)
        NB = 4
        NF = FX // P
        wgu = wgu + [S(f"wgu{n}", [P, KD, 2, FX]) for n in range(2, NB)]
        wdn = wdn + [S(f"wdn{n}", [P, NF, D]) for n in range(2, NB)]
        idxs = S("idxs", [P, NB], U32)
        xg = S("xg", [P, NB, D])
        xgT = S("xgT", [P, 2, KD, P])
        eth = S("eth", [P, 2, FX])
        eh = S("eh", [P, FX])
        hid = S("hid", [P, 2, FX])
        hidT = S("hidT", [P, NF, P])
        ysb = S("ysb", [P, 2, D])
        idf = S("idf", [P, 1])
        w_in_ = [sem(f"e_w{n}") for n in range(NB)]
        got = [sem(f"e_got{n}") for n in range(NB)]
        y_out = [sem("e_yout0"), sem("e_yout1")]
        (x_turned, x_kept, gu_done, th_ready, a_ready, hid_ready, ht_turned, ht_kept, dn_done, y_dve, y_act,
         idx_ready) = (sem("e_" + n) for n in ("xturned", "xkept", "gu", "th", "a", "hid", "htturned", "htkept", "dn",
                                               "ydve", "yact", "idx"))
        rest_in = sem("e_rest")

        def load(sp, e, par):
            load_expert(sp, e, wgu[par], wdn[par], w_exp_gate, w_exp_up, w_exp_down, w_in_[par])

        def turn_x(pe, par):
            for k in range(KD):
                last = pe.transpose(bank[k // 4][:, k % 4 * P:k % 4 * P + P], xg[:, par, k:D:KD], C(C_ID))
            return last

        def gate_up(pe, par, slot, to):
            for k in range(KD):
                last = pe.matmul(to[:, :], xgT[:, slot, k, :], wgu[par][:, k, :, :].rearrange("p a f -> p (a f)"), start=(k == 0), stop=(k == KD - 1))
            return last

        def turn_h(pe, slot):
            for j in range(NF):
                last = pe.transpose(bank[4][:, j * P:(j + 1) * P], hid[:, slot, j:FX:NF], C(C_ID))
            return last

        def down(pe, par):
            for h in range(2):
                for j in range(NF):
                    last = pe.matmul(bank[5 + h][:, :], hidT[:, j, :], wdn[par][:, j, h * 512:(h + 1) * 512], start=(j == 0), stop=(j == NF - 1))
            return last

        def turns(body):
            def run(eng):
                with eng.Fori(0, NX // NB - 1) as i:
                    for par in range(NB):
                        body(i * NB + par, i, par, True, True)
                for par in range(NB):
                    body(NX - NB + par, NX // NB - 1, par, par < NB - 1, par < NB - 2)
            return run

        with nc.Block() as block:
            @block.sync
            def _(sp):
                sp.wait_ge(got[1], 16)
                for par in range(2, NB):
                    load(sp, par, par)
                rows = lambda ap: ap.partition_broadcast(P)
                sp.dma_start(x1[:, :, :], x1d.rearrange("(t p) n -> p t n", p=P)).then_inc(rest_in, 16)
                for cond in range(2):
                    sp.dma_start(g2[:, cond, :], rows(ada[cond, 5 * D:6 * D])).then_inc(rest_in, 16)
                sp.dma_start(lg2[:, :], rows(ln2_g[0])).then_inc(rest_in, 16)
                sp.dma_start(lb2[:, :], rows(ln2_b[0])).then_inc(rest_in, 16)
                with sp.Fori(0, NX // NB - 1) as i:
                    for par in range(NB):
                        sp.wait_ge(dn_done, i * NB + par + 1)
                        load(sp, i * NB + par + NB, par)
                sp.wait_ge(rest_in, 80)

            @block.gpsimd
            def _(pool):
                def gather(e, par):
                    pool.tensor_copy(idxs[:, par:par + 1], idx[:, bass.ds(e, 1)]).then_inc(idx_ready, 1)
                    hold(pool, idx_ready, e + 1)
                    pool.indirect_dma_start(out=xg[:, par, :], out_offset=None, in_=h2d,
                                            in_offset=bass.IndirectOffsetOnAxis(ap=idxs[:, par:par + 1], axis=0)).then_inc(got[par], 16)

                for par in range(NB):
                    gather(par, par)
                with pool.Fori(0, NX // NB - 1) as i:
                    for par in range(NB):
                        pool.wait_ge(x_turned, i * NB + par + 1)
                        pool.wait_ge(got[par], i * 16 + 16)
                        gather(i * NB + par + NB, par)

            @block.tensor
            def _(pe):
                pe.wait_ge(got[0], 16)
                turn_x(pe, 0).then_inc(x_turned, 1)
                pe.wait_ge(got[1], 16)
                pe.wait_ge(x_kept, 1)
                turn_x(pe, 1).then_inc(x_turned, 1)
                pe.wait_ge(w_in_[0], 48)
                gate_up(pe, 0, 0, bank[2]).then_inc(gu_done, 1)

                def body(e, i, par, one, two):
                    if one:
                        p1, i1 = (par + 1) % NB, i + (par + 1) // NB
                        pe.wait_ge(w_in_[p1], i1 * 48 + 48)
                        pe.wait_ge(x_kept, e + 2)
                        gate_up(pe, p1, p1 % 2, bank[2 + p1 % 2]).then_inc(gu_done, 1)
                    pe.wait_ge(hid_ready, e + 1)
                    turn_h(pe, par % 2).then_inc(ht_turned, 1)
                    if two:
                        p2, i2 = (par + 2) % NB, i + (par + 2) // NB
                        pe.wait_ge(got[p2], i2 * 16 + 16)
                        turn_x(pe, p2).then_inc(x_turned, 1)
                    pe.wait_ge(ht_kept, e + 1)
                    pe.wait_ge(y_dve, e + 1)
                    pe.wait_ge(y_act, e + 1)
                    down(pe, par).then_inc(dn_done, 1)

                turns(body)(pe)

            @block.scalar
            def _(act):
                act.drain().then_inc(y_act, 1)
                for par in range(2):
                    act.drain().then_inc(w_in_[par], 48)

                def keep_x(e, slot, wait):
                    act.wait_ge(x_turned, e + 1)
                    if wait:
                        act.wait_ge(gu_done, e - 1)
                    for h in range(2):
                        last = act.copy(xgT[:, slot, 4 * h:4 * h + 4, :], bank[h][:, :].rearrange("p (k n) -> p k n", n=P))
                    last.then_inc(x_kept, 1)

                def tanh(e, slot):
                    act.wait_ge(gu_done, e + 1)
                    act.activation(eth[:, slot, :], bank[2 + slot][:, 0:FX], ACT.Tanh, scale=0.5).then_inc(th_ready, 1)

                keep_x(0, 0, False)
                keep_x(1, 1, False)
                tanh(0, 0)

                def body(e, i, par, one, two):
                    if one:
                        tanh(e + 1, (par + 1) % 2)
                    act.wait_ge(ht_turned, e + 1)
                    act.copy(hidT[:, :, :], bank[4][:, 0:FX].rearrange("p (j n) -> p j n", n=P)).then_inc(ht_kept, 1)
                    if two:
                        keep_x(e + 2, par % 2, True)
                    act.wait_ge(dn_done, e + 1)
                    act.wait_ge(y_out[par % 2], (i * 2 + par // 2) * 16 + 16)
                    act.copy(ysb[:, par % 2, 512:D], bank[6][:, :]).then_inc(y_act, 1)
                    act.wait_ge(y_act, e + 2)
                    act.wait_ge(y_dve, e + 2)
                    act.dma_start(yd[bass.ds(e * P, P), :], ysb[:, par % 2, :]).then_inc(y_out[par % 2], 16)

                for o in y_out:
                    act.drain().then_inc(o, 16)
                turns(body)(act)
                for o in y_out:
                    act.wait_ge(o, (NX // 2 + 1) * 16)

            @block.vector
            def _(dve):
                dve.drain().then_inc(y_dve, 1)

                def hidden(e, slot):
                    dve.wait_ge(th_ready, e + 1)
                    dve.scalar_tensor_tensor(out=eh[:, :], in0=eth[:, slot, :], scalar=1.0, in1=bank[2 + slot][:, 0:FX], op0=ALU.add, op1=ALU.mult).then_inc(a_ready, 1)
                    dve.wait_ge(a_ready, e + 1)
                    dve.tensor_tensor(out=hid[:, slot, :], in0=eh[:, :], in1=bank[2 + slot][:, FX:2 * FX], op=ALU.mult).then_inc(hid_ready, 1)

                hidden(0, 0)

                def body(e, i, par, one, two):
                    if one:
                        dve.wait_ge(hid_ready, e + 1)
                        hidden(e + 1, (par + 1) % 2)
                    dve.wait_ge(dn_done, e + 1)
                    dve.wait_ge(y_out[par % 2], (i * 2 + par // 2) * 16 + 16)
                    dve.tensor_copy(ysb[:, par % 2, 0:512], bank[5][:, :]).then_inc(y_dve, 1)

                turns(body)(dve)

        (o_w, o_idx, o_int, o_x, o_xt, o_xk, o_gu, o_th, o_a, o_h, o_ht, o_hk, o_dn, o_y, o_out) = (
            sem("o_" + n) for n in ("w", "idx", "int", "x", "xt", "xk", "gu", "th", "a", "h", "ht", "hk", "dn", "y", "out"))

        def further(body):
            def run(eng):
                blocks = eng.value_load(more[0:1, NMORE:NMORE + 1], min_val=0, max_val=NMORE)
                with eng.If(blocks > 0):
                    with eng.Fori(0, blocks) as n:
                        body(eng, n, n * P + NX * P)
            return run

        with nc.Block() as block:
            def sp_body(sp, n, at):
                e = sp.value_load(more[0:1, bass.ds(n, 1)], min_val=0, max_val=NX - 1)
                one = lambda w: w[0, bass.ds(e, 1), :, :].rearrange("a d f -> (a d) f")
                load_expert(sp, e, wgu[0], wdn[0], w_exp_gate, w_exp_up, w_exp_down, o_w)
                sp.dma_start(idf[:, :], lists[bass.ds(at, P), :]).then_inc(o_idx, 16)
                sp.wait_ge(o_y, 2 * n + 2)
                sp.dma_start(yd[bass.ds(at, P), :], ysb[:, 0, :]).then_inc(o_out, 16)
                hold(sp, o_out, 16 * n + 16)

            def pool_body(pool, n, at):
                hold(pool, o_idx, 16 * n + 16)
                pool.tensor_copy(idxs[:, 0:1], idf[:, :]).then_inc(o_int, 1)
                hold(pool, o_int, n + 1)
                pool.indirect_dma_start(out=xg[:, 0, :], out_offset=None, in_=h2d,
                                        in_offset=bass.IndirectOffsetOnAxis(ap=idxs[:, 0:1], axis=0)).then_inc(o_x, 16)
                pool.wait_ge(o_x, 16 * n + 16)

            def pe_body(pe, n, at):
                pe.wait_ge(o_x, 16 * n + 16)
                turn_x(pe, 0).then_inc(o_xt, 1)
                pe.wait_ge(o_xk, n + 1)
                pe.wait_ge(o_w, 48 * n + 48)
                gate_up(pe, 0, 0, bank[2]).then_inc(o_gu, 1)
                pe.wait_ge(o_h, n + 1)
                turn_h(pe, 0).then_inc(o_ht, 1)
                pe.wait_ge(o_hk, n + 1)
                down(pe, 0).then_inc(o_dn, 1)

            def act_body(act, n, at):
                act.wait_ge(o_xt, n + 1)
                for h in range(2):
                    last = act.copy(xgT[:, 0, 4 * h:4 * h + 4, :], bank[h][:, :].rearrange("p (k n) -> p k n", n=P))
                last.then_inc(o_xk, 1)
                act.wait_ge(o_gu, n + 1)
                act.activation(eth[:, 0, :], bank[2][:, 0:FX], ACT.Tanh, scale=0.5).then_inc(o_th, 1)
                act.wait_ge(o_ht, n + 1)
                act.copy(hidT[:, :, :], bank[4][:, 0:FX].rearrange("p (j n) -> p j n", n=P)).then_inc(o_hk, 1)
                act.wait_ge(o_dn, n + 1)
                act.copy(ysb[:, 0, 512:D], bank[6][:, :]).then_inc(o_y, 1)
                act.wait_ge(o_y, 2 * n + 2)

            def dve_body(dve, n, at):
                dve.wait_ge(o_th, n + 1)
                dve.scalar_tensor_tensor(out=eh[:, :], in0=eth[:, 0, :], scalar=1.0, in1=bank[2][:, 0:FX], op0=ALU.add, op1=ALU.mult).then_inc(o_a, 1)
                dve.wait_ge(o_a, n + 1)
                dve.tensor_tensor(out=hid[:, 0, :], in0=eh[:, :], in1=bank[2][:, FX:2 * FX], op=ALU.mult).then_inc(o_h, 1)
                dve.wait_ge(o_dn, n + 1)
                dve.tensor_copy(ysb[:, 0, 0:512], bank[5][:, :]).then_inc(o_y, 1)
                dve.wait_ge(o_y, 2 * n + 2)

            block.sync(further(sp_body))
            block.gpsimd(further(pool_body))
            block.tensor(further(pe_body))
            block.scalar(further(act_body))
            block.vector(further(dve_body))


def combine(nc, sb, sem, half, slots, wts, yd, x1, g2, lg, lb, y_prompt, y_sample):
    own = ExitStack()
    with own:
        S = lambda name, shape, dt=F32: sb(name, shape, dt, own)
        yg = S("yg", [P, NT, 2, D])
        bn = S("cbn", [P, NT, 2, 6])
        mv = S("cmv", [P, NT, 2])
        ve = S("cve", [P, NT])
        rs = S("crs", [P, NT])
        nb = S("cnb", [P, NT])
        got = [sem(f"c_got{t}") for t in range(NT)]
        scaled, summed, ve_ready, rs_ready, nb_ready, normed, weighed, out_ready, out_done, own_dve = (sem("c_" + n) for n in (
            "scaled", "summed", "ve", "rs", "nb", "normed", "weighed", "ready", "out", "dve"))
        last_weighed, last_ready = sem("c_lastweighed"), sem("c_lastready")
        with nc.Block() as block:
            @block.sync
            def _(sp):
                for t in range(NT):
                    if t < NT - 1:
                        sp.wait_ge(out_ready, t + 1)
                    else:
                        sp.wait_ge(last_ready, 1)
                    to = y_prompt[0] if t == 0 else y_sample[0, (t - 1) * P:t * P, :]
                    sp.dma_start(to, x1[:, t, :]).then_inc(out_done, 16)
                sp.wait_ge(out_done, 16 * NT)

            @block.scalar
            def _(act):
                for t in range(NT):
                    act.wait_ge(got[t], 32)
                    act.activation(yg[:, t, 0, :], yg[:, t, 0, :], ACT.Copy, scale=wts[:, t, 0:1]).then_inc(scaled, 1)
                for t in range(NT):
                    act.wait_ge(nb_ready, t + 1)
                    act.activation(yg[:, t, 1, :], x1[:, t, :], ACT.Identity, bias=nb[:, t:t + 1], scale=rs[:, t:t + 1]).then_inc(normed, 1)

            def back(eng, t, weighed, at, out_ready):
                a = yg[:, t, 1, :]
                eng.wait_ge(normed, t + 1)
                eng.tensor_tensor(out=a, in0=a, in1=lg[:, :], op=ALU.mult).then_inc(weighed, 1)
                eng.wait_ge(weighed, at)
                eng.tensor_tensor(out=x1[:, t, :], in0=a, in1=lb[:, :], op=ALU.add).then_inc(out_ready, 1)

            @block.gpsimd
            def _(pool):
                for t in range(NT):
                    for n in range(2):
                        pool.indirect_dma_start(out=yg[:, t, n, :], out_offset=None, in_=yd,
                                                in_offset=bass.IndirectOffsetOnAxis(ap=slots[:, t, n:n + 1], axis=0)).then_inc(got[t], 16)
                for t in range(NT):
                    pool.wait_ge(ve_ready, t + 1)
                    pool.tensor_tensor(out=rs[:, t:t + 1], in0=ve[:, t:t + 1], in1=half[:, 0:1], op=ALU.pow).then_inc(rs_ready, 1)
                    if t > 0:
                        back(pool, t - 1, weighed, t, out_ready)

            @block.vector
            def _(dve):
                st = Steps(dve, own_dve)
                TT, TS, STT = dve.tensor_tensor, dve.tensor_scalar, dve.scalar_tensor_tensor

                def front(t):
                    cond = min(t, 1)
                    a = yg[:, t, 0, :]
                    dve.wait_ge(scaled, t + 1)
                    st.link(STT(out=a, in0=yg[:, t, 1, :], scalar=wts[:, t, 1:2], in1=a, op0=ALU.mult, op1=ALU.add))
                    st.link(TT(out=a, in0=a, in1=g2[:, cond, :], op=ALU.mult))
                    st.link(STT(out=x1[:, t, :], in0=x1[:, t, :], scalar=ALPHA, in1=a, op0=ALU.mult, op1=ALU.add))
                    dve.bn_stats(bn[:, t, 0, :], x1[:, t, 0:512])
                    st.link(dve.bn_stats(bn[:, t, 1, :], x1[:, t, 512:D]))
                    st.link(dve.bn_aggr(mv[:, t, :], bn[:, t, :, :]))
                    TS(out=ve[:, t:t + 1], in0=mv[:, t, 1:2], scalar1=EPS, scalar2=None, op0=ALU.add).then_inc(ve_ready, 1)
                    dve.wait_ge(rs_ready, t + 1)
                    TS(out=nb[:, t:t + 1], in0=mv[:, t, 0:1], scalar1=rs[:, t:t + 1], scalar2=-1.0, op0=ALU.mult, op1=ALU.mult).then_inc(nb_ready, 1)

                for t in range(NT):
                    front(t)
                back(dve, NT - 1, last_weighed, 1, last_ready)


_INS = ["x_prompt", "x_sample", "state_gdn", "state_ssd", "c", "c_ctx", "w_ada", "b_ada", "w_in", "gdn_conv_w",
        "gdn_conv_b", "gdn_a_log", "gdn_dt_bias", "gdn_norm_w", "w_gdn_out", "ssd_conv_w", "ssd_conv_b", "ssd_a_log",
        "ssd_dt_bias", "ssd_d", "ssd_norm_w", "w_ssd_out", "w_o", "ln1_g", "ln1_b", "w_router_group",
        "b_router_group", "w_router_expert", "b_router_expert", "w_exp_gate", "w_exp_up", "w_exp_down", "ln2_g",
        "ln2_b"]
_OUTS = [(1, SEQ, D), (1, DEC, D), (1, 1, 2, GH, P, P), (1, 1, 2, SH, SP_, SN)]


def kernel(**inputs):
    import numpy as _np
    import concourse.bacc as _bacc
    from concourse import mybir as _mybir
    from concourse.bass_utils import run_bass_kernel_spmd as _run

    nc = _bacc.Bacc("TRN2", target_bir_lowering=False, num_devices=1)
    const, levels = constants()
    data = [(name, inputs[name]) for name in _INS]
    data += [("const", const), ("small", small_constants()), ("levels", levels), ("pos", positions())]
    arrays, args = {}, []
    for name, value in data:
        a = _np.ascontiguousarray(value)
        arrays[f"in_{name}_dram"] = a
        args.append(nc.dram_tensor(f"in_{name}_dram", a.shape, _mybir.dt.from_np(a.dtype), kind="ExternalInput").ap())
    for i, shape in enumerate(_OUTS):
        args.append(nc.dram_tensor(f"out_{i}_dram", shape, F32, kind="ExternalOutput").ap())
    build(nc, *args)
    r = _run(nc, [arrays], core_ids=[0])
    return tuple(r.results[0][f"out_{i}_dram"] for i in range(len(_OUTS)))
```
